# Optimizing a Trainium2 kernel written in Bass

```python
import math
import jax, jax.numpy as jnp
from jax import lax
import numpy as np

D_MODEL = 1024
BATCH = 1
SEQ = 512
DEPTH = 2

HEAD_DIM = 64
ROT_DIM = HEAD_DIM // 4
ROPE_THETA = 500000.0
BLOCK = 128
NORM_EPS = 1e-6

RWKV_HEADS = 6
RWKV_WIDTH = RWKV_HEADS * HEAD_DIM
DECAY_RANK = 64
ICL_RANK = 64
GN_EPS = 64e-5
DECAY_SCALE = math.exp(-0.5)

DSA_HEADS = 4
DSA_WIDTH = DSA_HEADS * HEAD_DIM
IDX_HEADS = 8
IDX_DIM = 32
IDX_ROT_DIM = IDX_DIM // 4
DSA_TOPK = 256

DIL_WINDOWS = (128, 512, 2048)
DIL_RATES = (1, 4, 16)
DIL_GROUPS = 3
DIL_HEADS_PER_GROUP = 2
DIL_HEADS = DIL_GROUPS * DIL_HEADS_PER_GROUP
DIL_WIDTH = DIL_HEADS * HEAD_DIM

MIX_WIDTH = RWKV_WIDTH + DSA_WIDTH + DIL_WIDTH
PLE_DIM = 256

RWKV_COLS = (RWKV_WIDTH, RWKV_WIDTH, RWKV_WIDTH, RWKV_WIDTH, DECAY_RANK, ICL_RANK)
RWKV_IN_WIDTH = 4 * RWKV_WIDTH + DECAY_RANK + ICL_RANK
DSA_COLS = (DSA_WIDTH, HEAD_DIM, HEAD_DIM, IDX_HEADS * IDX_DIM, IDX_DIM, IDX_HEADS, DSA_WIDTH)
DSA_IN_WIDTH = 2 * DSA_WIDTH + 2 * HEAD_DIM + IDX_HEADS * IDX_DIM + IDX_DIM + IDX_HEADS
DIL_COLS = (DIL_WIDTH, DIL_WIDTH, DIL_WIDTH, DIL_WIDTH)
DIL_IN_WIDTH = 4 * DIL_WIDTH
IN_COLS = RWKV_IN_WIDTH + DSA_IN_WIDTH + DIL_IN_WIDTH


def rms_norm(x, g):
    xf = x.astype(jnp.float32)
    y = xf * lax.rsqrt(jnp.mean(xf * xf, axis=-1, keepdims=True) + NORM_EPS)
    return (y * g.astype(jnp.float32)).astype(x.dtype)

def split_cols(z, widths):
    out, off = [], 0
    for w in widths:
        out.append(z[..., off:off + w])
        off += w
    return out

def rope_tables(seq, rot_dim):
    half = rot_dim // 2
    inv = ROPE_THETA ** (-jnp.arange(half, dtype=jnp.float32) / half)
    ang = jnp.arange(seq, dtype=jnp.float32)[:, None] * inv[None, :]
    return jnp.cos(ang), jnp.sin(ang)

def partial_rope(x, cos, sin):
    half = cos.shape[-1]
    c = cos[None, :, None, :].astype(x.dtype)
    s = sin[None, :, None, :].astype(x.dtype)
    x1, x2, rest = x[..., :half], x[..., half:2 * half], x[..., 2 * half:]
    return jnp.concatenate([x1 * c - x2 * s, x2 * c + x1 * s, rest], axis=-1)

def token_shift_mix(z, mu):
    prev = jnp.pad(z, ((0, 0), (1, 0), (0, 0)))[:, :-1]
    return z + (prev - z) * mu

def rwkv7_branch(z, mu, w0, w_up, a0, a_up, k_k, k_a, r_k, ln_g, ln_b):
    B, S, _ = z.shape
    f32 = jnp.float32
    z = token_shift_mix(z, mu)
    r, k, v, g, wd, ad = split_cols(z, RWKV_COLS)
    heads = lambda t: t.astype(f32).reshape(B, S, RWKV_HEADS, HEAD_DIM)
    per_head = lambda t: t.astype(f32).reshape(RWKV_HEADS, HEAD_DIM)
    w = jnp.exp(-DECAY_SCALE * jax.nn.sigmoid((w0 + jnp.tanh(wd) @ w_up).astype(f32)))
    a = jax.nn.sigmoid((a0 + ad @ a_up).astype(f32))
    r, k, v, w, a = heads(r), heads(k), heads(v), heads(w), heads(a)
    kk = k * per_head(k_k)
    kk = kk / jnp.maximum(jnp.linalg.norm(kk, axis=-1, keepdims=True), 1e-12)
    k = k * (1.0 + (a - 1.0) * per_head(k_a))

    def step(state, inp):
        r_t, w_t, k_t, v_t, kk_t, a_t = inp
        sa = jnp.einsum('bhvk,bhk->bhv', state, -kk_t)
        state = (state * w_t[:, :, None, :]
                 + sa[..., None] * (kk_t * a_t)[:, :, None, :]
                 + v_t[..., None] * k_t[:, :, None, :])
        return state, jnp.einsum('bhvk,bhk->bhv', state, r_t)

    seq_first = lambda t: jnp.moveaxis(t, 1, 0)
    s0 = jnp.zeros((B, RWKV_HEADS, HEAD_DIM, HEAD_DIM), f32)
    _, y = lax.scan(step, s0, (seq_first(r), seq_first(w), seq_first(k), seq_first(v), seq_first(kk), seq_first(a)))
    y = jnp.moveaxis(y, 0, 1)
    mean = jnp.mean(y, axis=-1, keepdims=True)
    var = jnp.mean(jnp.square(y - mean), axis=-1, keepdims=True)
    y = ((y - mean) * lax.rsqrt(var + GN_EPS)).reshape(B, S, RWKV_WIDTH) * ln_g.astype(f32) + ln_b.astype(f32)
    bonus = jnp.sum(r * k * r_k.astype(f32), axis=-1, keepdims=True) * v
    y = y + bonus.reshape(B, S, RWKV_WIDTH)
    return (y * jax.nn.silu(g.astype(f32))).astype(z.dtype)

def dsa_branch(z, cos, sin, icos, isin):
    B, S, _ = z.shape
    f32 = jnp.float32
    q, k, v, iq, ik, iw, g = split_cols(z, DSA_COLS)
    q = partial_rope(q.reshape(B, S, DSA_HEADS, HEAD_DIM), cos, sin)
    k = partial_rope(k[:, :, None, :], cos, sin)[:, :, 0]
    iq = partial_rope(iq.reshape(B, S, IDX_HEADS, IDX_DIM), icos, isin)
    ik = partial_rope(ik[:, :, None, :], icos, isin)[:, :, 0]
    iw = iw * (IDX_HEADS ** -0.5)
    topk = min(DSA_TOPK, S // 4)
    nb = S // BLOCK
    key_pos = jnp.arange(S)
    gather = jax.vmap(lambda table, idx: table[idx])

    def block_fn(args):
        qb, iqb, iwb, start = args
        qpos = start + jnp.arange(BLOCK)
        sc = jnp.einsum('bqhd,bsd->bqhs', iqb, ik).astype(f32) * (IDX_DIM ** -0.5)
        sc = jnp.einsum('bqhs,bqh->bqs', jax.nn.relu(sc), iwb.astype(f32))
        sc = jnp.where((key_pos[None, :] <= qpos[:, None])[None], sc, -jnp.inf)
        _, idx = lax.top_k(sc, topk)
        valid = idx <= qpos[None, :, None]
        ks = gather(k, idx)
        vs = gather(v, idx)
        att = jnp.einsum('bqhd,bqkd->bqhk', qb, ks).astype(f32) * (HEAD_DIM ** -0.5)
        att = jnp.where(valid[:, :, None, :], att, -jnp.inf)
        probs = jax.nn.softmax(att, axis=-1).astype(vs.dtype)
        return jnp.einsum('bqhk,bqkd->bqhd', probs, vs)

    blocks = lambda t: jnp.moveaxis(t.reshape(B, nb, BLOCK, *t.shape[2:]), 1, 0)
    out = lax.map(block_fn, (blocks(q), blocks(iq), blocks(iw), jnp.arange(nb) * BLOCK))
    out = jnp.moveaxis(out, 0, 1).reshape(B, S, DSA_WIDTH)
    return out * jax.nn.silu(g)

def banded_attention(q, k, v, max_steps):
    N, n, H, dh = q.shape
    nb = -(-n // BLOCK)
    pad = nb * BLOCK - n
    to_blocks = lambda t: jnp.pad(t, ((0, 0), (0, pad), (0, 0), (0, 0))).reshape(N, nb, BLOCK, H, dh)
    qb, kb, vb = to_blocks(q), to_blocks(k), to_blocks(v)
    prev = lambda t: jnp.concatenate([jnp.zeros_like(t[:, :1]), t[:, :-1]], axis=1)
    kc = jnp.concatenate([prev(kb), kb], axis=2)
    vc = jnp.concatenate([prev(vb), vb], axis=2)
    s = jnp.einsum('nbqhd,nbkhd->nbhqk', qb, kc).astype(jnp.float32) * (HEAD_DIM ** -0.5)
    qi = jnp.arange(BLOCK)[:, None] + BLOCK
    kj = jnp.arange(2 * BLOCK)[None, :]
    dist = qi - kj
    band = (dist >= 0) & (dist <= max_steps)
    has_prev = (jnp.arange(nb)[:, None, None] > 0) | (kj[None] >= BLOCK)
    mask = band[None] & has_prev
    s = jnp.where(mask[None, :, None], s, -jnp.inf)
    m = jnp.max(s, axis=-1, keepdims=True)
    e = jnp.exp(s - m)
    l = jnp.sum(e, axis=-1, keepdims=True)
    o = jnp.einsum('nbhqk,nbkhd->nbqhd', (e / l).astype(v.dtype), vc)
    lse = (m + jnp.log(l))[..., 0]
    o = o.reshape(N, nb * BLOCK, H, dh)[:, :n]
    lse = jnp.moveaxis(lse, 2, 3).reshape(N, nb * BLOCK, H)[:, :n]
    return o, lse

def dilated_group(q, k, v, rate, steps):
    B, S, H, dh = q.shape
    n = S // rate
    to_res = lambda t: jnp.swapaxes(t.reshape(B, n, rate, H, dh), 1, 2).reshape(B * rate, n, H, dh)
    o, lse = banded_attention(to_res(q), to_res(k), to_res(v), steps)
    o = jnp.swapaxes(o.reshape(B, rate, n, H, dh), 1, 2).reshape(B, S, H, dh)
    lse = jnp.swapaxes(lse.reshape(B, rate, n, H), 1, 2).reshape(B, S, H)
    return o, lse

def dilated_branch(z, cos, sin):
    B, S, _ = z.shape
    q, k, v, g = split_cols(z, DIL_COLS)
    heads = lambda t: t.reshape(B, S, DIL_HEADS, HEAD_DIM)
    q = partial_rope(heads(q), cos, sin)
    k = partial_rope(heads(k), cos, sin)
    v = heads(v)
    outs, lses = [], []
    for gi in range(DIL_GROUPS):
        hs = slice(gi * DIL_HEADS_PER_GROUP, (gi + 1) * DIL_HEADS_PER_GROUP)
        o, lse = dilated_group(q[:, :, hs], k[:, :, hs], v[:, :, hs], DIL_RATES[gi], DIL_WINDOWS[gi] // DIL_RATES[gi])
        outs.append(o)
        lses.append(lse)
    o = jnp.stack(outs, axis=2)
    alpha = jax.nn.softmax(jnp.stack(lses, axis=2), axis=2)
    o = (o * alpha[..., None].astype(o.dtype)).reshape(B, S, DIL_WIDTH)
    return o * jax.nn.silu(g)

def first_inputs(seed: int = 0) -> dict:
    key = jax.random.key(seed)
    ks = jax.random.split(key, 20)
    f32 = jnp.float32
    nrm = lambda kk, shape, scale: scale * jax.random.normal(kk, shape, f32)
    L = DEPTH
    return {
        'x': nrm(ks[0], (BATCH, SEQ, D_MODEL), 1.0),
        'p': nrm(ks[1], (DEPTH, BATCH, SEQ, PLE_DIM), 1.0),
        'norm_g': 1.0 + nrm(ks[2], (L, D_MODEL), 0.05),
        'w_in': nrm(ks[3], (L, D_MODEL, IN_COLS), D_MODEL ** -0.5),
        'tshift_mu': jax.random.uniform(ks[4], (L, RWKV_IN_WIDTH), f32),
        'rwkv_w0': jax.random.uniform(ks[5], (L, RWKV_WIDTH), f32, -6.0, 1.0),
        'rwkv_w_up': nrm(ks[6], (L, DECAY_RANK, RWKV_WIDTH), DECAY_RANK ** -0.5),
        'rwkv_a0': nrm(ks[7], (L, RWKV_WIDTH), 0.5),
        'rwkv_a_up': nrm(ks[8], (L, ICL_RANK, RWKV_WIDTH), ICL_RANK ** -0.5),
        'rwkv_k_k': 0.85 + nrm(ks[9], (L, RWKV_WIDTH), 0.05),
        'rwkv_k_a': 1.0 + nrm(ks[10], (L, RWKV_WIDTH), 0.05),
        'rwkv_r_k': nrm(ks[11], (L, RWKV_HEADS, HEAD_DIM), 0.1),
        'rwkv_ln_g': 1.0 + nrm(ks[12], (L, RWKV_WIDTH), 0.05),
        'rwkv_ln_b': nrm(ks[13], (L, RWKV_WIDTH), 0.01),
        'w_out': nrm(ks[14], (L, MIX_WIDTH, D_MODEL), 0.5 * MIX_WIDTH ** -0.5),
        'ple_norm_g': 1.0 + nrm(ks[15], (L, D_MODEL), 0.05),
        'ple_w_gate': nrm(ks[16], (L, D_MODEL, D_MODEL), D_MODEL ** -0.5),
        'ple_w_proj': nrm(ks[17], (L, PLE_DIM, D_MODEL), 0.5 * PLE_DIM ** -0.5),
        'final_norm_g': 1.0 + nrm(ks[18], (D_MODEL,), 0.05),
    }

def first_block(x, p, norm_g, w_in, tshift_mu, rwkv_w0, rwkv_w_up, rwkv_a0, rwkv_a_up, rwkv_k_k, rwkv_k_a,
              rwkv_r_k, rwkv_ln_g, rwkv_ln_b, w_out, ple_norm_g, ple_w_gate, ple_w_proj, final_norm_g):
    S = x.shape[1]
    cos, sin = rope_tables(S, ROT_DIM)
    icos, isin = rope_tables(S, IDX_ROT_DIM)
    for i in range(DEPTH):
        h = rms_norm(x, norm_g[i])
        z = h @ w_in[i]
        z_a, z_b, z_c = split_cols(z, (RWKV_IN_WIDTH, DSA_IN_WIDTH, DIL_IN_WIDTH))
        y_a = rwkv7_branch(z_a, tshift_mu[i], rwkv_w0[i], rwkv_w_up[i], rwkv_a0[i], rwkv_a_up[i],
                           rwkv_k_k[i], rwkv_k_a[i], rwkv_r_k[i], rwkv_ln_g[i], rwkv_ln_b[i])
        y_b = dsa_branch(z_b, cos, sin, icos, isin)
        y_c = dilated_branch(z_c, cos, sin)
        y = jnp.concatenate([y_a, y_b, y_c], axis=-1)
        x = x + y @ w_out[i]
        gate = jax.nn.sigmoid(rms_norm(x, ple_norm_g[i]) @ ple_w_gate[i])
        x = x + gate * (p[i] @ ple_w_proj[i])
    return rms_norm(x, final_norm_g)


DEPTH_2 = 1

GRID_W = 64
N_Q_HEADS = 8
N_KV_HEADS = 2
ATTN_WIDTH = N_Q_HEADS * HEAD_DIM
KV_WIDTH = N_KV_HEADS * HEAD_DIM
Q_BLOCK = 128
ROPE_THETA_2 = 10000.0
DN_HEADS = 8
DN_HEAD_DIM = 64
DN_WIDTH = DN_HEADS * DN_HEAD_DIM
CONV_WIDTH = 5
CHUNK = 64
N_BRANCHES = 2
N_EXPERTS = 16
CAPACITY_FACTOR = 2
D_EXPERT = 1024
EPS = 1e-6
IN_SPLITS = (ATTN_WIDTH, KV_WIDTH, KV_WIDTH, DN_WIDTH, DN_WIDTH, DN_WIDTH, DN_WIDTH, 2 * DN_HEADS, 2 * DN_HEADS, N_BRANCHES * D_MODEL)
D_IN = sum(IN_SPLITS)


def rmsnorm(x, w):
    xf = x.astype(jnp.float32)
    y = xf * lax.rsqrt(jnp.mean(xf * xf, axis=-1, keepdims=True) + EPS)
    return (y * w.astype(jnp.float32)).astype(x.dtype)

def l2norm(x):
    xf = x.astype(jnp.float32)
    return xf * lax.rsqrt(jnp.sum(xf * xf, axis=-1, keepdims=True) + EPS)

def heads(t, n):
    B, S, _ = t.shape
    return t.reshape(B, S, n, -1).transpose(0, 2, 1, 3)

def rope_axis(x, pos):
    d = x.shape[-1]
    freqs = ROPE_THETA_2 ** (-(jnp.arange(d // 2, dtype=jnp.float32) * 2.0 / d))
    ang = pos.astype(jnp.float32)[:, None] * freqs[None, :]
    cos = jnp.concatenate([jnp.cos(ang), jnp.cos(ang)], axis=-1)
    sin = jnp.concatenate([jnp.sin(ang), jnp.sin(ang)], axis=-1)
    xf = x.astype(jnp.float32)
    x1, x2 = xf[..., : d // 2], xf[..., d // 2 :]
    rot = jnp.concatenate([-x2, x1], axis=-1)
    return (xf * cos + rot * sin).astype(x.dtype)

def axial_rope(x, row, col):
    hd = x.shape[-1] // 2
    return jnp.concatenate([rope_axis(x[..., :hd], row), rope_axis(x[..., hd:], col)], axis=-1)

def block_attention(q, k, v):
    B, Hq, S, dh = q.shape
    Hkv = k.shape[1]
    G = Hq // Hkv
    nb = S // Q_BLOCK
    qb = q.reshape(B, Hkv, G, nb, Q_BLOCK, dh).transpose(3, 0, 1, 2, 4, 5).astype(jnp.float32)
    kf = k.astype(jnp.float32)
    vf = v.astype(jnp.float32)
    scale = dh ** -0.5

    def one_block(qi):
        s = jnp.einsum('bhgqd,bhkd->bhgqk', qi, kf) * scale
        p = jax.nn.softmax(s, axis=-1)
        return jnp.einsum('bhgqk,bhkd->bhgqd', p, vf)

    o = lax.map(one_block, qb)
    return o.transpose(1, 2, 3, 0, 4, 5).reshape(B, Hq, S, dh).astype(q.dtype)

def short_conv(x, w):
    K, C = w.shape
    return lax.conv_general_dilated(x, w[:, None, :], window_strides=(1,), padding=[(K // 2, K // 2)],
                                    dimension_numbers=('NWC', 'WIO', 'NWC'), feature_group_count=C)

def gated_delta_chunked(q, k, v, beta, g):
    B, H, S, dk = q.shape
    dv = v.shape[-1]
    N = S // CHUNK
    q = q.reshape(B, H, N, CHUNK, dk)
    k = k.reshape(B, H, N, CHUNK, dk)
    v = v.reshape(B, H, N, CHUNK, dv)
    beta = beta.reshape(B, H, N, CHUNK)
    gc = jnp.cumsum(g.reshape(B, H, N, CHUNK), axis=-1)
    idx = jnp.arange(CHUNK)
    incl = idx[:, None] >= idx[None, :]
    strict = idx[:, None] > idx[None, :]
    decay = jnp.exp(jnp.where(incl, gc[..., :, None] - gc[..., None, :], -jnp.inf))
    kb = k * beta[..., None]
    vb = v * beta[..., None]
    L = jnp.where(strict, jnp.einsum('bhncd,bhnsd->bhncs', kb, k) * decay, 0.0)
    eye = jnp.eye(CHUNK, dtype=jnp.float32)
    T = lax.linalg.triangular_solve(eye + L, jnp.broadcast_to(eye, L.shape), left_side=True, lower=True,
                                    unit_diagonal=True)
    u = T @ vb
    w = T @ (kb * jnp.exp(gc)[..., None])
    a_intra = jnp.where(incl, jnp.einsum('bhncd,bhnsd->bhncs', q, k) * decay, 0.0)
    qg = q * jnp.exp(gc)[..., None]
    kd = k * jnp.exp(gc[..., -1:] - gc)[..., None]
    gl = jnp.exp(gc[..., -1])
    xs = tuple(jnp.moveaxis(t, 2, 0) for t in (u, w, a_intra, qg, kd, gl))

    def step(state, inp):
        u_n, w_n, a_n, qg_n, kd_n, gl_n = inp
        v_new = u_n - w_n @ state
        o_n = qg_n @ state + a_n @ v_new
        state = state * gl_n[..., None, None] + jnp.einsum('bhck,bhcv->bhkv', kd_n, v_new)
        return state, o_n

    _, o = lax.scan(step, jnp.zeros((B, H, dk, dv), jnp.float32), xs)
    return jnp.moveaxis(o, 0, 2).reshape(B, H, S, dv)

def hybrid_mixer(h, row, col, w_in, q_norm_w, k_norm_w, conv_w, a_log, dt_bias, dn_norm_w, w_attn_up, w_dn_up, w_o):
    B, S, D = h.shape
    proj = h @ w_in
    aq, ak, av, dq, dk, dv, dz, b_raw, a_raw, g_raw = jnp.split(proj, np.cumsum(IN_SPLITS)[:-1].tolist(), axis=-1)

    q = axial_rope(rmsnorm(heads(aq, N_Q_HEADS), q_norm_w), row, col)
    k = axial_rope(rmsnorm(heads(ak, N_KV_HEADS), k_norm_w), row, col)
    v = heads(av, N_KV_HEADS)
    attn = block_attention(q, k, v).transpose(0, 2, 1, 3).reshape(B, S, ATTN_WIDTH)

    qkv = jax.nn.silu(short_conv(jnp.concatenate([dq, dk, dv], axis=-1), conv_w))
    cq, ck, cv = jnp.split(qkv, 3, axis=-1)
    qd = l2norm(heads(cq, DN_HEADS)) * (DN_HEAD_DIM ** -0.5)
    kd = l2norm(heads(ck, DN_HEADS))
    vd = heads(cv, DN_HEADS).astype(jnp.float32)
    beta = jax.nn.sigmoid(b_raw.astype(jnp.float32)).reshape(B, S, 2, DN_HEADS).transpose(2, 0, 3, 1)
    a_in = a_raw.astype(jnp.float32).reshape(B, S, 2, DN_HEADS) + dt_bias.astype(jnp.float32)
    g = -jnp.exp(a_log.astype(jnp.float32))[:, None, :, None] * jax.nn.softplus(a_in.transpose(2, 0, 3, 1))
    flip = lambda t: jnp.flip(t, axis=2)
    o_fwd = gated_delta_chunked(qd, kd, vd, beta[0], g[0])
    o_bwd = flip(gated_delta_chunked(flip(qd), flip(kd), flip(vd), flip(beta[1]), flip(g[1])))
    o = (o_fwd + o_bwd).transpose(0, 2, 1, 3)
    o = rmsnorm(o, dn_norm_w) * jax.nn.silu(dz.astype(jnp.float32).reshape(B, S, DN_HEADS, DN_HEAD_DIM))
    dn = o.reshape(B, S, DN_WIDTH).astype(h.dtype)

    gate_a, gate_d = jnp.split(jax.nn.sigmoid(g_raw), N_BRANCHES, axis=-1)
    merged = gate_a * (attn @ w_attn_up) + gate_d * (dn @ w_dn_up)
    return merged @ w_o

def expert_choice_ffn(h, w_router, w_gate, w_up, w_down):
    B, S, D = h.shape
    cap = CAPACITY_FACTOR * S // N_EXPERTS
    aff = jax.nn.softmax((h @ w_router).astype(jnp.float32), axis=-1)
    gates, idx = lax.top_k(aff.transpose(0, 2, 1), cap)
    bidx = jnp.arange(B)[:, None, None]
    xe = h[bidx, idx]
    hg = jnp.einsum('becd,edf->becf', xe, w_gate)
    hu = jnp.einsum('becd,edf->becf', xe, w_up)
    y = jnp.einsum('becf,efd->becd', jax.nn.silu(hg) * hu, w_down)
    y = y * gates[..., None].astype(y.dtype)
    return jnp.zeros_like(h).at[bidx, idx].add(y)

def second_inputs(seed: int = 0) -> dict:
    key = jax.random.key(seed)
    ks = jax.random.split(key, 24)
    f32 = jnp.float32

    def nrm(k, shape, fan_in):
        return jax.random.normal(k, shape, f32) * (fan_in ** -0.5)

    def gain(k, shape):
        return 1.0 + 0.02 * jax.random.normal(k, shape, f32)

    dt = jnp.exp(jax.random.uniform(ks[11], (DEPTH_2, 2, DN_HEADS), f32, np.log(1e-3), np.log(1e-1)))
    return {
        'x': jax.random.normal(ks[0], (BATCH, SEQ, D_MODEL), f32),
        'c': jax.random.normal(ks[1], (BATCH, D_MODEL), f32),
        'w_ada': nrm(ks[2], (DEPTH_2, D_MODEL, 6 * D_MODEL), D_MODEL),
        'b_ada': 0.01 * jax.random.normal(ks[3], (DEPTH_2, 6 * D_MODEL), f32),
        'norm1_w': gain(ks[4], (DEPTH_2, D_MODEL)),
        'w_in': nrm(ks[5], (DEPTH_2, D_MODEL, D_IN), D_MODEL),
        'q_norm_w': gain(ks[6], (DEPTH_2, HEAD_DIM)),
        'k_norm_w': gain(ks[7], (DEPTH_2, HEAD_DIM)),
        'conv_w': nrm(ks[8], (DEPTH_2, CONV_WIDTH, 3 * DN_WIDTH), CONV_WIDTH),
        'a_log': jnp.log(jax.random.uniform(ks[9], (DEPTH_2, 2, DN_HEADS), f32, 1.0, 16.0)),
        'dt_bias': dt + jnp.log(-jnp.expm1(-dt)),
        'dn_norm_w': gain(ks[10], (DEPTH_2, DN_HEAD_DIM)),
        'w_attn_up': nrm(ks[12], (DEPTH_2, ATTN_WIDTH, D_MODEL), ATTN_WIDTH),
        'w_dn_up': nrm(ks[13], (DEPTH_2, DN_WIDTH, D_MODEL), DN_WIDTH),
        'w_o': nrm(ks[14], (DEPTH_2, D_MODEL, D_MODEL), D_MODEL),
        'norm2_w': gain(ks[15], (DEPTH_2, D_MODEL)),
        'w_router': nrm(ks[16], (DEPTH_2, D_MODEL, N_EXPERTS), D_MODEL),
        'w_gate': nrm(ks[17], (DEPTH_2, N_EXPERTS, D_MODEL, D_EXPERT), D_MODEL),
        'w_up': nrm(ks[18], (DEPTH_2, N_EXPERTS, D_MODEL, D_EXPERT), D_MODEL),
        'w_down': nrm(ks[19], (DEPTH_2, N_EXPERTS, D_EXPERT, D_MODEL), D_EXPERT),
    }

def second_block(x, c, w_ada, b_ada, norm1_w, w_in, q_norm_w, k_norm_w, conv_w, a_log, dt_bias, dn_norm_w,
              w_attn_up, w_dn_up, w_o, norm2_w, w_router, w_gate, w_up, w_down):
    B, S, D = x.shape
    rows = S // GRID_W
    row = jnp.broadcast_to(jnp.arange(rows)[:, None], (rows, GRID_W)).reshape(S)
    col = jnp.broadcast_to(jnp.arange(GRID_W)[None, :], (rows, GRID_W)).reshape(S)
    for l in range(DEPTH_2):
        mod = jax.nn.silu(c) @ w_ada[l] + b_ada[l]
        sh1, sc1, gt1, sh2, sc2, gt2 = [m[:, None, :] for m in jnp.split(mod, 6, axis=-1)]
        h = rmsnorm(x, norm1_w[l]) * (1.0 + sc1) + sh1
        x = x + gt1 * hybrid_mixer(h, row, col, w_in[l], q_norm_w[l], k_norm_w[l], conv_w[l], a_log[l], dt_bias[l],
                                   dn_norm_w[l], w_attn_up[l], w_dn_up[l], w_o[l])
        h2 = rmsnorm(x, norm2_w[l]) * (1.0 + sc2) + sh2
        x = x + gt2 * expert_choice_ffn(h2, w_router[l], w_gate[l], w_up[l], w_down[l])
    return x


def setup_inputs(seed=0):
    out = dict(first_inputs(seed))
    for name, value in second_inputs(seed + 1).items():
        if name != "x":
            out[name + "_2"] = value
    return out


def reference(
    x, p, norm_g, w_in, tshift_mu, rwkv_w0, rwkv_w_up, rwkv_a0, rwkv_a_up, rwkv_k_k, rwkv_k_a,
    rwkv_r_k, rwkv_ln_g, rwkv_ln_b, w_out, ple_norm_g, ple_w_gate, ple_w_proj, final_norm_g,
    c_2, w_ada_2, b_ada_2, norm1_w_2, w_in_2, q_norm_w_2, k_norm_w_2, conv_w_2, a_log_2,
    dt_bias_2, dn_norm_w_2, w_attn_up_2, w_dn_up_2, w_o_2, norm2_w_2, w_router_2, w_gate_2,
    w_up_2, w_down_2,
):
    x = first_block(
        x, p, norm_g, w_in, tshift_mu, rwkv_w0, rwkv_w_up, rwkv_a0, rwkv_a_up, rwkv_k_k,
        rwkv_k_a, rwkv_r_k, rwkv_ln_g, rwkv_ln_b, w_out, ple_norm_g, ple_w_gate, ple_w_proj,
        final_norm_g,
    )
    return second_block(
        x, c_2, w_ada_2, b_ada_2, norm1_w_2, w_in_2, q_norm_w_2, k_norm_w_2, conv_w_2, a_log_2,
        dt_bias_2, dn_norm_w_2, w_attn_up_2, w_dn_up_2, w_o_2, norm2_w_2, w_router_2, w_gate_2,
        w_up_2, w_down_2,
    )


_drawn_inputs = setup_inputs


def setup_inputs(seed=0):
    import zlib

    import numpy as np

    out = dict(_drawn_inputs(seed))
    spreads = {}
    factors = {'rwkv_k_k': 3.395,
     'rwkv_ln_g': 4.351,
     'rwkv_ln_b': 4.35,
     'ple_norm_g': 3.194,
     'norm1_w_2': 3.547,
     'q_norm_w_2': 8.0,
     'k_norm_w_2': 8.0,
     'dn_norm_w_2': 11.891,
     'norm2_w_2': 8.0}
    for name, (base, spread) in spreads.items():
        noise = np.random.default_rng([zlib.crc32(name.encode()), seed]).standard_normal(out[name].shape)
        drawn = base * np.exp(spread * noise) if base else spread * noise
        out[name] = __import__('jax').numpy.asarray(drawn.astype(out[name].dtype))
    for name, factor in factors.items():
        out[name] = (out[name] * factor).astype(out[name].dtype)
    return out
```

```python
import math
from contextlib import ExitStack, contextmanager

import numpy as np

import concourse.bass as bass
from concourse import mybir

F32 = mybir.dt.float32
U32 = mybir.dt.uint32
ALU = mybir.AluOpType
ACT = mybir.ActivationFunctionType
AX = mybir.AxisListType

P = 128
S = 512
D = 1024
KT = D // P
TT = S // P
DEPTH = 2
HD = 64
CH = 64
NCH = S // CH
LEVELS = (1, 2, 4, 8, 16, 32)

RW, RP = 384, 3
DECAY_SCALE = math.exp(-0.5)
NEG = -1e30
TAKEN = -3e38
TOPK = 128
NORM_EPS = 1e-6

A_Q, A_K, A_DQ, A_DK, A_IQ, A_IK, A_G, A_DG, N_A = 0, 2, 3, 6, 9, 11, 12, 14, 17
R_R, R_K, R_V, R_G, R_WA, N_R = 0, 3, 6, 9, 12, 13
V_DSA, V_IW, V_D0, V_D1, N_V = 0, 64, 72, 200, 456


def constant_parts():
    i = np.arange(P)
    t = np.arange(CH)
    parts = {}
    parts["ident"] = np.eye(P)
    parts["ones"] = np.ones((P, P))
    same = (i[:, None] // HD) == (i[None, :] // HD)
    parts["head_ones"] = same * 1.0
    parts["sum_until"] = same & (i[:, None] <= i[None, :])
    parts["sum_from"] = same & (i[:, None] >= i[None, :])
    parts["ident2"] = (i[:, None] % CH) == t[None, :]

    def rotation(width, half):
        m = np.zeros((P, P))
        for c in range(P):
            d = c % width
            if d < half:
                m[c + half, c] = -1.0
            elif d < 2 * half:
                m[c - half, c] = 1.0
        return m

    parts["rot_head"] = rotation(64, 8)
    parts["rot_index"] = rotation(32, 4)
    parts["rot_axial"] = rotation(32, 16)
    q, k = i[:, None], i[None, :]
    causal = k <= q
    parts["neg_causal"] = np.where(causal, 0.0, NEG)
    parts["neg_prev"] = np.where(k >= q, 0.0, NEG)
    parts["neg_mod4"] = np.where(causal & ((q - k) % 4 == 0), 0.0, NEG)
    r, c = t[:, None], t[None, :]
    lower = []
    for s in LEVELS:
        lower.append((r // (2 * s) == c // (2 * s)) & (r % (2 * s) >= s) & (c % (2 * s) < s))
    lower = np.stack(lower)
    upper = lower.transpose(0, 2, 1)
    two = lambda m: np.concatenate([m, m], axis=0)
    wide = lambda ms: two(np.concatenate(list(ms), axis=1))
    parts["level"] = wide([m for s in range(6) for m in (lower[s], upper[s], lower[s])])
    parts["strict"] = wide([c < r, c > r])
    parts["strict_T"] = wide([c > r, c < r])
    parts["incl_T"] = wide([c >= r, c <= r])
    parts["chunk_carry"] = np.broadcast_to((np.arange(S) % CH) != 0, (P, S))

    parts["slots"] = np.broadcast_to(np.arange(64)[None, :], (P, 64))
    return {n: np.asarray(a, np.float32) for n, a in parts.items()}


def rope_tables():
    tables = {}
    pos = np.arange(S, dtype=np.float32)

    def rope(width, half, rows, ang):
        cos, sin = np.ones((P, S), np.float32), np.zeros((P, S), np.float32)
        for ch in range(P):
            d = ch % width
            if d < 2 * half:
                cos[ch], sin[ch] = np.cos(ang[:, d % half]), np.sin(ang[:, d % half])
        return cos, sin

    for name, width, half in (("head", 64, 8), ("index", 32, 4)):
        inv = np.float32(500000.0) ** (-np.arange(half, dtype=np.float32) / np.float32(half))
        cos, sin = rope(width, half, P, pos[:, None] * inv[None, :].astype(np.float32))
        tables[f"cos_{name}"], tables[f"sin_{name}"] = cos, sin
    freqs = np.float32(10000.0) ** (-(np.arange(16, dtype=np.float32) * np.float32(2.0) / np.float32(32)))
    cos, sin = np.ones((P, S), np.float32), np.zeros((P, S), np.float32)
    for ch in range(P):
        where = (np.arange(S) // 64 if ch % 64 < 32 else np.arange(S) % 64).astype(np.float32)
        ang = where * freqs[ch % 16]
        cos[ch], sin[ch] = np.cos(ang), np.sin(ang)
    tables["cos_axial"], tables["sin_axial"] = cos, sin
    return tables


def constant_offsets():
    at, where = 0, {}
    for n, a in constant_parts().items():
        where[n] = (at, a.shape[1])
        at += a.shape[1]
    return where, at


LAYER_COLUMNS = (("norm_g", 8), ("mu", N_R), ("w0", 3), ("a0", 3), ("k_k", 3), ("k_a", 3), ("r_k", 3),
                 ("ln_g", 3), ("ln_b", 3), ("ple_g", 8))
LAST_COLUMNS = (("final_g", 8), ("norm1", 8), ("norm2", 8), ("b_ada", 48), ("c", 8), ("q_norm", 1),
                ("k_norm", 1), ("dn_norm", 1), ("conv", 60), ("a_log", 8), ("dt_bias", 8))


def offsets(columns):
    at, where = 0, {}
    for n, k in columns:
        where[n] = (at, k)
        at += k
    return where, at


class Core:

    def __init__(self, ps, c, cols, last):
        self.ps, self.c, self.cols, self.last, self.table = ps, c, cols, last, None


class Job:

    def __init__(self, q, k, keys, bias, v, out, gate, rows):
        self.q, self.k, self.keys, self.bias, self.v, self.out, self.gate, self.rows = q, k, keys, bias, v, out, gate, rows


JOINED = []


@contextmanager
def together(nc):
    with ExitStack() as stack:
        cleared = []
        with nc.Block(no_gpsimd_drain=True) as block:
            JOINED.append((block, stack, cleared))
            yield
            JOINED.pop()
        for sem in cleared:
            nc.sync.sem_clear(sem)
        nc.all_engine_barrier()


@contextmanager
def phase(nc, **counts):
    with ExitStack() as stack:
        sems = {}
        for name, n in counts.items():
            made = [stack.enter_context(nc.semaphore(f"{name}_{i}_{nc.next_id()}")) for i in range(max(n, 1))]
            sems[name] = made if n else made[0]
            if JOINED:
                JOINED[-1][2].extend(made)
        if JOINED:
            JOINED[-1][1].push(stack.pop_all())
            yield JOINED[-1][0], sems
            return
        with nc.Block(no_gpsimd_drain=True) as block:
            yield block, sems
        for made in sems.values():
            for sem in made if isinstance(made, list) else [made]:
                nc.sync.sem_clear(sem)
        nc.all_engine_barrier()


class Own:

    def __init__(self, eng, sem):
        self.eng, self.sem, self.n = eng, sem, 0

    def mark(self, ins):
        self.n += 1
        ins.then_inc(self.sem, 1)
        return self.n

    def step(self, ins):
        self.mark(ins)
        self.eng.wait_ge(self.sem, self.n)

    def settle(self):
        self.eng.wait_ge(self.sem, self.n)


def buffer(nc, stack, name, shape):
    stack = JOINED[-1][1] if JOINED else stack
    return stack.enter_context(nc.sbuf_tensor(f"{name}_{nc.next_id()}", list(shape), F32))


def load(nc, *pairs):
    with phase(nc, loaded=0) as (block, s):
        @block.sync
        def _(sp):
            for target, source in pairs:
                sp.dma_start(target, source).then_inc(s["loaded"], 16)
    return s["loaded"], 16 * len(pairs)


def norm(nc, M, src, gain, out, scratch=None, shift=None, source=None, params=None):
    total = M.ps[:, 7, :]
    squares = out if scratch is None else scratch
    with ExitStack() as stack:
        rstd = buffer(nc, stack, "rstd", [P, S])
        with phase(nc, squared=0, summed=0, var_ready=0, root_ready=0, dve=0) as (block, s):
            @block.scalar
            def _(act):
                for k in range(KT):
                    if source:
                        act.wait_ge(source[0], source[1] + k)
                    nc.scalar.activation(squares[:, k, :], src[:, k, :], ACT.Square).then_inc(s["squared"], 1)
                act.wait_ge(s["var_ready"], 1)
                nc.scalar.activation(rstd[:, :], rstd[:, :], ACT.Sqrt).then_inc(s["root_ready"], 1)
                if shift is not None:
                    for k in range(KT):
                        act.wait_ge(s["dve"], k + 2)
                        nc.scalar.activation(out[:, k, :], out[:, k, :], ACT.Identity,
                                             bias=shift(k)).then_inc(s["squared"], 1)

            @block.tensor
            def _(pe):
                for k in range(KT):
                    pe.wait_ge(s["squared"], k + 1)
                    last = nc.tensor.matmul(total, M.c("ones"), squares[:, k, :], start=(k == 0),
                                            stop=(k == KT - 1))
                last.then_inc(s["summed"], 1)

            @block.vector
            def _(dve):
                own = Own(dve, s["dve"])
                dve.wait_ge(s["summed"], 1)
                own.step(nc.vector.tensor_scalar(rstd[:, :], total, 1.0 / D, NORM_EPS, ALU.mult, ALU.add))
                nc.vector.reciprocal(rstd[:, :], rstd[:, :]).then_inc(s["var_ready"], 1)
                dve.wait_ge(s["root_ready"], 1)
                if params:
                    dve.wait_ge(*params)
                for k in range(KT):
                    own.mark(nc.vector.scalar_tensor_tensor(out=out[:, k, :], in0=src[:, k, :], scalar=gain(k),
                                                            in1=rstd[:, :], op0=ALU.mult, op1=ALU.mult))
    return (s["dve"], KT + 1) if shift is None else (s["squared"], 2 * KT)


def project(nc, M, weights, n, kt, src, unroll, finish, ready=None):
    ps = M.ps
    assert n % unroll == 0
    rounds = n // unroll
    with ExitStack() as stack:
        ring = buffer(nc, stack, "weight_ring", [P, unroll, kt, P])
        with phase(nc, landed=unroll, tile_done=unroll, bank_free=unroll) as (block, s):
            @block.sync
            def _(sp):
                for u in range(unroll):
                    sp.dma_start(ring[:, u], weights(u)).then_inc(s["landed"][u], 16)
                if rounds > 1:
                    with sp.Fori(1, rounds) as r:
                        for u in range(unroll):
                            sp.wait_ge(s["tile_done"][u], r)
                            sp.dma_start(ring[:, u], weights(r * unroll + u)).then_inc(s["landed"][u], 16)

            @block.tensor
            def _(pe):
                if ready:
                    pe.wait_ge(*ready)
                with pe.Fori(0, rounds) as r:
                    for u in range(unroll):
                        pe.wait_ge(s["landed"][u], r * 16 + 16)
                        pe.wait_ge(s["bank_free"][u], r + 1)
                        for k in range(kt):
                            last = nc.tensor.matmul(ps[:, u, :], ring[:, u, k, :], src[:, k, :],
                                                    start=(k == 0), stop=(k == kt - 1))
                        last.then_inc(s["tile_done"][u], 1)

            @block.scalar
            def _(act):
                for u in range(unroll):
                    act.sem_inc(s["bank_free"][u], 1)
                with act.Fori(0, rounds) as r:
                    for u in range(unroll):
                        act.wait_ge(s["tile_done"][u], r + 1)
                        finish(act, r * unroll + u, ps[:, u, :]).then_inc(s["bank_free"][u], 1)


class SideProjection:
    SEMAPHORES = dict(side_landed=4, side_done=0, side_taken=0)

    def __init__(self, nc, M, tiles, kt, src, ring, slots, banks):
        self.nc, self.ps, self.tiles, self.kt, self.src, self.banks = nc, M.ps, tiles, kt, src, banks
        self.ring, self.slots = ring, slots
        self.products = kt * len(tiles)
        self.multiplied = self.taken = 0

    def attach(self, s):
        self.s = s

    def load(self, sp):
        for j, (weights, _) in enumerate(self.tiles):
            if j >= self.slots:
                sp.wait_ge(self.s["side_done"], j - self.slots + 1)
            sp.dma_start(self.ring[:, j % self.slots], weights).then_inc(self.s["side_landed"][j % self.slots], 16)

    def multiply(self, pe, upto):
        banks = len(self.banks)
        while self.multiplied < min(upto, self.products):
            j, k = divmod(self.multiplied, self.kt)
            if k == 0:
                pe.wait_ge(self.s["side_landed"][j % self.slots], 16 * (j // self.slots) + 16)
                if j >= banks:
                    pe.wait_ge(self.s["side_taken"], j - banks + 1)
            ins = self.nc.tensor.matmul(self.ps[:, self.banks[j % banks], :], self.ring[:, j % self.slots, k, :],
                                        self.src[:, k, :], start=(k == 0), stop=(k == self.kt - 1))
            if k == self.kt - 1:
                ins.then_inc(self.s["side_done"], 1)
            self.multiplied += 1

    def take(self, act, upto):
        while self.taken < min(upto, len(self.tiles)):
            j = self.taken
            act.wait_ge(self.s["side_done"], j + 1)
            self.tiles[j][1](act, self.ps[:, self.banks[j % len(self.banks)], :]).then_inc(self.s["side_taken"], 1)
            self.taken += 1


def token_major(nc, M, weights, width, src, out, slices, ready=None):
    ps = M.ps
    with ExitStack() as stack:
        w = buffer(nc, stack, "token_weights", [P, KT, width])
        with phase(nc, landed=0, tile_done=0, copied=0) as (block, s):
            @block.sync
            def _(sp):
                sp.dma_start(w[:, :, :], weights).then_inc(s["landed"], 16)

            @block.tensor
            def _(pe):
                pe.wait_ge(s["landed"], 16)
                if ready:
                    pe.wait_ge(*ready)
                for t in range(TT):
                    for a, b, tokens in slices:
                        for k in range(KT):
                            last = nc.tensor.matmul(ps[:, 4 + t, a:b], tokens(src[:, k, :], t), w[:, k, a:b],
                                                    start=(k == 0), stop=(k == KT - 1))
                    last.then_inc(s["tile_done"], 1)

            @block.vector
            def _(dve):
                for t in range(TT):
                    dve.wait_ge(s["tile_done"], t + 1)
                    nc.vector.tensor_copy(out[:, t, :], ps[:, 4 + t, 0:width]).then_inc(s["copied"], 1)


def in_order(row, t):
    return row[:, t * P:(t + 1) * P]


def by_residue(row, t):
    return row.rearrange("p (i r) -> p r i", r=4)[:, t, :]


def rope(nc, M, z, jobs):
    ps = M.ps
    with ExitStack() as stack:
        turned = buffer(nc, stack, "turned", [P, 2, S])
        with phase(nc, rotated=0, scaled=0, rot_used=0, dve=0) as (block, s):
            @block.tensor
            def _(pe):
                for j, (tile, table) in enumerate(jobs):
                    if j >= 4:
                        pe.wait_ge(s["rot_used"], j - 3)
                    nc.tensor.matmul(ps[:, j % 4, :], M.c(f"rot_{table}"), z[:, tile, :], start=True,
                                     stop=True).then_inc(s["rotated"], 1)

            @block.gpsimd
            def _(pool):
                for j, (tile, table) in enumerate(jobs):
                    pool.wait_ge(s["rotated"], j + 1)
                    nc.gpsimd.tensor_tensor(z[:, tile, :], z[:, tile, :], M.table(f"cos_{table}"),
                                            ALU.mult).then_inc(s["scaled"], 1)

            @block.vector
            def _(dve):
                own = Own(dve, s["dve"])
                for j, (tile, table) in enumerate(jobs):
                    dve.wait_ge(s["rotated"], j + 1)
                    if j >= 2:
                        dve.wait_ge(s["dve"], j - 1)
                    nc.vector.tensor_tensor(turned[:, j % 2, :], ps[:, j % 4, :], M.table(f"sin_{table}"),
                                            ALU.mult).then_inc(s["rot_used"], 1)
                    dve.wait_ge(s["rot_used"], j + 1)
                    dve.wait_ge(s["scaled"], j + 1)
                    own.mark(nc.vector.tensor_tensor(z[:, tile, :], z[:, tile, :], turned[:, j % 2, :], ALU.add))


def attention(nc, M, jobs, maxima, sums, side):
    ps, n = M.ps, len(jobs)
    side_share = lambda i: -(-side.products * i // n)
    scale = HD ** -0.5
    with ExitStack() as stack:
        sb = lambda name, shape: buffer(nc, stack, name, shape)
        scores, probs, probs_t = sb("scores", [P, 2, S]), sb("probs", [P, 2, S]), sb("probs_t", [P, 2, S])
        minus_max, inverse = sb("minus_max", [P, 2]), sb("inverse", [P, 2])
        with phase(nc, scores_ready=0, bank_free=0, max_ready=0, exp_done=0, probs_ready=0, transposed=0,
                   probs_t_ready=0, pv_done=0, out_done=0, dve=0, **SideProjection.SEMAPHORES) as (block, s):
            side.attach(s)

            @block.sync
            def _(sp):
                side.load(sp)

            @block.tensor
            def _(pe):
                for i in range(n + 3):
                    if i < n:
                        job = jobs[i]
                        if i >= 2:
                            pe.wait_ge(s["bank_free"], i - 1)
                        nc.tensor.matmul(ps[:, i % 2, 0:job.keys], job.q, job.k, start=True,
                                         stop=True).then_inc(s["scores_ready"], 1)
                    side.multiply(pe, (side_share(i) + side_share(i + 1)) // 2)
                    if 2 <= i <= n + 1:
                        j = i - 2
                        pe.wait_ge(s["probs_ready"], j + 1)
                        if j >= 2:
                            pe.wait_ge(s["probs_t_ready"], j - 1)
                        for t in range(jobs[j].keys // P):
                            last = nc.tensor.transpose(ps[:, 2 + j % 2, t * P:(t + 1) * P],
                                                       probs[:, j % 2, t * P:(t + 1) * P], M.c("ident"))
                        last.then_inc(s["transposed"], 1)
                    side.multiply(pe, side_share(i + 1))
                    if i >= 3:
                        j = i - 3
                        job = jobs[j]
                        pe.wait_ge(s["probs_t_ready"], j + 1)
                        if j >= 2:
                            pe.wait_ge(s["out_done"], j - 1)
                        for t, v in enumerate(job.v):
                            last = nc.tensor.matmul(ps[job.rows:job.rows + HD, 4 + j % 2, 0:P], v,
                                                    probs_t[:, j % 2, t * P:(t + 1) * P],
                                                    start=(t == 0), stop=(t == len(job.v) - 1))
                        last.then_inc(s["pv_done"], 1)

            @block.scalar
            def _(act):
                for i in range(n + 2):
                    if i < n:
                        job = jobs[i]
                        act.wait_ge(s["max_ready"], i + 1)
                        if i >= 2:
                            act.wait_ge(s["transposed"], i - 1)
                        source = ps[:, i % 2, 0:job.keys] if job.bias is None else scores[:, i % 2, 0:job.keys]
                        nc.scalar.activation(probs[:, i % 2, 0:job.keys], source, ACT.Exp,
                                             bias=minus_max[:, i % 2:i % 2 + 1],
                                             scale=scale if job.bias is None else 1.0,
                                             accum_out=sums[:, i:i + 1]).then_inc(s["exp_done"], 1)
                        if job.bias is None:
                            act.wait_ge(s["exp_done"], i + 1)
                            act.sem_inc(s["bank_free"], 1)
                    if i >= 2:
                        j = i - 2
                        act.wait_ge(s["transposed"], j + 1)
                        if j >= 2:
                            act.wait_ge(s["pv_done"], j - 1)
                        nc.scalar.activation(probs_t[:, j % 2, 0:jobs[j].keys], ps[:, 2 + j % 2, 0:jobs[j].keys],
                                             ACT.Copy).then_inc(s["probs_t_ready"], 1)
                    side.take(act, side_share(i) // side.kt)
                side.take(act, len(side.tiles))

            @block.vector
            def _(dve):
                own = Own(dve, s["dve"])
                for i in range(n + 3):
                    if i < n:
                        job = jobs[i]
                        dve.wait_ge(s["scores_ready"], i + 1)
                        if i >= 2:
                            dve.wait_ge(s["exp_done"], i - 1)
                        source = ps[:, i % 2, 0:job.keys]
                        if job.bias is not None:
                            nc.vector.scalar_tensor_tensor(out=scores[:, i % 2, 0:job.keys], in0=source, scalar=scale,
                                                           in1=job.bias, op0=ALU.mult,
                                                           op1=ALU.add).then_inc(s["bank_free"], 1)
                            dve.wait_ge(s["bank_free"], i + 1)
                            source = scores[:, i % 2, 0:job.keys]
                        own.step(nc.vector.reduce_max(maxima[:, i:i + 1], source, AX.X))
                        nc.vector.tensor_scalar(minus_max[:, i % 2:i % 2 + 1], maxima[:, i:i + 1],
                                                -scale if job.bias is None else -1.0, None,
                                                ALU.mult).then_inc(s["max_ready"], 1)
                    if 1 <= i <= n:
                        j = i - 1
                        dve.wait_ge(s["exp_done"], j + 1)
                        own.step(nc.vector.reciprocal(inverse[:, j % 2:j % 2 + 1], sums[:, j:j + 1]))
                        keys = jobs[j].keys
                        nc.vector.tensor_scalar(probs[:, j % 2, 0:keys], probs[:, j % 2, 0:keys],
                                                inverse[:, j % 2:j % 2 + 1], None, ALU.mult).then_inc(s["probs_ready"], 1)
                    if i >= 3:
                        j = i - 3
                        job = jobs[j]
                        dve.wait_ge(s["pv_done"], j + 1)
                        made = ps[job.rows:job.rows + HD, 4 + j % 2, 0:P]
                        if job.gate is None:
                            nc.vector.tensor_copy(job.out, made).then_inc(s["out_done"], 1)
                        else:
                            nc.vector.tensor_tensor(job.out, made, job.gate, ALU.mult).then_inc(s["out_done"], 1)


def index_topk(nc, M, z, tok, bias, side):
    ps = M.ps
    with ExitStack() as stack:
        sb = lambda name, shape: buffer(nc, stack, name, shape)
        weight, relus, best = sb("index_weight", [P, TT, 8]), sb("relus", [P, 2, S]), sb("best", [P, 3, 8])
        with phase(nc, scored=0, relu_done=0, added=0, dve=0, **SideProjection.SEMAPHORES) as (block, s):
            side.attach(s)

            @block.sync
            def _(sp):
                side.load(sp)

            @block.tensor
            def _(pe):
                for j in range(24):
                    b, h = 1 + j // 8, j % 8
                    if j >= 4:
                        pe.wait_ge(s["relu_done"], j - 3)
                    rows = slice(32 * (h % 4), 32 * (h % 4) + 32)
                    nc.tensor.matmul(ps[:, h % 4, 0:(b + 1) * P], z[rows, A_IQ + h // 4, b * P:(b + 1) * P],
                                     z[rows, A_IK, 0:(b + 1) * P], start=True, stop=True,
                                     tile_position=(32 * (h % 4), 0)).then_inc(s["scored"], 1)
                    side.multiply(pe, 1*j-3)
                side.multiply(pe, side.products)

            @block.scalar
            def _(act):
                for j in range(24):
                    b, h = 1 + j // 8, j % 8
                    act.wait_ge(s["scored"], j + 1)
                    if j >= 2:
                        act.wait_ge(s["added"], j - 1)
                    nc.scalar.activation(relus[:, j % 2, 0:(b + 1) * P], ps[:, h % 4, 0:(b + 1) * P], ACT.Relu,
                                         scale=32 ** -0.5).then_inc(s["relu_done"], 1)
                    side.take(act, ((1*j-3) - 2) // KT)
                side.take(act, len(side.tiles))

            @block.vector
            def _(dve):
                own = Own(dve, s["dve"])
                own.step(nc.vector.tensor_scalar(weight[:, :, :], tok[:, :, V_IW:V_IW + 8], 8 ** -0.5, None, ALU.mult))
                own.step(nc.vector.tensor_copy(bias(0), M.c("neg_causal")))
                for j in range(24):
                    b, h = 1 + j // 8, j % 8
                    dve.wait_ge(s["relu_done"], j + 1)
                    r, w = relus[:, j % 2, 0:(b + 1) * P], weight[:, b, h:h + 1]
                    if h == 0:
                        ins = nc.vector.tensor_scalar(bias(b), r, w, None, ALU.mult)
                    else:
                        ins = nc.vector.scalar_tensor_tensor(out=bias(b), in0=r, scalar=w, in1=bias(b),
                                                             op0=ALU.mult, op1=ALU.add)
                    ins.then_inc(s["added"], 1)
                    dve.wait_ge(s["added"], j + 1)
                for b in range(1, TT):
                    last = bias(b)[:, b * P:(b + 1) * P]
                    own.step(nc.vector.tensor_tensor(last, last, M.c("neg_causal"), ALU.add))
                for turn in range(TOPK // 8):
                    for b in range(1, TT):
                        own.mark(nc.vector.max(best[:, b - 1, :], bias(b)))
                    own.settle()
                    for b in range(1, TT):
                        own.mark(nc.vector.match_replace(out=bias(b), in_to_replace=best[:, b - 1, :],
                                                         in_values=bias(b), imm_value=TAKEN))
                    own.settle()
                for b in range(1, TT):
                    own.mark(nc.vector.tensor_scalar(bias(b), bias(b), -2e38, NEG, ALU.is_gt, ALU.mult))


def combine_groups(nc, M, z, od, maxima, sums, y):
    ps = M.ps
    with ExitStack() as stack:
        sb = lambda name, shape: buffer(nc, stack, name, shape)
        lse, diag, first = sb("lse", [P, 24]), sb("diag", [P, 6, S]), sb("first", [P, S])
        top, share, total = sb("top", [P, S]), sb("share", [P, 3, S]), sb("total", [P, S])
        with phase(nc, logs=0, diag_ready=0, spread_done=0, first_ready=0, centred=0, exp_done=0, dve=0) as (block, s):
            @block.scalar
            def _(act):
                nc.scalar.activation(lse[:, :], sums, ACT.Ln).then_inc(s["logs"], 1)
                act.wait_ge(s["spread_done"], 6)
                nc.scalar.activation(first[:, :], ps[:, 0, :], ACT.Copy).then_inc(s["first_ready"], 1)
                act.wait_ge(s["centred"], 3)
                nc.scalar.activation(share[:, :, :], share[:, :, :], ACT.Exp).then_inc(s["exp_done"], 1)

            @block.tensor
            def _(pe):
                for g in range(3):
                    for j in range(2):
                        pe.wait_ge(s["diag_ready"], 2 * g + j + 1)
                        row = ps[HD * j:HD * j + HD, g, :]
                        out = row.rearrange("p (t i) -> p t i", t=4) if g == 0 else row.rearrange(
                            "p (i r) -> p r i", r=4)
                        nc.tensor.matmul(out, M.c("ones")[:, 0:HD],
                                         diag[:, 2 * g + j, :].rearrange("p (t i) -> p t i", t=4),
                                         start=True, stop=True).then_inc(s["spread_done"], 1)

            @block.vector
            def _(dve):
                own = Own(dve, s["dve"])
                dve.wait_ge(s["logs"], 1)
                own.step(nc.vector.tensor_tensor(lse[:, :], lse[:, :], maxima, ALU.add))
                for g in range(3):
                    for j in range(2):
                        col = lse[:, 8 * g + j:8 * g + j + 7:2].unsqueeze(2).broadcast_to([P, 4, P])
                        nc.vector.tensor_tensor(diag[:, 2 * g + j, :].rearrange("p (t i) -> p t i", t=4),
                                                M.c("ident").unsqueeze(1).broadcast_to([P, 4, P]), col,
                                                ALU.mult).then_inc(s["diag_ready"], 1)
                dve.wait_ge(s["first_ready"], 1)
                own.step(nc.vector.tensor_tensor(top[:, :], first[:, :], ps[:, 1, :], ALU.max))
                own.step(nc.vector.tensor_tensor(top[:, :], top[:, :], ps[:, 2, :], ALU.max))
                for g in range(3):
                    nc.vector.tensor_tensor(share[:, g, :], ps[:, g, :], top[:, :], ALU.subtract).then_inc(s["centred"], 1)
                dve.wait_ge(s["exp_done"], 1)
                own.step(nc.vector.tensor_tensor(total[:, :], share[:, 0, :], share[:, 1, :], ALU.add))
                own.step(nc.vector.tensor_tensor(total[:, :], total[:, :], share[:, 2, :], ALU.add))
                own.step(nc.vector.reciprocal(total[:, :], total[:, :]))
                for g in range(3):
                    own.mark(nc.vector.tensor_tensor(share[:, g, :], share[:, g, :], total[:, :], ALU.mult))
                own.settle()
                for g in range(3):
                    own.mark(nc.vector.tensor_tensor(share[:, g, :], share[:, g, :], od[:, g, :], ALU.mult))
                own.settle()
                for g in range(3):
                    own.mark(nc.vector.tensor_tensor(y[:, 5 + g, :], share[:, g, :], z[:, A_DG + g, :], ALU.mult))


def attention_branches(nc, M, h, y, w_attn, w_tok, w_rwkv, raw, make_h):
    with ExitStack() as stack:
        sb = lambda name, shape: buffer(nc, stack, name, shape)
        z, tok = sb("attn_z", [P, N_A, S]), sb("attn_tok", [P, TT, N_V])
        bias_all = sb("bias", [P, P + 2 * P + 3 * P + 4 * P])
        bias = lambda b: bias_all[:, P * (b * (b + 1) // 2):P * ((b + 1) * (b + 2) // 2)]
        od, maxima, sums = sb("dilated_out", [P, 3, S]), sb("maxima", [P, 40]), sb("sums", [P, 40])
        keep = lambda act, j, made: nc.scalar.activation(z[:, j, :], made, ACT.Copy)
        ring = sb("side_ring", [P, 4, KT, P])
        with together(nc):
            ready = make_h()
            project(nc, M, w_attn, A_G, KT, h, 4, keep, ready)
            token_major(nc, M, w_tok, N_V, h, tok, ((0, V_D1, in_order), (V_D1, N_V, by_residue)), ready)
        rope(nc, M, z, [(t, "head") for t in range(A_IQ)] + [(t, "index") for t in range(A_IQ, A_IK + 1)])
        silu = lambda j: (w_attn(j), lambda act, made: nc.scalar.activation(z[:, j, :], made, ACT.Silu))
        mixed = lambda j: (w_rwkv(j), lambda act, made: nc.scalar.activation(raw[:, j, 1:S + 1], made, ACT.Copy))
        early = 4
        side = SideProjection(nc, M, [silu(j) for j in range(A_G, N_A)] + [mixed(j) for j in range(early)], KT, h, ring,
                              4, (4, 5, 6, 7))
        index_topk(nc, M, z, tok, bias, side)
        jobs = []
        for b in range(TT):
            for hd in range(4):
                rows = HD * (hd % 2)
                here = slice(b * P, (b + 1) * P)
                jobs.append(Job(
                    q=z[rows:rows + HD, A_Q + hd // 2, here], k=z[rows:rows + HD, A_K, 0:(b + 1) * P],
                    keys=(b + 1) * P, bias=bias(b), v=[tok[:, t, V_DSA:V_DSA + HD] for t in range(b + 1)],
                    out=y[rows:rows + HD, 3 + hd // 2, here], gate=z[rows:rows + HD, A_G + hd // 2, here], rows=rows))
        both = sb("band", [P, 2 * P])
        with phase(nc, dve=0) as (block, s):
            @block.vector
            def _(dve):
                own = Own(dve, s["dve"])
                own.mark(nc.vector.memset(raw[:, :, 0:1], 0.0))
                own.mark(nc.vector.tensor_copy(both[:, 0:P], M.c("neg_prev")))
                own.mark(nc.vector.tensor_copy(both[:, P:2 * P], M.c("neg_causal")))
        for g in range(3):
            for t in range(TT):
                for j in range(2):
                    rows = HD * j
                    row = lambda buf, tile: buf[rows:rows + HD, tile, :]
                    v0 = (V_D0 if g == 0 else V_D1 + P * (g - 1)) + HD * j
                    if g == 0:
                        here, first = slice(t * P, (t + 1) * P), max(t - 1, 0)
                        job = Job(q=row(z, A_DQ)[:, here], k=row(z, A_DK)[:, first * P:(t + 1) * P],
                                              keys=(t + 1 - first) * P, bias=both[:, :] if t else M.c("neg_causal"),
                                              v=[tok[:, u, v0:v0 + HD] for u in range(first, t + 1)],
                                              out=row(od, 0)[:, here], gate=None, rows=rows)
                    else:
                        job = Job(q=by_residue(row(z, A_DQ + g), t), k=by_residue(row(z, A_DK + g), t),
                                              keys=P, bias=M.c("neg_causal" if g == 1 else "neg_mod4"),
                                              v=[tok[:, t, v0:v0 + HD]], out=by_residue(row(od, g), t),
                                              gate=None, rows=rows)
                    jobs.append(job)
        side = SideProjection(nc, M, [mixed(j) for j in range(early, N_R)], KT, h, ring, 4, (6, 7))
        attention(nc, M, jobs, maxima, sums, side)
        combine_groups(nc, M, z, od, maxima[:, 16:40], sums[:, 16:40], y)


def invert(nc, M, lower, inv, inv_t, groups, gsize, signs, dirs):
    ps = M.ps
    blocks = gsize
    level = M.c("level").rearrange("p (l d t) -> p l d t", l=6, d=3)
    strict_sum = ALU.subtract if signs > 0 else ALU.add

    def mask(lv, flip):
        m = level[:, lv, flip:flip + dirs, :]
        if dirs == 1:
            return m.broadcast_to([P, blocks, CH])
        return m.unsqueeze(2).broadcast_to([P, dirs, blocks // dirs, CH])

    def view(ap):
        return ap if dirs == 1 else ap.rearrange("p (d b) t -> p d b t", d=dirs)

    def bank(i):
        return ps[:, i, 0:blocks * CH].rearrange("p (b t) -> p b t", b=blocks)

    with ExitStack() as stack:
        sb = lambda name, shape: buffer(nc, stack, name, shape)
        half, parts = sb("half", [P, 2, blocks, CH]), sb("parts", [P, 2, 2, blocks, CH])
        eye = M.c("ident2").unsqueeze(1).broadcast_to([P, blocks, CH])
        with phase(nc, lt_ready=0, t_ready=0, half_ready=0, half_copied=0, product=0, product_used=0, dve=0) as (block, s):
            def pairs():
                for b in range(blocks):
                    for rows in (slice(0, HD), slice(HD, P)):
                        yield b, rows

            def second(pe, job):
                g = job % groups
                pe.wait_ge(s["half_copied"], job + 1)
                if job >= 2:
                    pe.wait_ge(s["product_used"], job - 1)
                for b, rows in pairs():
                    y = half[rows, job % 2, b, :]
                    if job < 4 * groups:
                        nc.tensor.matmul(bank(4 + job % 2)[rows, b, :], y, inv[rows, g, b, :], start=True, stop=True)
                    last = nc.tensor.matmul(bank(6 + job % 2)[rows, b, :], inv[rows, g, b, :], y, start=True, stop=True)
                last.then_inc(s["product"], 1)

            @block.tensor
            def _(pe):
                for g in range(groups):
                    if g >= 2:
                        pe.wait_ge(s["t_ready"], g - 1)
                    for b, rows in pairs():
                        last = nc.tensor.matmul(bank(g % 2)[rows, b, :], lower[rows, g, b, :],
                                                M.c("ident2")[rows, :], start=True, stop=True)
                    last.then_inc(s["lt_ready"], 1)
                job = 0
                for lv in range(1, 6):
                    for g in range(groups):
                        pe.wait_ge(s["t_ready"], lv * groups - groups + g + 1)
                        if job >= 2:
                            pe.wait_ge(s["half_copied"], job - 1)
                        for b, rows in pairs():
                            last = nc.tensor.matmul(bank(2 + job % 2)[rows, b, :], lower[rows, g, b, :],
                                                    inv_t[rows, g, b, :], start=True, stop=True)
                        last.then_inc(s["half_ready"], 1)
                        job += 1
                        if job >= 2:
                            second(pe, job - 2)
                second(pe, job - 1)

            @block.scalar
            def _(act):
                for job in range(5 * groups):
                    act.wait_ge(s["half_ready"], job + 1)
                    if job >= 2:
                        act.wait_ge(s["product"], job - 1)
                    nc.scalar.activation(half[:, job % 2], bank(2 + job % 2), ACT.Copy,
                                         ).then_inc(s["half_copied"], 1)

            @block.vector
            def _(dve):
                own = Own(dve, s["dve"])
                for g in range(groups):
                    dve.wait_ge(s["lt_ready"], g + 1)
                    own.mark(nc.vector.tensor_tensor(view(inv[:, g]), view(lower[:, g]), mask(0, 0), ALU.mult))
                    own.step(nc.vector.tensor_tensor(view(inv_t[:, g]), view(bank(g % 2)), mask(0, 1), ALU.mult))
                    own.mark(nc.vector.tensor_tensor(inv[:, g], eye, inv[:, g], strict_sum))
                    own.step(nc.vector.tensor_tensor(inv_t[:, g], eye, inv_t[:, g], strict_sum))
                    dve.sem_inc(s["t_ready"], 1)
                for job in range(5 * groups):
                    lv, g = 1 + job // groups, job % groups
                    dve.wait_ge(s["product"], job + 1)
                    k = job % 2
                    if lv < 5:
                        own.mark(nc.vector.tensor_tensor(view(parts[:, k, 0]), view(bank(4 + k)), mask(lv, 0), ALU.mult))
                    own.mark(nc.vector.tensor_tensor(view(parts[:, k, 1]), view(bank(6 + k)), mask(lv, 1), ALU.mult))
                    own.settle()
                    dve.sem_inc(s["product_used"], 1)
                    if lv < 5:
                        own.mark(nc.vector.tensor_tensor(inv[:, g], inv[:, g], parts[:, k, 0], strict_sum))
                    own.step(nc.vector.tensor_tensor(inv_t[:, g], inv_t[:, g], parts[:, k, 1], strict_sum))
                    dve.sem_inc(s["t_ready"], 1)


def rwkv_branch(nc, M, x, y, raw, up_weights, w_out, col):
    ps = M.ps
    with ExitStack() as outer:
        sb = lambda name, shape: buffer(nc, outer, name, shape)
        z = sb("mixed", [P, N_R, S])
        at, bt, kt_, bonus = (sb(x, [P, RP, S]) for x in ("rw_a", "rw_b", "rw_k", "bonus"))
        end_decay = sb("end_decay", [P, RP, NCH])
        r, k, v = z[:, R_R:R_R + 3, :], z[:, R_K:R_K + 3, :], z[:, R_V:R_V + 3, :]

        with phase(nc, dve=0) as (block, s):
            @block.vector
            def _(dve):
                own = Own(dve, s["dve"])
                own.step(nc.vector.tensor_tensor(z[:, :, :], raw[:, :, 0:S], raw[:, :, 1:S + 1], ALU.subtract))
                for j in range(N_R):
                    own.mark(nc.vector.scalar_tensor_tensor(out=z[:, j, :], in0=z[:, j, :], scalar=col("mu", j),
                                                            in1=raw[:, j, 1:S + 1], op0=ALU.mult, op1=ALU.add))

        with ExitStack() as stack:
            sbt = lambda name, shape: buffer(nc, stack, name, shape)
            up = sbt("up", [P, RW])
            logw, cum, rate, tmp = (sbt(x, [P, RP, S]) for x in ("logw", "cum", "rate", "tmp"))
            grow, keep = sbt("grow", [P, RP, S]), sbt("keep", [P, RP])
            with phase(nc, up_landed=0, tanh_done=0, raised=0, sig_done=0, log_ready=0, exps=0, squares=0, normed=0,
                       root_ready=0, root=0, rk_ready=0, rk_summed=0, gated=0, dve=0) as (block, s):
                @block.sync
                def _(sp):
                    sp.dma_start(up[:, :], up_weights).then_inc(s["up_landed"], 16)

                @block.tensor
                def _(pe):
                    pe.wait_ge(s["up_landed"], 16)
                    pe.wait_ge(s["tanh_done"], 1)
                    for j in range(RP):
                        nc.tensor.matmul(ps[:, j, :], up[0:HD, j * P:(j + 1) * P], z[0:HD, R_WA, :], start=True,
                                         stop=True).then_inc(s["raised"], 1)
                        nc.tensor.matmul(ps[:, 3 + j, :], up[HD:P, j * P:(j + 1) * P], z[HD:P, R_WA, :],
                                         start=True, stop=True).then_inc(s["raised"], 1)
                    pe.wait_ge(s["squares"], 1)
                    pe.wait_ge(s["sig_done"], 6)
                    for j in range(RP):
                        nc.tensor.matmul(ps[:, j, :], M.c("head_ones"), tmp[:, j, :], start=True,
                                         stop=True).then_inc(s["normed"], 1)
                    pe.wait_ge(s["rk_ready"], 1)
                    for j in range(RP):
                        nc.tensor.matmul(ps[:, 3 + j, :], M.c("head_ones"), bonus[:, j, :], start=True,
                                         stop=True).then_inc(s["rk_summed"], 1)

                @block.scalar
                def _(act):
                    nc.scalar.activation(z[0:HD, R_WA, :], z[0:HD, R_WA, :], ACT.Tanh).then_inc(s["tanh_done"], 1)
                    for j in range(RP):
                        act.wait_ge(s["raised"], 2 * j + 2)
                        nc.scalar.activation(logw[:, j, :], ps[:, j, :], ACT.Sigmoid,
                                             bias=col("w0", j)).then_inc(s["sig_done"], 1)
                        nc.scalar.activation(rate[:, j, :], ps[:, 3 + j, :], ACT.Sigmoid,
                                             bias=col("a0", j)).then_inc(s["sig_done"], 1)
                    act.wait_ge(s["root_ready"], 1)
                    nc.scalar.activation(tmp[:, :, :], tmp[:, :, :], ACT.Copy).then_inc(s["squares"], 1)
                    for j in range(RP):
                        act.wait_ge(s["normed"], j + 1)
                        nc.scalar.activation(grow[:, j, :], ps[:, j, :], ACT.Sqrt).then_inc(s["root"], 1)
                    act.wait_ge(s["log_ready"], 1)
                    act.wait_ge(s["rk_ready"], 1)
                    nc.scalar.activation(tmp[:, :, :], cum[:, :, :], ACT.Exp).then_inc(s["exps"], 1)
                    act.wait_ge(s["root_ready"], 2)
                    nc.scalar.activation(grow[:, :, :], cum[:, :, :], ACT.Exp, scale=-1.0).then_inc(s["exps"], 1)
                    nc.scalar.activation(logw[:, :, :], logw[:, :, :], ACT.Exp).then_inc(s["exps"], 1)
                    nc.scalar.activation(z[:, R_G:R_G + 3, :], z[:, R_G:R_G + 3, :], ACT.Silu).then_inc(s["gated"], 1)

                @block.vector
                def _(dve):
                    own = Own(dve, s["dve"])
                    V = nc.vector
                    own.mark(V.tensor_scalar(keep[:, :], M.cols("k_a"), -1.0, 1.0, ALU.mult, ALU.add))
                    for j in range(RP):
                        own.mark(V.tensor_scalar(at[:, j, :], k[:, j, :], col("k_k", j), None, ALU.mult))
                    own.settle()
                    V.tensor_tensor(tmp[:, :, :], at[:, :, :], at[:, :, :], ALU.mult).then_inc(s["root_ready"], 1)
                    dve.wait_ge(s["sig_done"], 6)
                    own.step(V.tensor_scalar(logw[:, :, :], logw[:, :, :], -DECAY_SCALE, None, ALU.mult))
                    for j in range(RP):
                        own.mark(V.tensor_tensor_scan(cum[:, j, :], M.c("chunk_carry"), logw[:, j, :], 0.0,
                                                      ALU.mult, ALU.add))
                    own.settle()
                    V.tensor_tensor(logw[:, :, :], cum[:, :, :], logw[:, :, :], ALU.subtract).then_inc(s["log_ready"], 1)
                    dve.wait_ge(s["root"], 3)
                    own.step(V.tensor_scalar(grow[:, :, :], grow[:, :, :], 1e-12, None, ALU.max))
                    own.step(V.reciprocal(grow[:, :, :], grow[:, :, :]))
                    own.step(V.tensor_tensor(at[:, :, :], at[:, :, :], grow[:, :, :], ALU.mult))
                    dve.sem_inc(s["root_ready"], 1)
                    dve.wait_ge(s["normed"], 3)
                    for j in range(RP):
                        own.mark(V.tensor_scalar(tmp[:, j, :], rate[:, j, :], col("k_a", j), keep[:, j:j + 1],
                                                 ALU.mult, ALU.add))
                    own.settle()
                    own.step(V.tensor_tensor(k, k, tmp[:, :, :], ALU.mult))
                    for j in range(RP):
                        own.mark(V.scalar_tensor_tensor(out=bonus[:, j, :], in0=r[:, j, :], scalar=col("r_k", j),
                                                        in1=k[:, j, :], op0=ALU.mult, op1=ALU.mult))
                    own.settle()
                    own.step(V.tensor_tensor(bt[:, :, :], at[:, :, :], rate[:, :, :], ALU.mult))
                    dve.sem_inc(s["rk_ready"], 1)
                    dve.wait_ge(s["exps"], 3)
                    own.mark(V.tensor_tensor(bt[:, :, :], bt[:, :, :], grow[:, :, :], ALU.mult))
                    own.mark(V.tensor_tensor(kt_[:, :, :], k, grow[:, :, :], ALU.mult))
                    own.mark(V.scalar_tensor_tensor(out=at[:, :, :], in0=at[:, :, :], scalar=-1.0, in1=logw[:, :, :],
                                                    op0=ALU.mult, op1=ALU.mult))
                    own.mark(V.tensor_tensor(r, r, tmp[:, :, :], ALU.mult))
                    own.mark(V.tensor_copy(end_decay[:, :, :], tmp[:, :, CH - 1:S:CH]))
                    dve.wait_ge(s["rk_summed"], 3)
                    for j in range(RP):
                        own.mark(V.tensor_tensor(bonus[:, j, :], ps[:, 3 + j, :], v[:, j, :], ALU.mult))

        with ExitStack() as stack:
            sbt = lambda name, shape: buffer(nc, stack, name, shape)
            block_shape = [P, NCH, RP, CH]
            ak_t, rb_t, rk_t = (sbt(x, block_shape) for x in ("ak_t", "rb_t", "rk_t"))
            spare = raw[:, :, :].rearrange("p j n -> p (j n)")[:, 0:4 * RP * S]
            v_tok, b_tok, k_tok, low = (spare[:, i * RP * S:(i + 1) * RP * S].rearrange("p (c j t) -> p c j t", c=NCH, j=RP)
                                        for i in range(4))
            inv, inv_t = sbt("inv", block_shape), sbt("inv_t", block_shape)
            chunked = lambda ap: ap.rearrange("p j (c t) -> p c j t", t=CH)
            rc, kc, vc, ac, bc = (chunked(x) for x in (r, kt_[:, :, :], v, at[:, :, :], bt[:, :, :]))
            eye = lambda c, j, rows: M.c("ident2")[rows, :]
            pick = lambda ap: (lambda c, j, rows: ap[rows, c, j, :])
            kinds = ((v_tok, pick(vc), eye, None), (b_tok, pick(bc), eye, None), (k_tok, pick(kc), eye, None),
                     (low, pick(ac), pick(bc), "strict"), (ak_t, pick(kc), pick(ac), "strict_T"),
                     (rb_t, pick(bc), pick(rc), "incl_T"), (rk_t, pick(kc), pick(rc), "incl_T"))
            bank = lambda i: ps[:, i, 0:2 * RP * CH].rearrange("p (c j t) -> p c j t", c=2, j=RP)
            todo = [(kind, c2) for c2 in range(NCH // 2) for kind in kinds]
            with phase(nc, made=0, taken=0) as (block, s):
                @block.tensor
                def _(pe):
                    for i, ((_, lhs, rhs, _), c2) in enumerate(todo):
                        if i >= 4:
                            pe.wait_ge(s["taken"], i - 3)
                        for c in range(2):
                            for j in range(RP):
                                for rows in (slice(0, HD), slice(HD, P)):
                                    last = nc.tensor.matmul(bank(i % 4)[rows, c, j, :], lhs(2 * c2 + c, j, rows),
                                                            rhs(2 * c2 + c, j, rows), start=True, stop=True)
                        last.then_inc(s["made"], 1)

                @block.vector
                def _(dve):
                    for i, ((target, _, _, mask), c2) in enumerate(todo):
                        dve.wait_ge(s["made"], i + 1)
                        out = target[:, 2 * c2:2 * c2 + 2]
                        if mask is None:
                            ins = nc.vector.tensor_copy(out, bank(i % 4))
                        else:
                            out = out.rearrange("p c j t -> p (c j) t")
                            made = bank(i % 4).rearrange("p c j t -> p (c j) t")
                            m = M.c(mask)[:, 0:CH].unsqueeze(1).broadcast_to([P, 2 * RP, CH])
                            ins = nc.vector.tensor_tensor(out, made, m, ALU.mult)
                        ins.then_inc(s["taken"], 1)

            pairs_of = lambda a: a[:, :, :, :].rearrange("p (g c) j t -> p g (c j) t", c=2)
            invert(nc, M, pairs_of(low), pairs_of(inv), pairs_of(inv_t), NCH // 2, 2 * RP, -1, 1)

            add = lambda j: (w_out(j)[:, RP:KT, :], lambda dve, made: nc.vector.tensor_tensor(x[:, j, :], made, x[:, j, :], ALU.add))
            side = SideProjection(nc, M, [add(j) for j in range(KT)], KT - RP, y[:, RP:KT, :],
                                  sbt("side_ring", [P, 4, KT - RP, P]), 4, (5, 6, 7))
            state, xs, sa = sbt("state", [P, 2, RP, HD]), sbt("xs", [P, 2, RP, CH]), sbt("sa", [P, 2, RP, CH])
            with phase(nc, zeroed=0, x_made=0, x_ready=0, sa_made=0, sa_ready=0, state_made=0, state_ready=0,
                       y_made=0, y_ready=0, dve=0, **SideProjection.SEMAPHORES) as (block, s):
                side.attach(s)

                @block.sync
                def _(sp):
                    side.load(sp)

                rows2 = (slice(0, HD), slice(HD, P))
                part = lambda i: ps[:, i, 0:RP * CH].rearrange("p (j t) -> p j t", j=RP)

                @block.tensor
                def _(pe):
                    mm = nc.tensor.matmul
                    for c in range(NCH):
                        old = state[:, c % 2]
                        pe.wait_ge(s["state_ready"], c + 1)
                        for j in range(RP):
                            for w in rows2:
                                mm(part(0)[w, j, :], ac[w, c, j, :], old[w, j, :], start=True, stop=False)
                                last = mm(part(0)[w, j, :], ak_t[w, c, j, :], v_tok[w, c, j, :], start=False, stop=True)
                        last.then_inc(s["x_made"], 1)
                        side.multiply(pe, (KT - RP) * c + 2)
                        pe.wait_ge(s["x_ready"], c + 1)
                        for j in range(RP):
                            for w in rows2:
                                last = mm(part(1)[w, j, :], inv_t[w, c, j, :], xs[w, c % 2, j, :], start=True, stop=True)
                        last.then_inc(s["sa_made"], 1)
                        side.multiply(pe, (KT - RP) * c + 4)
                        pe.wait_ge(s["sa_ready"], c + 1)
                        for j in range(RP):
                            for w in rows2:
                                mm(part(2)[w, j, :], b_tok[w, c, j, :], sa[w, c % 2, j, :], start=True, stop=False)
                                last = mm(part(2)[w, j, :], k_tok[w, c, j, :], v_tok[w, c, j, :], start=False, stop=True)
                        last.then_inc(s["state_made"], 1)
                        if c >= 2:
                            pe.wait_ge(s["y_ready"], c - 1)
                        for j in range(RP):
                            for w in rows2:
                                mm(part(3 + c % 2)[w, j, :], old[w, j, :], rc[w, c, j, :], start=True, stop=False)
                                mm(part(3 + c % 2)[w, j, :], sa[w, c % 2, j, :], rb_t[w, c, j, :], start=False, stop=False)
                                last = mm(part(3 + c % 2)[w, j, :], v_tok[w, c, j, :], rk_t[w, c, j, :], start=False, stop=True)
                        last.then_inc(s["y_made"], 1)
                        side.multiply(pe, (KT - RP) * (c + 1))

                @block.scalar
                def _(act):
                    for c in range(NCH):
                        act.wait_ge(s["y_made"], c + 1)
                        nc.scalar.activation(y[:, 0:RP, c * CH:(c + 1) * CH], part(3 + c % 2), ACT.Copy).then_inc(s["y_ready"], 1)

                @block.vector
                def _(dve):
                    own = Own(dve, s["dve"])
                    nc.vector.memset(state[:, 0], 0.0).then_inc(s["state_ready"], 1)
                    for c in range(NCH):
                        dve.wait_ge(s["x_made"], c + 1)
                        nc.vector.tensor_copy(xs[:, c % 2], part(0)).then_inc(s["x_ready"], 1)
                        dve.wait_ge(s["sa_made"], c + 1)
                        nc.vector.tensor_copy(sa[:, c % 2], part(1)).then_inc(s["sa_ready"], 1)
                        if c == NCH - 1:
                            break
                        side.take(dve, c)
                        dve.wait_ge(s["state_made"], c + 1)
                        if c >= 1:
                            dve.wait_ge(s["y_made"], c)
                        new = state[:, (c + 1) % 2]
                        own.step(nc.vector.tensor_tensor(new, part(2), state[:, c % 2], ALU.add))
                        nc.vector.tensor_tensor(new, new, end_decay[:, :, c:c + 1].broadcast_to([P, RP, HD]),
                                                ALU.mult).then_inc(s["state_ready"], 1)
                    side.take(dve, KT)

        with ExitStack() as stack:
            sbt = lambda name, shape: buffer(nc, stack, name, shape)
            sq, rstd = sbt("sq", [P, RP, S]), sbt("rstd", [P, RP, S])
            yr = y[:, 0:RP, :]
            with phase(nc, mean_made=0, squared=0, var_made=0, inv_ready=0, root=0, dve=0) as (block, s):
                @block.tensor
                def _(pe):
                    for j in range(RP):
                        nc.tensor.matmul(ps[:, j, :], M.c("head_ones"), y[:, j, :], start=True, stop=True).then_inc(s["mean_made"], 1)
                    for j in range(RP):
                        pe.wait_ge(s["squared"], j + 1)
                        nc.tensor.matmul(ps[:, 3 + j, :], M.c("head_ones"), sq[:, j, :], start=True, stop=True).then_inc(s["var_made"], 1)

                @block.scalar
                def _(act):
                    for j in range(RP):
                        act.wait_ge(s["dve"], j + 1)
                        nc.scalar.activation(sq[:, j, :], y[:, j, :], ACT.Square).then_inc(s["squared"], 1)
                    act.wait_ge(s["inv_ready"], 1)
                    nc.scalar.activation(rstd[:, :, :], rstd[:, :, :], ACT.Sqrt).then_inc(s["root"], 1)

                @block.vector
                def _(dve):
                    own = Own(dve, s["dve"])
                    for j in range(RP):
                        dve.wait_ge(s["mean_made"], j + 1)
                        own.mark(nc.vector.scalar_tensor_tensor(out=y[:, j, :], in0=ps[:, j, :], scalar=-1.0 / HD,
                                                                in1=y[:, j, :], op0=ALU.mult, op1=ALU.add))
                    for j in range(RP):
                        dve.wait_ge(s["var_made"], j + 1)
                        own.mark(nc.vector.tensor_scalar(rstd[:, j, :], ps[:, 3 + j, :], 1.0 / HD, 64e-5, ALU.mult, ALU.add))
                    own.settle()
                    nc.vector.reciprocal(rstd[:, :, :], rstd[:, :, :]).then_inc(s["inv_ready"], 1)
                    dve.wait_ge(s["root"], 1)
                    own.step(nc.vector.tensor_tensor(yr, yr, rstd[:, :, :], ALU.mult))
                    for j in range(RP):
                        own.mark(nc.vector.tensor_scalar(y[:, j, :], y[:, j, :], col("ln_g", j), col("ln_b", j),
                                                         ALU.mult, ALU.add))
                    own.settle()
                    own.step(nc.vector.tensor_tensor(yr, yr, bonus[:, :, :], ALU.add))
                    own.step(nc.vector.tensor_tensor(yr, yr, z[:, R_G:R_G + 3, :], ALU.mult))


def add_projection(nc, M, weights, n, kt, src, x, gain=None, ready=None):
    ps = M.ps
    with ExitStack() as stack:
        ring = buffer(nc, stack, "weight_ring", [P, 4, kt, P])
        with phase(nc, landed=4, tile_done=0, added=0) as (block, s):
            @block.sync
            def _(sp):
                for j in range(n):
                    if j >= 4:
                        sp.wait_ge(s["tile_done"], j - 3)
                    sp.dma_start(ring[:, j % 4], weights(j)).then_inc(s["landed"][j % 4], 16)

            @block.tensor
            def _(pe):
                if ready:
                    pe.wait_ge(*ready)
                for j in range(n):
                    pe.wait_ge(s["landed"][j % 4], 16 * (j // 4) + 16)
                    if j >= 4:
                        pe.wait_ge(s["added"], j - 3)
                    for k in range(kt):
                        last = nc.tensor.matmul(ps[:, j % 4, :], ring[:, j % 4, k, :], src[:, k, :],
                                                start=(k == 0), stop=(k == kt - 1))
                    last.then_inc(s["tile_done"], 1)

            @block.vector
            def _(dve):
                for j in range(n):
                    dve.wait_ge(s["tile_done"], j + 1)
                    if gain is None:
                        ins = nc.vector.tensor_tensor(x[:, j, :], ps[:, j % 4, :], x[:, j, :], ALU.add)
                    else:
                        ins = nc.vector.scalar_tensor_tensor(out=x[:, j, :], in0=ps[:, j % 4, :], scalar=gain(j),
                                                             in1=x[:, j, :], op0=ALU.mult, op1=ALU.add)
                    ins.then_inc(s["added"], 1)
    return s["added"], 1


def gated_embedding(nc, M, w_gate, w_proj, p_layer, h, x, ready):
    ps = M.ps
    with ExitStack() as stack:
        sb = lambda name, shape: buffer(nc, stack, name, shape)
        ring, proj, emb, gate = sb("weight_ring", [P, 4, KT, P]), sb("proj", [P, KT, 2, P]), sb("emb", [P, 2, S]), sb("gate", [P, 2, S])
        with phase(nc, small_landed=0, landed=4, tile_done=0, gated=0, scaled=0, added=0) as (block, s):
            @block.sync
            def _(sp):
                sp.dma_start(proj[:, :, :, :], w_proj).then_inc(s["small_landed"], 16)
                sp.dma_start(emb[:, :, :], p_layer).then_inc(s["small_landed"], 16)
                for j in range(KT):
                    if j >= 4:
                        sp.wait_ge(s["tile_done"], j - 3)
                    sp.dma_start(ring[:, j % 4], w_gate(j)).then_inc(s["landed"][j % 4], 16)

            @block.tensor
            def _(pe):
                pe.wait_ge(s["small_landed"], 32)
                pe.wait_ge(*ready)
                for j in range(KT):
                    pe.wait_ge(s["landed"][j % 4], 16 * (j // 4) + 16)
                    if j >= 4:
                        pe.wait_ge(s["added"], j - 3)
                    for k in range(2):
                        nc.tensor.matmul(ps[:, 4 + j % 4, :], proj[:, j, k, :], emb[:, k, :], start=(k == 0), stop=(k == 1))
                    for k in range(KT):
                        last = nc.tensor.matmul(ps[:, j % 4, :], ring[:, j % 4, k, :], h[:, k, :],
                                                start=(k == 0), stop=(k == KT - 1))
                    last.then_inc(s["tile_done"], 1)

            @block.scalar
            def _(act):
                for j in range(KT):
                    act.wait_ge(s["tile_done"], j + 1)
                    if j >= 2:
                        act.wait_ge(s["added"], j - 1)
                    nc.scalar.activation(gate[:, j % 2, :], ps[:, j % 4, :], ACT.Sigmoid).then_inc(s["gated"], 1)

            @block.vector
            def _(dve):
                for j in range(KT):
                    dve.wait_ge(s["gated"], j + 1)
                    g = gate[:, j % 2, :]
                    nc.vector.tensor_tensor(g, ps[:, 4 + j % 4, :], g, ALU.mult).then_inc(s["scaled"], 1)
                    dve.wait_ge(s["scaled"], j + 1)
                    nc.vector.tensor_tensor(x[:, j, :], x[:, j, :], g, ALU.add).then_inc(s["added"], 1)


def modulation(nc, M, w_ada, mod):
    ps = M.ps
    rounds, strips, slots = 3, 4, 4
    units = rounds * KT // 2
    quarter = lambda g: slice(32 * g, 32 * g + 1)
    with ExitStack() as stack:
        ring, c = buffer(nc, stack, "weight_ring", [P, slots, strips, 2, S]), buffer(nc, stack, "silu_c", [P, KT])
        rows = buffer(nc, stack, "rows", [P, rounds, S])
        with phase(nc, landed=slots, c_ready=0, used=0, row_ready=0, turned=0, dve=0) as (block, s):
            @block.sync
            def _(sp):
                for i in range(units):
                    if i >= slots:
                        sp.wait_ge(s["used"], i - slots + 1)
                    sp.dma_start(ring[:, i % slots], w_ada[i]).then_inc(s["landed"][i % slots], 16)

            @block.scalar
            def _(act):
                nc.scalar.activation(c[:, :], M.last("c"), ACT.Silu).then_inc(s["c_ready"], 1)

            @block.tensor
            def _(pe):
                pe.wait_ge(s["c_ready"], 1)
                for i in range(units):
                    r, kp = i // 4, i % 4
                    pe.wait_ge(s["landed"][i % slots], 16 * (i // slots) + 16)
                    for k2 in range(2):
                        k = 2 * kp + k2
                        for g in range(strips):
                            last = nc.tensor.matmul(ps[quarter(g), r, :], c[:, k:k + 1], ring[:, i % slots, g, k2, :],
                                                    start=(k == 0), stop=(k == KT - 1))
                    last.then_inc(s["used"], 1)
                pe.wait_ge(s["row_ready"], strips)
                for r in range(rounds):
                    for g in range(strips):
                        for i in range(4):
                            last = nc.tensor.matmul(ps[:, 4 + g, 4 * r + i:4 * r + i + 1],
                                                    rows[quarter(g), r, i * P:(i + 1) * P], M.c("ones")[quarter(g), 0:1],
                                                    start=True, stop=True)
                last.then_inc(s["turned"], 1)

            @block.vector
            def _(dve):
                dve.wait_ge(s["used"], units)
                for g in range(strips):
                    nc.vector.tensor_copy(rows[quarter(g)], ps[quarter(g), 0:rounds, :]).then_inc(s["row_ready"], 1)
                dve.wait_ge(s["turned"], 1)
                by_strip = lambda ap: ap.rearrange("p (r g i) -> p g r i", r=rounds, g=strips)
                nc.vector.tensor_tensor(by_strip(mod[:, :]), ps[:, 4:8, 0:4 * rounds].rearrange("p g (r i) -> p g r i", i=4),
                                        by_strip(M.last("b_ada")), ALU.add).then_inc(s["dve"], 1)


def head_norm(nc, M, z, groups, scratch, rstd):
    ps = M.ps
    n = groups[-1][1]
    with phase(nc, squared=0, summed=0, shifted=0, inverse=0, root=0, dve=0) as (block, s):
        @block.scalar
        def _(act):
            for j in range(n):
                if j >= 2:
                    act.wait_ge(s["summed"], j - 1)
                nc.scalar.activation(scratch[:, j % 2, :], z[:, j, :], ACT.Square).then_inc(s["squared"], 1)
            act.wait_ge(s["inverse"], 1)
            nc.scalar.activation(rstd[:, 0:n, :], rstd[:, 0:n, :], ACT.Sqrt).then_inc(s["root"], 1)

        @block.tensor
        def _(pe):
            for j in range(n):
                pe.wait_ge(s["squared"], j + 1)
                if j >= 4:
                    pe.wait_ge(s["shifted"], j - 3)
                nc.tensor.matmul(ps[:, j % 4, :], M.c("head_ones"), scratch[:, j % 2, :], start=True,
                                 stop=True).then_inc(s["summed"], 1)

        @block.vector
        def _(dve):
            own = Own(dve, s["dve"])
            for a, b, share, eps, _ in groups:
                for j in range(a, b):
                    dve.wait_ge(s["summed"], j + 1)
                    nc.vector.tensor_scalar(rstd[:, j, :], ps[:, j % 4, :], share, eps, ALU.mult,
                                            ALU.add).then_inc(s["shifted"], 1)
            dve.wait_ge(s["shifted"], n)
            nc.vector.reciprocal(rstd[:, 0:n, :], rstd[:, 0:n, :]).then_inc(s["inverse"], 1)
            dve.wait_ge(s["root"], 1)
            for a, b, _, _, gain in groups:
                own.mark(nc.vector.scalar_tensor_tensor(out=z[:, a:b, :], in0=z[:, a:b, :], scalar=gain,
                                                        in1=rstd[:, a:b, :], op0=ALU.mult, op1=ALU.mult))


def full_attention(nc, M, a, h, out, raw, make_h):
    with ExitStack() as stack:
        sb = lambda name, shape: buffer(nc, stack, name, shape)
        z, tok, tables = sb("attn_z", [P, 6, S]), sb("attn_tok", [P, TT, P]), sb("tables", [P, 2, S])
        maxima, sums = sb("maxima", [P, 32]), sb("sums", [P, 32])
        M.table = lambda n: tables[:, 0 if n == "cos_axial" else 1, :]
        with together(nc):
            landed = load(nc, (tables[:, :, :], a["tables"][:, 4:6, :]))
            ready = make_h()
            project(nc, M, lambda j: a["w_attn2"][j], 6, KT, h, 3,
                    lambda act, j, made: nc.scalar.activation(z[:, j, :], made, ACT.Copy), ready)
            token_major(nc, M, a["w_v2"], P, h, tok, ((0, P, in_order),), ready)
            with phase(nc, cleared=0) as (block, s):
                @block.vector
                def _(dve):
                    dve.wait_ge(*landed)
                    nc.vector.memset(raw[:, :, 0:2], 0.0).then_inc(s["cleared"], 1)
                    nc.vector.memset(raw[:, :, S + 2:S + 4], 0.0).then_inc(s["cleared"], 1)
        with ExitStack() as inner:
            scratch, rstd = buffer(nc, inner, "scratch", [P, 2, S]), buffer(nc, inner, "rstd", [P, 6, S])
            head_norm(nc, M, z, ((0, 4, 1.0 / HD, NORM_EPS, M.last("q_norm")), (4, 6, 1.0 / HD, NORM_EPS, M.last("k_norm"))),
                      scratch, rstd)
        rope(nc, M, z, [(t, "axial") for t in range(6)])
        jobs = []
        for hd in range(8):
            rows, kv = HD * (hd % 2), hd // 4
            for b in range(TT):
                here = slice(b * P, (b + 1) * P)
                jobs.append(Job(q=z[rows:rows + HD, hd // 2, here], k=z[rows:rows + HD, 4 + kv, :], keys=S,
                                            bias=None, v=[tok[:, t, HD * kv:HD * kv + HD] for t in range(TT)],
                                            out=out[rows:rows + HD, hd // 2, here], gate=None, rows=rows))
        mixed = lambda j: (a["w_conv2"][j], lambda act, made: nc.scalar.activation(raw[:, j, 2:S + 2], made, ACT.Copy))
        side = SideProjection(nc, M, [mixed(j) for j in range(12)], KT, h, sb("side_ring", [P, 4, KT, P]), 4, (6, 7))
        attention(nc, M, jobs, maxima, sums, side)


def delta_net(nc, M, a, h, out, shared, raw, gated):
    ps = M.ps
    JP = 4
    NB = 2 * JP
    halves = (slice(0, HD), slice(HD, P))
    with ExitStack() as outer:
        sb = lambda name, shape: buffer(nc, outer, name, shape)
        big = [P, NCH, 2, JP, CH]
        key = sb("key", [P, JP, S])
        beta, decay_in, decay_out, decay_end = (sb(x, [P, NCH, 2, JP]) for x in ("beta", "decay_in", "decay_out", "decay_end"))
        q_dec, bv, kd = (sb(x, big) for x in ("q_dec", "bv", "kd"))
        low, at = (shared[:, i].rearrange("p (n d j t) -> p n d j t", n=NCH, d=2, j=JP) for i in range(2))
        chunk = lambda ap, c: ap[:, :, c * CH:(c + 1) * CH]
        with ExitStack() as stack:
            sbt = lambda name, shape: buffer(nc, stack, name, shape)
            qv = sbt("query_value", [P, 2 * JP, S])
            query, value = qv[:, 0:JP, :], qv[:, JP:2 * JP, :]
            dest = lambda j: (qv[:, j, :] if j < 4 else key[:, j - 4, :] if j < 8 else qv[:, j - 4, :])
            conv = M.last("conv").rearrange("p (j i) -> p j i", i=5)
            with phase(nc, first=0, summed=0, dve=0, gated=0) as (block, s):
                @block.scalar
                def _(act):
                    for j in range(12):
                        nc.scalar.activation(dest(j), raw[:, j, 0:S], ACT.Copy, scale=conv[:, j, 0:1]).then_inc(s["first"], 1)
                    for j in range(12):
                        act.wait_ge(s["summed"], j + 1)
                        nc.scalar.activation(dest(j), dest(j), ACT.Silu).then_inc(s["gated"], 1)

                @block.vector
                def _(dve):
                    own = Own(dve, s["dve"])
                    for j in range(12):
                        dve.wait_ge(s["first"], j + 1)
                        for i in range(1, 5):
                            ins = nc.vector.scalar_tensor_tensor(out=dest(j), in0=raw[:, j, i:i + S], scalar=conv[:, j, i:i + 1],
                                                                 in1=dest(j), op0=ALU.mult, op1=ALU.add)
                            if i < 4:
                                own.step(ins)
                            else:
                                ins.then_inc(s["summed"], 1)
            with ExitStack() as inner:
                scratch, rstd = buffer(nc, inner, "scratch", [P, 2, S]), buffer(nc, inner, "rstd", [P, JP, S])
                head_norm(nc, M, query, ((0, JP, 1.0, 1e-6, HD ** -0.5),), scratch, rstd)
                head_norm(nc, M, key, ((0, JP, 1.0, 1e-6, 1.0),), scratch, rstd)

            w_ba, raw_ba = sbt("w_ba", [P, KT, 32]), sbt("raw_ba", [P, 2, NCH, 2, JP])
            mag, cum, total = sbt("mag", [P, NCH, 2, JP]), sbt("cum", [P, NCH, 2, JP]), sbt("total", [P, NCH, 2, JP])
            gate, coef = sbt("gate", [P, NCH, 2, JP]), sbt("coef", [P, 2 * JP])
            with phase(nc, landed=0, made=0, copied=0, exps=0, act_in=0, g_ready=0, summed=0, cum_ready=0, dve=0) as (block, s):
                @block.sync
                def _(sp):
                    sp.dma_start(w_ba[:, :, :], a["w_ba2"]).then_inc(s["landed"], 16)

                @block.tensor
                def _(pe):
                    pe.wait_ge(s["landed"], 16)
                    for c in range(NCH):
                        for hp, w in enumerate(halves):
                            for k in range(KT):
                                last = nc.tensor.matmul(ps[w, 0, 16 * c:16 * c + 16], h[:, k, c * CH:(c + 1) * CH],
                                                        w_ba[:, k, 16 * hp:16 * hp + 16], start=(k == 0), stop=(k == KT - 1))
                    last.then_inc(s["made"], 1)
                    pe.wait_ge(s["g_ready"], 1)
                    for d, m in enumerate(("sum_until", "sum_from")):
                        for n in range(NCH):
                            nc.tensor.matmul(ps[:, 1, (2 * n + d) * JP:(2 * n + d + 1) * JP], M.c(m), gate[:, n, d, :], start=True, stop=True)
                    nc.tensor.matmul(ps[:, 2, 0:2 * NCH * JP], M.c("head_ones"), gate[:, :, :, :].rearrange("p n d j -> p (n d j)"),
                                     start=True, stop=True).then_inc(s["summed"], 1)

                @block.scalar
                def _(act):
                    act.wait_ge(s["copied"], 4)
                    nc.scalar.activation(beta[:, :, :, :], raw_ba[:, 0], ACT.Sigmoid).then_inc(s["exps"], 1)
                    nc.scalar.activation(coef[:, :], M.last("a_log"), ACT.Exp).then_inc(s["exps"], 1)
                    act.wait_ge(s["act_in"], 1)
                    nc.scalar.activation(mag[:, :, :, :], mag[:, :, :, :], ACT.Exp, scale=-1.0).then_inc(s["exps"], 1)
                    act.wait_ge(s["act_in"], 2)
                    nc.scalar.activation(mag[:, :, :, :], mag[:, :, :, :], ACT.Ln).then_inc(s["exps"], 1)
                    act.wait_ge(s["cum_ready"], 1)
                    nc.scalar.activation(decay_in[:, :, :, :], cum[:, :, :, :], ACT.Exp).then_inc(s["exps"], 1)
                    nc.scalar.activation(decay_out[:, :, :, :], mag[:, :, :, :], ACT.Exp).then_inc(s["exps"], 1)
                    nc.scalar.activation(decay_end[:, :, :, :], total[:, :, :, :], ACT.Exp).then_inc(s["exps"], 1)

                @block.vector
                def _(dve):
                    own = Own(dve, s["dve"])
                    V = nc.vector
                    dve.wait_ge(s["made"], 1)
                    made = ps[:, 0, 0:16 * NCH].rearrange("p (c k d j) -> p c k d j", c=NCH, k=2, d=2)
                    for kind in range(2):
                        V.tensor_copy(raw_ba[:, kind, :, 0, :], made[:, :, kind, 0, :]).then_inc(s["copied"], 1)
                        V.tensor_copy(raw_ba[:, kind, :, 1, :], made[:, ::-1, kind, 1, :]).then_inc(s["copied"], 1)
                    dve.wait_ge(s["copied"], 4)
                    av = raw_ba[:, 1].rearrange("p n d j -> p n (d j)")
                    bias = M.last("dt_bias").unsqueeze(1).broadcast_to([P, NCH, 2 * JP])
                    own.step(V.tensor_tensor(av, av, bias, ALU.add))
                    own.step(V.tensor_scalar(mag[:, :, :, :], raw_ba[:, 1], -1.0, None, ALU.mult))
                    V.tensor_tensor(mag[:, :, :, :], mag[:, :, :, :], raw_ba[:, 1], ALU.max).then_inc(s["act_in"], 1)
                    dve.wait_ge(s["exps"], 3)
                    V.tensor_scalar(mag[:, :, :, :], mag[:, :, :, :], 1.0, None, ALU.add).then_inc(s["act_in"], 1)
                    own.step(V.tensor_scalar(raw_ba[:, 1], raw_ba[:, 1], 0.0, None, ALU.max))
                    dve.wait_ge(s["exps"], 4)
                    own.step(V.tensor_tensor(raw_ba[:, 1], raw_ba[:, 1], mag[:, :, :, :], ALU.add))
                    own.step(V.tensor_scalar(coef[:, :], coef[:, :], -1.0, None, ALU.mult))
                    V.tensor_tensor(gate[:, :, :, :].rearrange("p n d j -> p n (d j)"), av,
                                    coef[:, :].unsqueeze(1).broadcast_to([P, NCH, 2 * JP]), ALU.mult).then_inc(s["g_ready"], 1)
                    dve.wait_ge(s["summed"], 1)
                    flat = lambda t: t[:, :, :, :].rearrange("p n d j -> p (n d j)")
                    own.mark(V.tensor_copy(flat(cum), ps[:, 1, 0:2 * NCH * JP]))
                    own.step(V.tensor_copy(flat(total), ps[:, 2, 0:2 * NCH * JP]))
                    V.tensor_tensor(mag[:, :, :, :], total[:, :, :, :], cum[:, :, :, :], ALU.subtract).then_inc(s["cum_ready"], 1)
                    dve.wait_ge(s["exps"], 7)
                    own.step(V.scalar_tensor_tensor(out=decay_in[:, :, :, :], in0=decay_in[:, :, :, :], scalar=-1.0,
                                                    in1=beta[:, :, :, :], op0=ALU.mult, op1=ALU.mult))

            rhs, dif = sbt("spread_rhs", [P, 2, NB, CH]), sbt("difference", [P, 2, NB, CH])
            per = lambda t, n: t[:, n].rearrange("p d j -> p (d j)")
            block_of = lambda t, n: t[:, n].rearrange("p d j t -> p (d j) t")
            bank8 = lambda i: ps[:, i, :].rearrange("p (b t) -> p b t", b=NB)
            with phase(nc, rhs_ready=0, spread=0, q_exp=0, capped=0, exp_done=0, masked=0, dve=0) as (block, s):
                @block.tensor
                def _(pe):
                    for n in range(NCH):
                        pe.wait_ge(s["rhs_ready"], n + 1)
                        if n >= 2:
                            pe.wait_ge(s["q_exp"], n - 1)
                            pe.wait_ge(s["capped"], 2 * n - 2)
                        nc.tensor.matmul(ps[:, n % 2, :], M.c("head_ones"), rhs[:, n % 2].rearrange("p b t -> p (b t)"),
                                         start=True, stop=True).then_inc(s["spread"], 1)

                @block.scalar
                def _(act):
                    for n in range(NCH):
                        act.wait_ge(s["spread"], n + 1)
                        nc.scalar.activation(block_of(q_dec, n), bank8(n % 2), ACT.Exp).then_inc(s["q_exp"], 1)
                        act.wait_ge(s["capped"], 2 * n + 2)
                        nc.scalar.activation(block_of(at, n), block_of(at, n), ACT.Exp).then_inc(s["exp_done"], 1)
                        nc.scalar.activation(block_of(low, n), block_of(low, n), ACT.Exp, scale=-1.0).then_inc(s["exp_done"], 1)

                @block.gpsimd
                def _(pool):
                    for n in range(NCH):
                        pool.wait_ge(s["exp_done"], 2 * n + 2)
                        for target, name in ((at, "incl_T"), (low, "strict")):
                            m = M.c(name).rearrange("p (d t) -> p d t", d=2).unsqueeze(2).broadcast_to([P, 2, JP, CH])
                            nc.gpsimd.tensor_tensor(target[:, n], target[:, n], m, ALU.mult).then_inc(s["masked"], 1)
                    pool.wait_ge(s["masked"], 2 * NCH)

                @block.vector
                def _(dve):
                    own = Own(dve, s["dve"])
                    for n in range(NCH):
                        c = per(cum, n).unsqueeze(2).broadcast_to([P, NB, CH])
                        if n >= 2:
                            dve.wait_ge(s["spread"], n - 1)
                        nc.vector.tensor_tensor(rhs[:, n % 2], M.c("ident2").unsqueeze(1).broadcast_to([P, NB, CH]), c,
                                                ALU.mult).then_inc(s["rhs_ready"], 1)
                        dve.wait_ge(s["q_exp"], n + 1)
                        own.step(nc.vector.tensor_tensor(dif[:, n % 2], bank8(n % 2), c, ALU.subtract))
                        nc.vector.tensor_scalar(block_of(at, n), dif[:, n % 2], 0.0, None, ALU.min).then_inc(s["capped"], 1)
                        nc.vector.tensor_scalar(block_of(low, n), dif[:, n % 2], 0.0, None, ALU.max).then_inc(s["capped"], 1)

            with phase(nc, made=0, taken=0, q_scaled=0, dve=0) as (block, s):
                bank4 = lambda i: ps[:, i, 0:JP * CH].rearrange("p (j t) -> p j t", j=JP)

                @block.tensor
                def _(pe):
                    for c in range(NCH):
                        if c >= 2:
                            pe.wait_ge(s["taken"], c - 1)
                        here = slice(c * CH, (c + 1) * CH)
                        for j in range(JP):
                            for w in halves:
                                kc, qc, vc = key[w, j, here], query[w, j, here], value[w, j, here]
                                for i, (lhs, rh) in enumerate(((kc, kc), (kc, qc), (kc, M.c("ident2")[w, :]), (vc, M.c("ident2")[w, :]))):
                                    last = nc.tensor.matmul(bank4(4 * (c % 2) + i)[w, j, :], lhs, rh, start=True, stop=True)
                        last.then_inc(s["made"], 1)

                @block.gpsimd
                def _(pool):
                    for n in range(NCH):
                        for d, c in ((0, n), (1, NCH - 1 - n)):
                            nc.gpsimd.tensor_tensor(q_dec[:, n, d], q_dec[:, n, d], chunk(query, c), ALU.mult).then_inc(s["q_scaled"], 1)
                    pool.wait_ge(s["q_scaled"], 2 * NCH)

                @block.vector
                def _(dve):
                    own = Own(dve, s["dve"])
                    for c in range(NCH):
                        dve.wait_ge(s["made"], c + 1)
                        b = 4 * (c % 2)
                        for d, n in ((0, c), (1, NCH - 1 - c)):
                            wide = lambda t: t[:, n, d, :].unsqueeze(2).broadcast_to([P, JP, CH])
                            own.mark(nc.vector.tensor_tensor(low[:, n, d], bank4(b), low[:, n, d], ALU.mult))
                            own.mark(nc.vector.tensor_tensor(at[:, n, d], bank4(b + 1), at[:, n, d], ALU.mult))
                            own.mark(nc.vector.tensor_tensor(kd[:, n, d], bank4(b + 2), wide(decay_out), ALU.mult))
                            own.step(nc.vector.tensor_tensor(bv[:, n, d], bank4(b + 3), wide(beta), ALU.mult))
                            own.step(nc.vector.tensor_tensor(low[:, n, d], low[:, n, d], wide(beta), ALU.mult))
                        dve.sem_inc(s["taken"], 1)

        with ExitStack() as stack:
            sbt = lambda name, shape: buffer(nc, stack, name, shape)
            inv, inv_t = sbt("inv", big), sbt("inv_t", big)
            flat = lambda t: t[:, :, :, :, :].rearrange("p n d j t -> p n (d j) t")
            invert(nc, M, flat(low), flat(inv), flat(inv_t), NCH, NB, 1, 2)

            state, kept = inv[:, 0:2], inv[:, 2:4]
            xs, fresh = inv[:, 4:6], inv[:, 6:8]
            silu = lambda j: (a["w_z2"][j], lambda act, made: nc.scalar.activation(gated[:, j, :], made, ACT.Silu))
            side = SideProjection(nc, M, [silu(j) for j in range(JP)], KT, h, sbt("side_ring", [P, 2, KT, P]), 2, (5, 6, 7))
            with phase(nc, x_made=0, scaled=0, x_ready=0, v_made=0, v_ready=0, state_made=0, kept_ready=0, state_ready=0,
                       o_made=0, o_ready=0, dve=0, **SideProjection.SEMAPHORES) as (block, s):
                side.attach(s)

                @block.sync
                def _(sp):
                    side.load(sp)

                bank = lambda i: ps[:, i, :].rearrange("p (d j t) -> p d j t", d=2, j=JP)

                @block.tensor
                def _(pe):
                    mm = nc.tensor.matmul
                    every = [(d, j, w) for d in range(2) for j in range(JP) for w in halves]
                    for n in range(NCH):
                        old, k2 = state[:, n % 2], n % 2
                        here = lambda d: slice((n if d == 0 else NCH - 1 - n) * CH, (n if d == 0 else NCH - 1 - n) * CH + CH)
                        pe.wait_ge(s["state_ready"], n + 1)
                        for d, j, w in every:
                            last = mm(bank(0)[w, d, j, :], key[w, j, here(d)], old[w, d, j, :], start=True, stop=True)
                        last.then_inc(s["x_made"], 1)
                        side.multiply(pe, JP * n + 2)
                        pe.wait_ge(s["x_ready"], n + 1)
                        for d, j, w in every:
                            last = mm(bank(1)[w, d, j, :], inv_t[w, n, d, j, :], xs[w, k2, d, j, :], start=True, stop=True)
                        last.then_inc(s["v_made"], 1)
                        side.multiply(pe, JP * n + 4)
                        pe.wait_ge(s["v_ready"], n + 1)
                        for d, j, w in every:
                            last = mm(bank(2)[w, d, j, :], kd[w, n, d, j, :], fresh[w, k2, d, j, :], start=True, stop=True)
                        last.then_inc(s["state_made"], 1)
                        if n >= 2:
                            pe.wait_ge(s["o_ready"], 2 * n - 2)
                        for d, j, w in every:
                            mm(bank(3 + k2)[w, d, j, :], old[w, d, j, :], q_dec[w, n, d, j, :], start=True, stop=False)
                            last = mm(bank(3 + k2)[w, d, j, :], fresh[w, k2, d, j, :], at[w, n, d, j, :], start=False, stop=True)
                        last.then_inc(s["o_made"], 1)

                @block.scalar
                def _(act):
                    for n in range(NCH):
                        act.wait_ge(s["v_made"], n + 1)
                        if n >= 2:
                            act.wait_ge(s["o_made"], n - 1)
                        nc.scalar.activation(fresh[:, n % 2], bank(1), ACT.Copy).then_inc(s["v_ready"], 1)
                        side.take(act, n // 2)
                    side.take(act, JP)

                @block.vector
                def _(dve):
                    own = Own(dve, s["dve"])
                    V = nc.vector
                    V.memset(state[:, 0], 0.0).then_inc(s["state_ready"], 1)
                    for n in range(NCH):
                        k2 = n % 2
                        wide = lambda t: t[:, n].unsqueeze(3).broadcast_to([P, 2, JP, CH])
                        dve.wait_ge(s["x_made"], n + 1)
                        own.step(V.tensor_tensor(xs[:, k2], bank(0), wide(decay_in), ALU.mult))
                        V.tensor_tensor(xs[:, k2], xs[:, k2], bv[:, n], ALU.add).then_inc(s["x_ready"], 1)
                        if n < NCH - 1:
                            dve.wait_ge(s["state_ready"], n + 1)
                            own.step(V.tensor_tensor(kept[:, k2], state[:, k2], wide(decay_end), ALU.mult))
                            dve.wait_ge(s["state_made"], n + 1)
                            if n >= 1:
                                dve.wait_ge(s["o_made"], n)
                            V.tensor_tensor(state[:, 1 - k2], bank(2), kept[:, k2], ALU.add).then_inc(s["state_ready"], 1)
                        dve.wait_ge(s["o_made"], n + 1)
                        for d, c in ((0, n), (1, NCH - 1 - n)):
                            o = chunk(out, c)
                            if n < NCH // 2:
                                ins = V.tensor_copy(o, bank(3 + k2)[:, d])
                            else:
                                dve.wait_ge(s["o_ready"], 2 * (NCH // 2))
                                ins = V.tensor_tensor(o, bank(3 + k2)[:, d], o, ALU.add)
                            ins.then_inc(s["o_ready"], 1)

    with ExitStack() as stack:
        sbt = lambda name, shape: buffer(nc, stack, name, shape)
        scratch, rstd = sbt("scratch", [P, 2, S]), sbt("rstd", [P, JP, S])
        head_norm(nc, M, out, ((0, JP, 1.0 / HD, NORM_EPS, M.last("dn_norm")),), scratch, rstd)
        with phase(nc, dve=0) as (block, s):
            @block.vector
            def _(dve):
                Own(dve, s["dve"]).step(nc.vector.tensor_tensor(out, out, gated[:, :, :], ALU.mult))


def merge(nc, M, w_merge, h, attn, delta, merged):
    ps = M.ps
    with ExitStack() as stack:
        ring, gates = buffer(nc, stack, "weight_ring", [P, 2, 24, P]), buffer(nc, stack, "gates", [P, 2, 2, S])
        with phase(nc, landed=2, tile_done=0, gated=0, taken=0, dve=0) as (block, s):
            parts = [(0, k, h[:, k, :]) for k in range(8)] + [(1, 8 + k, h[:, k, :]) for k in range(8)] + [
                (2, 16 + k, attn[:, k, :]) for k in range(4)] + [(3, 20 + k, delta[:, k, :]) for k in range(4)]

            @block.sync
            def _(sp):
                for m in range(KT):
                    if m >= 2:
                        sp.wait_ge(s["tile_done"], m - 1)
                    sp.dma_start(ring[:, m % 2], w_merge[m]).then_inc(s["landed"][m % 2], 16)

            @block.tensor
            def _(pe):
                for m in range(KT):
                    pe.wait_ge(s["landed"][m % 2], 16 * (m // 2) + 16)
                    if m >= 2:
                        pe.wait_ge(s["taken"], m - 1)
                    for i, (bank, k, src) in enumerate(parts):
                        last = nc.tensor.matmul(ps[:, 4 * (m % 2) + bank, :], ring[:, m % 2, k, :], src,
                                                start=(i == 0 or parts[i - 1][0] != bank),
                                                stop=(i == 23 or parts[i + 1][0] != bank))
                    last.then_inc(s["tile_done"], 1)

            @block.scalar
            def _(act):
                for m in range(KT):
                    act.wait_ge(s["tile_done"], m + 1)
                    if m >= 2:
                        act.wait_ge(s["taken"], m - 1)
                    nc.scalar.activation(gates[:, m % 2], ps[:, 4 * (m % 2):4 * (m % 2) + 2, :], ACT.Sigmoid).then_inc(s["gated"], 1)

            @block.vector
            def _(dve):
                own = Own(dve, s["dve"])
                for m in range(KT):
                    g = gates[:, m % 2]
                    dve.wait_ge(s["gated"], m + 1)
                    own.step(nc.vector.tensor_tensor(g, ps[:, 4 * (m % 2) + 2:4 * (m % 2) + 4, :], g, ALU.mult))
                    nc.vector.tensor_tensor(merged[:, m, :], g[:, 0, :], g[:, 1, :], ALU.add).then_inc(s["taken"], 1)
    return s["taken"], KT


def route(nc, M, w_router, h, tokens, aff, chosen):
    ps = M.ps
    E, CAP = 16, 64
    with ExitStack() as stack:
        sb = lambda name, shape: buffer(nc, stack, name, shape)
        w, stat = sb("w_router", [P, KT, E]), sb("stat", [P, TT])
        rank, taken, best = sb("rank", [E, S]), sb("taken", [E, S]), sb("best", [E, 8])
        ones_row, slot = sb("ones_row", [E, S]), sb("slot", [P, TT, E])
        with phase(nc, landed=0, logits=0, centred=0, exp_done=0, aff_ready=0, turned=0, slot_ready=0, slots_made=0,
                   h_turned=0, h_copied=0, dve=0) as (block, s):
            @block.sync
            def _(sp):
                sp.dma_start(w[:, :, :], w_router).then_inc(s["landed"], 16)

            @block.tensor
            def _(pe):
                pe.wait_ge(s["landed"], 16)
                for t in range(TT):
                    for k in range(KT):
                        last = nc.tensor.matmul(ps[:, 0, E * t:E * t + E], h[:, k, t * P:(t + 1) * P], w[:, k, :],
                                                start=(k == 0), stop=(k == KT - 1))
                last.then_inc(s["logits"], 1)
                for i in range(2 * TT):
                    t, half = i // 2, i % 2
                    if i >= 4:
                        pe.wait_ge(s["h_copied"], i - 3)
                    for k in range(4):
                        last = nc.tensor.transpose(ps[:, 4 + i % 4, k * P:(k + 1) * P], h[:, 4 * half + k, t * P:(t + 1) * P], M.c("ident"))
                    last.then_inc(s["h_turned"], 1)
                pe.wait_ge(s["aff_ready"], 1)
                for t in range(TT):
                    last = nc.tensor.transpose(ps[0:E, 1, t * P:(t + 1) * P], aff[:, t, :], M.c("ident"))
                last.then_inc(s["turned"], 1)
                pe.wait_ge(s["slot_ready"], 1)
                for t in range(TT):
                    last = nc.tensor.transpose(ps[:, 2, t * E:(t + 1) * E], rank[:, t * P:(t + 1) * P], M.c("ident")[0:E, 0:E])
                last.then_inc(s["slots_made"], 1)

            @block.scalar
            def _(act):
                act.wait_ge(s["centred"], 1)
                nc.scalar.activation(aff[:, :, :], aff[:, :, :], ACT.Exp).then_inc(s["exp_done"], 1)
                for i in range(2 * TT):
                    act.wait_ge(s["h_turned"], i + 1)
                    nc.scalar.activation(tokens[:, i // 2, 512 * (i % 2):512 * (i % 2) + 512], ps[:, 4 + i % 4, :], ACT.Copy).then_inc(s["h_copied"], 1)

            @block.vector
            def _(dve):
                own = Own(dve, s["dve"])
                V = nc.vector
                own.mark(V.memset(ones_row[:, :], 1.0))
                dve.wait_ge(s["logits"], 1)
                logits = ps[:, 0, 0:E * TT].rearrange("p (t e) -> p t e", t=TT)
                own.step(V.reduce_max(stat[:, :], logits, AX.X))
                V.tensor_tensor(aff[:, :, :], logits, stat[:, :].unsqueeze(2).broadcast_to([P, TT, E]), ALU.subtract).then_inc(s["centred"], 1)
                dve.wait_ge(s["exp_done"], 1)
                own.step(V.reduce_sum(stat[:, :], aff[:, :, :], AX.X))
                own.step(V.reciprocal(stat[:, :], stat[:, :]))
                V.tensor_tensor(aff[:, :, :], aff[:, :, :], stat[:, :].unsqueeze(2).broadcast_to([P, TT, E]), ALU.mult).then_inc(s["aff_ready"], 1)
                dve.wait_ge(s["turned"], 1)
                own.step(V.tensor_copy(rank[:, :], ps[0:E, 1, :]))
                for _ in range(CAP // 8):
                    own.step(V.max(best[:, :], rank[:, :]))
                    own.step(V.match_replace(out=rank[:, :], in_to_replace=best[:, :], in_values=rank[:, :], imm_value=-1.0))
                own.step(V.tensor_scalar(taken[:, :], rank[:, :], 0.0, None, ALU.is_lt))
                own.step(V.tensor_tensor_scan(rank[:, :], ones_row[:, :], taken[:, :], 0.0, ALU.mult, ALU.add))
                own.step(V.tensor_tensor(rank[:, :], rank[:, :], taken[:, :], ALU.mult))
                V.tensor_scalar(rank[:, :], rank[:, :], -1.0, None, ALU.add).then_inc(s["slot_ready"], 1)
                dve.wait_ge(s["slots_made"], 1)
                own.step(V.tensor_copy(slot[:, :, :].rearrange("p t e -> p (t e)"), ps[:, 2, 0:TT * E]))
                for t in range(TT):
                    wide = lambda ap: ap[:, t, :].unsqueeze(2).broadcast_to([P, E, CAP])
                    own.step(V.tensor_tensor(chosen[:, t], M.c("slots").unsqueeze(1).broadcast_to([P, E, CAP]), wide(slot), ALU.is_equal))


def gather(nc, M, tokens, chosen, inputs):
    ps = M.ps
    with phase(nc, made=0, copied=0) as (block, s):
        @block.tensor
        def _(pe):
            for i in range(16):
                k, half = i // 2, i % 2
                if i >= 4:
                    pe.wait_ge(s["copied"], i - 3)
                for t in range(TT):
                    last = nc.tensor.matmul(ps[:, i % 4, :], tokens[:, t, k * P:(k + 1) * P],
                                            chosen[:, t, 8 * half:8 * half + 8, :].rearrange("p e c -> p (e c)"),
                                            start=(t == 0), stop=(t == TT - 1))
                last.then_inc(s["made"], 1)

        @block.scalar
        def _(act):
            for i in range(16):
                act.wait_ge(s["made"], i + 1)
                nc.scalar.activation(inputs[:, i // 2, 8 * (i % 2):8 * (i % 2) + 8, :].rearrange("p e c -> p (e c)"),
                                     ps[:, i % 4, :], ACT.Copy).then_inc(s["copied"], 1)


def turn_weights(nc, M, chosen, aff, back):
    ps = M.ps
    with phase(nc, cleared=0, weighted=0, turned=0, copied=0) as (block, s):
        @block.vector
        def _(dve):
            nc.vector.memset(back[:, 0, :], 0.0).then_inc(s["cleared"], 1)
            for t in range(TT):
                nc.vector.tensor_tensor(chosen[:, t], chosen[:, t], aff[:, t, :].unsqueeze(2).broadcast_to([P, 16, 64]),
                                        ALU.mult).then_inc(s["weighted"], 1)
            for i in range(8):
                dve.wait_ge(s["turned"], i + 1)
                nc.vector.tensor_copy(back[:, i + 1, :], ps[:, i % 4, :]).then_inc(s["copied"], 1)

        @block.tensor
        def _(pe):
            pe.wait_ge(s["weighted"], TT)
            for i in range(8):
                if i >= 4:
                    pe.wait_ge(s["copied"], i - 3)
                for t in range(TT):
                    last = nc.tensor.transpose(ps[:, i % 4, t * P:(t + 1) * P],
                                               chosen[:, t, 2 * i:2 * i + 2, :].rearrange("p e c -> p (e c)"), M.c("ident"))
                last.then_inc(s["turned"], 1)


PAIRS, UNITS, SLOTS = 8, 24, 8


def first_experts(nc, ring, w_expert, landed):
    with phase(nc) as (block, s):
        @block.sync
        def _(sp):
            for i in range(SLOTS):
                sp.dma_start(ring[:, i], w_expert[0, i]).then_inc(landed[i], 16)


def experts(nc, M, w_expert, inputs, made, back, gain, x, ring, landed):
    ps = M.ps
    one, two = slice(0, HD), slice(HD, P)
    with ExitStack() as stack:
        sb = lambda name, shape: buffer(nc, stack, name, shape)
        xe, act_in, act_t = sb("xe", [P, 2, KT, 64]), sb("act_in", [P, 2, D]), sb("act_t", [P, 2, KT, 64])
        turned_in = lambda a, b: ps[:, 4:6, :].rearrange("p b (f c) -> p (b f) c", f=4)[:, :, a:b]
        with phase(nc, used=SLOTS, x_ready=0, in_copied=0, turned=0, silu_done=0, act_ready=0, out_ready=0,
                   summed=0, added=0) as (block, s):
            used = s["used"]

            @block.sync
            def _(sp):
                with sp.Fori(0, PAIRS - 1) as r:
                    for i in range(UNITS):
                        j = i + SLOTS
                        sp.wait_ge(used[i % SLOTS], r * 3 + i // SLOTS + 1)
                        sp.dma_start(ring[:, i % SLOTS], w_expert[r + j // UNITS, j % UNITS]).then_inc(landed[i % SLOTS], 16)
                for i in range(UNITS - SLOTS):
                    sp.wait_ge(used[i % SLOTS], (PAIRS - 1) * 3 + i // SLOTS + 1)
                    sp.dma_start(ring[:, i % SLOTS], w_expert[PAIRS - 1, i + SLOTS]).then_inc(landed[i % SLOTS], 16)

            @block.gpsimd
            def _(pool):
                with pool.Fori(0, PAIRS) as r:
                    for ep in range(2):
                        pool.wait_ge(s["in_copied"], r * 2 + ep + 1)
                        nc.gpsimd.tensor_copy(xe[:, ep], inputs[:, :, bass.ds(r * 2 + ep, 1), :].rearrange(
                            "p k o c -> p k (o c)")).then_inc(s["x_ready"], 1)

            @block.tensor
            def _(pe):
                with pe.Fori(0, PAIRS) as r:
                    def arrived(unit):
                        pe.wait_ge(landed[unit % SLOTS], r * 48 + 16 * (unit // SLOTS) + 16)

                    for ep in range(2):
                        if ep == 1:
                            pe.wait_ge(s["out_ready"], r + 1)
                            for m in range(KT):
                                pe.wait_ge(s["added"], r * 8 + m + 1)
                                nc.tensor.matmul(ps[:, 4 + m % 2, :], made[:, m * P:(m + 1) * P],
                                                 back[:, bass.ds(r, 1), :].rearrange("p o n -> p (o n)"),
                                                 start=True, stop=True).then_inc(s["summed"], 1)
                        pe.wait_ge(s["x_ready"], r * 2 + ep + 1)
                        for kp in range(4):
                            gate, up = 8 * ep + 2 * kp, 8 * ep + 2 * kp + 1
                            arrived(gate)
                            arrived(up)
                            for k2 in range(2):
                                k = 2 * kp + k2
                                for half in range(2):
                                    for unit, w in ((gate, one), (up, two)):
                                        last = nc.tensor.matmul(ps[w, 2 * ep + half, :], xe[:, ep, k, :],
                                                                ring[:, unit % SLOTS, k2, S * half:S * half + S],
                                                                start=(k == 0), stop=(k == KT - 1))
                                        if k2 == 1 and half == 1:
                                            last.then_inc(used[unit % SLOTS], 1)
                    pe.wait_ge(s["added"], r * 8 + 10)
                    for ep in range(2):
                        pe.wait_ge(s["in_copied"], r * 2 + ep + 3)
                        pe.wait_ge(s["act_ready"], r * 2 + ep + 1)
                        for f in range(KT):
                            last = nc.tensor.transpose(ps[:, 4 + f // 4, (f % 4) * P:(f % 4 + 1) * P],
                                                       act_in[:, ep, f * P:(f + 1) * P], M.c("ident"))
                        last.then_inc(s["turned"], 1)
                    pe.wait_ge(s["act_ready"], r * 2 + 3)
                    pe.wait_ge(s["out_ready"], r + 1)
                    for fp in range(4):
                        units = (16 + 2 * fp, 17 + 2 * fp)
                        for unit in units:
                            arrived(unit)
                        for f2 in range(2):
                            f = 2 * fp + f2
                            for half in range(2):
                                for ep, w in ((0, one), (1, two)):
                                    last = nc.tensor.matmul(ps[w, 6 + half, :], act_t[:, ep, f, :],
                                                            ring[:, units[ep] % SLOTS, f2, S * half:S * half + S],
                                                            start=(f == 0), stop=(f == KT - 1))
                                    if f2 == 1 and half == 1:
                                        last.then_inc(used[units[ep] % SLOTS], 1)
                pe.wait_ge(s["out_ready"], PAIRS + 1)
                for m in range(KT):
                    if m >= 4:
                        pe.wait_ge(s["added"], PAIRS * 8 + m - 1)
                    nc.tensor.matmul(ps[:, m % 4, :], made[:, m * P:(m + 1) * P], back[:, PAIRS, :],
                                     start=True, stop=True).then_inc(s["summed"], 1)

            @block.scalar
            def _(act):
                act.sem_inc(s["in_copied"], 2)
                with act.Fori(0, PAIRS) as r:
                    for ep in range(2):
                        act.wait_ge(used[7], r * 3 + ep + 1)
                        nc.scalar.activation(act_in[:, ep, :], ps[:, 2 * ep:2 * ep + 2, :].rearrange("p b n -> p (b n)"),
                                             ACT.Copy).then_inc(s["in_copied"], 1)
                    act.wait_ge(s["out_ready"], r + 1)
                    for ep in range(2):
                        act.wait_ge(s["turned"], r * 2 + ep + 1)
                        nc.scalar.activation(act_t[:, ep], turned_in(0, 64), ACT.Silu).then_inc(s["silu_done"], 1)

            @block.vector
            def _(dve):
                def add(m, bank):
                    nc.vector.scalar_tensor_tensor(out=x[:, m, :], in0=ps[:, bank, :], scalar=gain(m), in1=x[:, m, :],
                                                   op0=ALU.mult, op1=ALU.add).then_inc(s["added"], 1)

                dve.sem_inc(s["act_ready"], 1)
                dve.sem_inc(s["added"], 2)
                nc.vector.memset(made, 0.0).then_inc(s["out_ready"], 1)
                with dve.Fori(0, PAIRS) as r:
                    dve.wait_ge(s["added"], r * 8 + 2)
                    for m in range(KT):
                        dve.wait_ge(s["summed"], r * 8 + m + 1)
                        add(m, 4 + m % 2)
                    for ep in range(2):
                        dve.wait_ge(s["silu_done"], r * 2 + ep + 1)
                        nc.vector.tensor_tensor(act_t[:, ep], turned_in(64, 128), act_t[:, ep], ALU.mult).then_inc(s["act_ready"], 1)
                    dve.wait_ge(used[7], r * 3 + 3)
                    nc.vector.tensor_copy(made, ps[:, 6:8, :].rearrange("p b n -> p (b n)")).then_inc(s["out_ready"], 1)
                dve.wait_ge(s["added"], PAIRS * 8 + 2)
                for m in range(KT):
                    dve.wait_ge(s["summed"], PAIRS * 8 + m + 1)
                    add(m, m % 4)


def second_block(nc, M, a, x, h, store):
    E = 16
    with ExitStack() as stack:
        sb = lambda name, shape: buffer(nc, stack, name, shape)
        mod, gains = sb("mod", [P, 6 * KT]), sb("gains", [P, 2, KT])
        modulation(nc, M, a["w_ada2"], mod)
        mcol = lambda i, k: mod[:, KT * i + k:KT * i + k + 1]
        with phase(nc, dve=0) as (block, s):
            @block.vector
            def _(dve):
                own = Own(dve, s["dve"])
                for i, name in enumerate(("norm1", "norm2")):
                    own.mark(nc.vector.scalar_tensor_tensor(out=gains[:, i, :], in0=mod[:, KT * (3 * i + 1):KT * (3 * i + 2)], scalar=1.0,
                                                            in1=M.last(name), op0=ALU.add, op1=ALU.mult))
        make_h = lambda: norm(nc, M, x, lambda k: gains[:, 0, k:k + 1], h, shift=lambda k: mcol(0, k))
        attn, delta = store[:, 0:4, :], store[:, 4:8, :]
        with ExitStack() as inner:
            matrices, gated = buffer(nc, inner, "matrices", [P, 2, KT * S]), buffer(nc, inner, "gated", [P, 4, S])
            raw = matrices[:, :, :].rearrange("p m n -> p (m n)")[:, 0:12 * (S + 4)].rearrange("p (j n) -> p j n", j=12)
            full_attention(nc, M, a, h, attn, raw, make_h)
            delta_net(nc, M, a, h, delta, matrices, raw, gated)
        with ExitStack() as inner:
            merged = buffer(nc, inner, "merged", [P, KT, S])
            with together(nc):
                ready = merge(nc, M, a["w_merge2"], h, attn, delta, merged)
                added = add_projection(nc, M, lambda j: a["w_o2"][j], KT, KT, merged, x, gain=lambda j: mcol(2, j), ready=ready)
                norm(nc, M, x, lambda k: gains[:, 1, k:k + 1], h, shift=lambda k: mcol(3, k), source=added)
        with ExitStack() as inner:
            sbi = lambda name, shape: buffer(nc, inner, name, shape)
            inputs, back, aff = sbi("expert_in", [P, KT, E, 64]), sbi("back", [P, PAIRS + 1, S]), sbi("aff", [P, TT, E])
            ring = sbi("expert_ring", [P, SLOTS, 2, D])
            landed = [inner.enter_context(nc.semaphore(f"expert_landed_{i}")) for i in range(SLOTS)]
            with ExitStack() as small:
                chosen = buffer(nc, small, "chosen", [P, TT, E, 64])
                tokens = store[:, 0:KT, :].rearrange("p (t k) n -> p t (k n)", t=TT)
                with together(nc):
                    route(nc, M, a["w_router2"], h, tokens, aff, chosen)
                    first_experts(nc, ring, a["w_expert2"], landed)
                gather(nc, M, tokens, chosen, inputs)
                turn_weights(nc, M, chosen, aff, back)
            made = store[:, 0:2, :].rearrange("p k n -> p (k n)")
            experts(nc, M, a["w_expert2"], inputs, made, back, lambda j: mcol(5, j), x, ring, landed)


def program(nc, a, out):
    with ExitStack() as stack:
        sb = lambda name, shape: buffer(nc, stack, name, shape)
        const_at, const_width = constant_offsets()
        layer_at, layer_width = offsets(LAYER_COLUMNS)
        last_at, last_width = offsets(LAST_COLUMNS)
        consts = sb("consts", [P, const_width])
        layer_cols, last_cols = sb("layer_cols", [P, layer_width]), sb("last_cols", [P, last_width])
        x, store = sb("x", [P, KT, S]), sb("store", [P, 2 * KT, S])
        y, h = store[:, 0:KT, :], store[:, KT:2 * KT, :]
        ps = stack.enter_context(nc.psum_tensor("ps", [P, 8, S], F32))
        M = Core(
            ps=ps, c=lambda n: consts[:, const_at[n][0]:sum(const_at[n])],
            cols=lambda n: layer_cols[:, layer_at[n][0]:sum(layer_at[n])],
            last=lambda n: last_cols[:, last_at[n][0]:sum(last_at[n])])
        col = lambda n, j: M.cols(n)[:, j:j + 1]
        lcol = lambda n, j: M.last(n)[:, j:j + 1]
        with phase(nc, landed=0) as (block, s):
            @block.sync
            def _(sp):
                sp.dma_start(consts[:, :], a["consts"]).then_inc(s["landed"], 16)
                sp.dma_start(x[:, :, :], a["x"]).then_inc(s["landed"], 16)
                sp.dma_start(last_cols[:, :], a["last_cols"]).then_inc(s["landed"], 16)
                sp.wait_ge(s["landed"], 48)

        with nc.Fori(0, DEPTH) as layer:
            with ExitStack() as inner:
                tables = buffer(nc, inner, "tables", [P, 4, S])
                names = ("cos_head", "sin_head", "cos_index", "sin_index")
                M.table = lambda n: tables[:, names.index(n), :]

                def make_h():
                    landed = load(nc, (layer_cols[:, :], a["layer_cols"][layer]), (tables[:, :, :], a["tables"][:, 0:4, :]))
                    return norm(nc, M, x, lambda k: col("norm_g", k), h, params=landed)

                raw = buffer(nc, inner, "raw", [P, N_R, S + 1])
                attention_branches(nc, M, h, y, lambda j: a["w_attn"][layer, j], a["w_tok"][layer],
                                   lambda j: a["w_rwkv"][layer, j], raw, make_h)
                w_out = lambda j: a["w_out"][layer, j]
                rwkv_branch(nc, M, x, y, raw, a["w_up"][layer], w_out, col)
                with together(nc):
                    added = add_projection(nc, M, lambda j: w_out(j)[:, 0:RP, :], KT, RP, y[:, 0:RP, :], x)
                    ready = norm(nc, M, x, lambda k: col("ple_g", k), h, source=added)
                    gated_embedding(nc, M, lambda j: a["ple_gate"][layer, j], a["ple_proj"][layer], a["p"][layer], h, x, ready)
        norm(nc, M, x, lambda k: lcol("final_g", k), x, scratch=h)
        second_block(nc, M, a, x, h, store)
        with phase(nc, stored=0) as (block, s):
            @block.sync
            def _(sp):
                sp.dma_start(out, x[:, :, :]).then_inc(s["stored"], 16)
                sp.wait_ge(s["stored"], 16)


def columns(vectors):
    return np.ascontiguousarray(np.concatenate([v.reshape(-1, P).T for v in vectors], axis=1))


def tiles(w, cols):
    w = w[:, cols]
    k, n = w.shape[0] // P, w.shape[1] // P
    return np.ascontiguousarray(w.reshape(k, P, n, P).transpose(2, 1, 0, 3))


def rows_first(w, cols=slice(None)):
    w = w[:, cols]
    return np.ascontiguousarray(w.reshape(w.shape[0] // P, P, w.shape[1]).transpose(1, 0, 2))


def layout(inp):
    r = np.arange
    g = {k: np.asarray(v) for k, v in inp.items()}
    dsa, dil = 1664, 2600
    attn = np.concatenate([dsa + r(256), np.tile(dsa + 256 + r(64), 2), dil + r(768), dsa + 384 + r(256),
                           np.tile(dsa + 640 + r(32), 4), dsa + 680 + r(256), dil + 1152 + r(384)])
    tok = np.concatenate([dsa + 320 + r(64), dsa + 672 + r(8), dil + 768 + r(384)])
    L = range(DEPTH)
    a = {
        "consts": np.concatenate(list(constant_parts().values()), axis=1),
        "tables": np.stack(list(rope_tables().values()), axis=1),
        "x": np.ascontiguousarray(g["x"][0].T.reshape(KT, P, S).transpose(1, 0, 2)),
        "p": np.stack([g["p"][l, 0].T.reshape(2, P, S).transpose(1, 0, 2) for l in L]),
        "layer_cols": np.stack([columns([g[n][l].reshape(-1) for n in (
            "norm_g", "tshift_mu", "rwkv_w0", "rwkv_a0", "rwkv_k_k", "rwkv_k_a", "rwkv_r_k", "rwkv_ln_g",
            "rwkv_ln_b", "ple_norm_g")]) for l in L]),
        "w_attn": np.stack([tiles(g["w_in"][l], attn) for l in L]),
        "w_rwkv": np.stack([tiles(g["w_in"][l], r(1664)) for l in L]),
        "w_tok": np.stack([rows_first(g["w_in"][l], tok) for l in L]),
        "w_up": np.concatenate([g["rwkv_w_up"], g["rwkv_a_up"]], axis=1),
        "w_out": np.stack([tiles(g["w_out"][l], slice(None)) for l in L]),
        "ple_gate": np.stack([tiles(g["ple_w_gate"][l], slice(None)) for l in L]),
        "ple_proj": np.stack([tiles(g["ple_w_proj"][l], slice(None)).transpose(1, 0, 2, 3) for l in L]),
    }
    w2 = g["w_in_2"][0]
    head_order = np.concatenate([kind + 8 * d + 2 * r(4) + hp for hp in range(2) for kind in (2816, 2832) for d in range(2)])
    a["w_attn2"] = tiles(w2, np.concatenate([r(512), np.tile(512 + r(64), 2), np.tile(576 + r(64), 2)]))
    a["w_v2"] = rows_first(w2, 640 + r(128))
    a["w_conv2"] = tiles(w2, 768 + r(1536))
    a["w_z2"] = tiles(w2, 2304 + r(512))
    a["w_ba2"] = rows_first(w2, head_order)
    a["w_merge2"] = np.concatenate([tiles(w2, 2848 + r(1024)), tiles(w2, 3872 + r(1024)),
                                    tiles(g["w_attn_up_2"][0], slice(None)), tiles(g["w_dn_up_2"][0], slice(None))], axis=2)
    a["w_ada2"] = g["w_ada_2"][0].reshape(4, 2, P, 3, 4, S).transpose(3, 0, 2, 4, 1, 5).reshape(12, P, 4, 2, S)
    a["w_o2"] = tiles(g["w_o_2"][0], slice(None))
    a["w_router2"] = rows_first(g["w_router_2"][0])
    cut = lambda w: w.reshape(8, 2, 4, 2, P, D).transpose(0, 1, 2, 4, 3, 5)
    up = np.stack([cut(g["w_gate_2"][0]), cut(g["w_up_2"][0])], axis=3).reshape(8, 16, P, 2, D)
    down = cut(g["w_down_2"][0]).transpose(0, 2, 1, 3, 4, 5).reshape(8, 8, P, 2, D)
    a["w_expert2"] = np.concatenate([up, down], axis=1)
    twice = lambda v: np.concatenate([v, v])
    conv = g["conv_w_2"][0]
    per_head = lambda v: np.repeat(v.reshape(2, 4, 2).transpose(2, 0, 1)[:, None], 64, axis=1).reshape(P, 8)
    a["last_cols"] = np.concatenate([
        columns([g["final_norm_g"], g["norm1_w_2"][0], g["norm2_w_2"][0], g["b_ada_2"][0], g["c_2"][0],
                 twice(g["q_norm_w_2"][0]), twice(g["k_norm_w_2"][0]), twice(g["dn_norm_w_2"][0])]),
        conv.reshape(5, 12, P).transpose(2, 1, 0).reshape(P, 60),
        per_head(g["a_log_2"][0]), per_head(g["dt_bias_2"][0])], axis=1)
    return {n: np.ascontiguousarray(v) for n, v in a.items()}


def kernel(**inputs):
    import concourse.bacc as bacc
    from concourse.bass_utils import run_bass_kernel_spmd

    nc = bacc.Bacc("TRN2", target_bir_lowering=False, num_devices=1)
    arrays = {f"in_{n}": v for n, v in layout(inputs).items()}
    aps = {n[3:]: nc.dram_tensor(n, v.shape, mybir.dt.from_np(v.dtype), kind="ExternalInput").ap() for n, v in arrays.items()}
    out = nc.dram_tensor("out", (P, KT, S), F32, kind="ExternalOutput").ap()
    program(nc, aps, out)
    got = run_bass_kernel_spmd(nc, [arrays], core_ids=[0]).results[0]["out"]
    return np.ascontiguousarray(got.transpose(1, 0, 2).reshape(D, S).T).reshape(1, S, D)
```

```python
import math
from contextlib import ExitStack, contextmanager

import numpy as np

import concourse.bass as bass
from concourse import mybir

F32 = mybir.dt.float32
U32 = mybir.dt.uint32
ALU = mybir.AluOpType
ACT = mybir.ActivationFunctionType
AX = mybir.AxisListType

P = 128
S = 512
D = 1024
KT = D // P
TT = S // P
DEPTH = 2
HD = 64
CH = 64
NCH = S // CH
LEVELS = (1, 2, 4, 8, 16, 32)

RW, RP = 384, 3
DECAY_SCALE = math.exp(-0.5)
NEG = -1e30
TAKEN = -3e38
TOPK = 128
NORM_EPS = 1e-6

A_Q, A_K, A_DQ, A_DK, A_IQ, A_IK, A_G, A_DG, N_A = 0, 2, 3, 6, 9, 11, 12, 14, 17
R_R, R_K, R_V, R_G, R_WA, N_R = 0, 3, 6, 9, 12, 13
V_DSA, V_IW, V_D0, V_D1, N_V = 0, 64, 72, 200, 456


def constant_parts():
    i = np.arange(P)
    t = np.arange(CH)
    parts = {}
    parts["ident"] = np.eye(P)
    parts["ones"] = np.ones((P, P))
    same = (i[:, None] // HD) == (i[None, :] // HD)
    parts["head_ones"] = same * 1.0
    row = np.arange(32)
    parts["head_rows"] = (i[:, None] // HD) == (row[None, :] // 16)
    parts["head_spread"] = (i[:, None] % 16 == 0) & ((i[:, None] % 32) // 16 == i[None, :] // HD)
    parts["sum_until"] = same & (i[:, None] <= i[None, :])
    parts["sum_from"] = same & (i[:, None] >= i[None, :])
    parts["ident2"] = (i[:, None] % CH) == t[None, :]

    def rotation(width, half):
        m = np.zeros((P, P))
        for c in range(P):
            d = c % width
            if d < half:
                m[c + half, c] = -1.0
            elif d < 2 * half:
                m[c - half, c] = 1.0
        return m

    parts["rot_head"] = rotation(64, 8)
    parts["rot_index"] = rotation(32, 4)
    parts["rot_axial"] = rotation(32, 16)
    q, k = i[:, None], i[None, :]
    causal = k <= q
    parts["neg_causal"] = np.where(causal, 0.0, NEG)
    parts["band"] = np.concatenate([np.where(k >= q, 0.0, NEG), parts["neg_causal"]], axis=1)
    parts["neg_mod4"] = np.where(causal & ((q - k) % 4 == 0), 0.0, NEG)
    r, c = t[:, None], t[None, :]
    lower = []
    for s in LEVELS:
        lower.append((r // (2 * s) == c // (2 * s)) & (r % (2 * s) >= s) & (c % (2 * s) < s))
    lower = np.stack(lower)
    upper = lower.transpose(0, 2, 1)
    two = lambda m: np.concatenate([m, m], axis=0)
    wide = lambda ms: two(np.concatenate(list(ms), axis=1))
    parts["level"] = wide([m for s in range(6) for m in (lower[s], upper[s], lower[s])])
    parts["strict"] = wide([c < r, c > r])
    parts["strict_T"] = wide([c > r, c < r])
    parts["incl_T"] = wide([c >= r, c <= r])
    parts["chunk_carry"] = np.broadcast_to((np.arange(S) % CH) != 0, (P, S))

    parts["slots"] = np.broadcast_to(np.arange(64)[None, :], (P, 64))
    return {n: np.asarray(a, np.float32) for n, a in parts.items()}


def rope_tables():
    tables = {}
    pos = np.arange(S, dtype=np.float32)

    def rope(width, half, rows, ang):
        cos, sin = np.ones((P, S), np.float32), np.zeros((P, S), np.float32)
        for ch in range(P):
            d = ch % width
            if d < 2 * half:
                cos[ch], sin[ch] = np.cos(ang[:, d % half]), np.sin(ang[:, d % half])
        return cos, sin

    for name, width, half in (("head", 64, 8), ("index", 32, 4)):
        inv = np.float32(500000.0) ** (-np.arange(half, dtype=np.float32) / np.float32(half))
        cos, sin = rope(width, half, P, pos[:, None] * inv[None, :].astype(np.float32))
        tables[f"cos_{name}"], tables[f"sin_{name}"] = cos, sin
    freqs = np.float32(10000.0) ** (-(np.arange(16, dtype=np.float32) * np.float32(2.0) / np.float32(32)))
    cos, sin = np.ones((P, S), np.float32), np.zeros((P, S), np.float32)
    for ch in range(P):
        where = (np.arange(S) // 64 if ch % 64 < 32 else np.arange(S) % 64).astype(np.float32)
        ang = where * freqs[ch % 16]
        cos[ch], sin[ch] = np.cos(ang), np.sin(ang)
    tables["cos_axial"], tables["sin_axial"] = cos, sin
    return tables


def constant_offsets():
    at, where = 0, {}
    for n, a in constant_parts().items():
        where[n] = (at, a.shape[1])
        at += a.shape[1]
    return where, at


LAYER_COLUMNS = (("norm_g", 8), ("mu", N_R), ("w0", 3), ("a0", 3), ("k_k", 3), ("k_a", 3), ("r_k", 3),
                 ("ln_g", 3), ("ln_b", 3), ("ple_g", 8), ("c_part", KT // DEPTH))
LAST_COLUMNS = (("final_g", 8), ("norm1", 8), ("norm2", 8), ("b_ada", 48), ("q_norm", 1),
                ("k_norm", 1), ("dn_norm", 1), ("conv", 60), ("a_log", 8), ("dt_bias", 8))


def offsets(columns):
    at, where = 0, {}
    for n, k in columns:
        where[n] = (at, k)
        at += k
    return where, at


class Core:

    def __init__(self, ps, c, cols, last):
        self.ps, self.c, self.cols, self.last, self.table = ps, c, cols, last, None


class Job:

    def __init__(self, q, k, keys, bias, v, out, gate, rows):
        self.q, self.k, self.keys, self.bias, self.v, self.out, self.gate, self.rows = q, k, keys, bias, v, out, gate, rows


JOINED = []


@contextmanager
def together(nc):
    with ExitStack() as stack:
        cleared = []
        with nc.Block(no_gpsimd_drain=True) as block:
            JOINED.append((block, stack, cleared))
            yield
            JOINED.pop()
        for sem in cleared:
            nc.sync.sem_clear(sem)
        nc.all_engine_barrier()


@contextmanager
def phase(nc, **counts):
    with ExitStack() as stack:
        sems = {}
        for name, n in counts.items():
            made = [stack.enter_context(nc.semaphore(f"{name}_{i}_{nc.next_id()}")) for i in range(max(n, 1))]
            sems[name] = made if n else made[0]
            if JOINED:
                JOINED[-1][2].extend(made)
        if JOINED:
            JOINED[-1][1].push(stack.pop_all())
            yield JOINED[-1][0], sems
            return
        with nc.Block(no_gpsimd_drain=True) as block:
            yield block, sems
        for made in sems.values():
            for sem in made if isinstance(made, list) else [made]:
                nc.sync.sem_clear(sem)
        nc.all_engine_barrier()


class Own:

    def __init__(self, eng, sem):
        self.eng, self.sem, self.n = eng, sem, 0

    def mark(self, ins):
        self.n += 1
        ins.then_inc(self.sem, 1)
        return self.n

    def step(self, ins):
        self.mark(ins)
        self.eng.wait_ge(self.sem, self.n)

    def settle(self):
        self.eng.wait_ge(self.sem, self.n)


def buffer(nc, stack, name, shape):
    stack = JOINED[-1][1] if JOINED else stack
    return stack.enter_context(nc.sbuf_tensor(f"{name}_{nc.next_id()}", list(shape), F32))


def load(nc, *pairs):
    with phase(nc, loaded=0) as (block, s):
        @block.sync
        def _(sp):
            for target, source in pairs:
                sp.dma_start(target, source).then_inc(s["loaded"], 16)
    return s["loaded"], 16 * len(pairs)


def norm(nc, M, src, gain, out, scratch=None, shift=None, source=None, params=None):
    total = M.ps[:, 7, :]
    squares = out if scratch is None else scratch
    with ExitStack() as stack:
        rstd = buffer(nc, stack, "rstd", [P, S])
        with phase(nc, squared=0, summed=0, var_ready=0, root_ready=0, dve=0) as (block, s):
            @block.scalar
            def _(act):
                for k in range(KT):
                    if source:
                        act.wait_ge(source[0], source[1] + k)
                    nc.scalar.activation(squares[:, k, :], src[:, k, :], ACT.Square).then_inc(s["squared"], 1)
                act.wait_ge(s["var_ready"], 1)
                nc.scalar.activation(rstd[:, :], rstd[:, :], ACT.Sqrt).then_inc(s["root_ready"], 1)
                if shift is not None:
                    for k in range(KT):
                        act.wait_ge(s["dve"], k + 2)
                        nc.scalar.activation(out[:, k, :], out[:, k, :], ACT.Identity,
                                             bias=shift(k)).then_inc(s["squared"], 1)

            @block.tensor
            def _(pe):
                for k in range(KT):
                    pe.wait_ge(s["squared"], k + 1)
                    last = nc.tensor.matmul(total, M.c("ones"), squares[:, k, :], start=(k == 0),
                                            stop=(k == KT - 1))
                last.then_inc(s["summed"], 1)

            @block.vector
            def _(dve):
                own = Own(dve, s["dve"])
                dve.wait_ge(s["summed"], 1)
                own.step(nc.vector.tensor_scalar(rstd[:, :], total, 1.0 / D, NORM_EPS, ALU.mult, ALU.add))
                nc.vector.reciprocal(rstd[:, :], rstd[:, :]).then_inc(s["var_ready"], 1)
                dve.wait_ge(s["root_ready"], 1)
                if params:
                    dve.wait_ge(*params)
                for k in range(KT):
                    own.mark(nc.vector.scalar_tensor_tensor(out=out[:, k, :], in0=src[:, k, :], scalar=gain(k),
                                                            in1=rstd[:, :], op0=ALU.mult, op1=ALU.mult))
    return (s["dve"], KT + 1) if shift is None else (s["squared"], 2 * KT)


def project(nc, M, weights, n, kt, src, unroll, finish, ready=None, ring=None):
    ps = M.ps
    assert n % unroll == 0
    rounds = n // unroll
    with ExitStack() as stack:
        if ring is None:
            ring = buffer(nc, stack, "weight_ring", [P, unroll, kt, P])
        with phase(nc, landed=unroll, tile_done=unroll, bank_free=unroll) as (block, s):
            @block.sync
            def _(sp):
                for u in range(unroll):
                    sp.dma_start(ring[:, u], weights(u)).then_inc(s["landed"][u], 16)
                if rounds > 1:
                    with sp.Fori(1, rounds) as r:
                        for u in range(unroll):
                            sp.wait_ge(s["tile_done"][u], r)
                            sp.dma_start(ring[:, u], weights(r * unroll + u)).then_inc(s["landed"][u], 16)

            @block.tensor
            def _(pe):
                if ready:
                    pe.wait_ge(*ready)
                with pe.Fori(0, rounds) as r:
                    for u in range(unroll):
                        pe.wait_ge(s["landed"][u], r * 16 + 16)
                        pe.wait_ge(s["bank_free"][u], r + 1)
                        for k in range(kt):
                            last = nc.tensor.matmul(ps[:, u, :], ring[:, u, k, :], src[:, k, :],
                                                    start=(k == 0), stop=(k == kt - 1))
                        last.then_inc(s["tile_done"][u], 1)

            @block.scalar
            def _(act):
                for u in range(unroll):
                    act.sem_inc(s["bank_free"][u], 1)
                with act.Fori(0, rounds) as r:
                    for u in range(unroll):
                        act.wait_ge(s["tile_done"][u], r + 1)
                        finish(act, r * unroll + u, ps[:, u, :]).then_inc(s["bank_free"][u], 1)


ADA_ROUNDS, ADA_STRIPS, ADA_SLOTS = 3, 4, 3
ADA_K = KT // DEPTH


def quarter_row(g):
    return slice(32 * g, 32 * g + 1)


class SideModulation:
    SEMAPHORES = dict(ada_landed=ADA_SLOTS, ada_used=0, ada_taken=0, c_ready=0)

    def __init__(self, nc, M, weights, c, rows, room, bank):
        self.nc, self.weights, self.c, self.rows, self.made = nc, weights, c, rows, M.ps[:, bank, :]
        self.slot = lambda i: room[:, (i % ADA_SLOTS) * ADA_STRIPS:(i % ADA_SLOTS + 1) * ADA_STRIPS, :]
        self.multiplied = 0

    def attach(self, s):
        self.s = s

    def load(self, sp):
        for i in range(ADA_ROUNDS * ADA_K):
            if i >= ADA_SLOTS:
                sp.wait_ge(self.s["ada_used"], i - ADA_SLOTS + 1)
            sp.dma_start(self.slot(i), self.weights(i)).then_inc(self.s["ada_landed"][i % ADA_SLOTS], 16)

    def prepare(self, act):
        self.nc.scalar.activation(self.c, self.c, ACT.Silu).then_inc(self.s["c_ready"], 1)

    def multiply(self, pe, upto):
        if self.multiplied == 0:
            pe.wait_ge(self.s["c_ready"], 1)
        while self.multiplied < upto:
            i = self.multiplied
            r, k = divmod(i, ADA_K)
            pe.wait_ge(self.s["ada_landed"][i % ADA_SLOTS], 16 * (i // ADA_SLOTS) + 16)
            if k == 0 and r > 0:
                pe.wait_ge(self.s["ada_taken"], ADA_STRIPS * r)
            for g in range(ADA_STRIPS):
                last = self.nc.tensor.matmul(self.made[quarter_row(g)], self.c[:, k:k + 1], self.slot(i)[:, g, :],
                                             start=(k == 0), stop=(k == ADA_K - 1))
            last.then_inc(self.s["ada_used"], 1)
            self.multiplied += 1

    def take(self, dve, r):
        dve.wait_ge(self.s["ada_used"], ADA_K * (r + 1))
        for g in range(ADA_STRIPS):
            row = self.rows[quarter_row(g), r, :]
            self.nc.vector.tensor_tensor(row, self.made[quarter_row(g)], row, ALU.add).then_inc(self.s["ada_taken"], 1)


class SideProjection:
    SEMAPHORES = dict(side_landed=4, side_done=0, side_taken=0)

    def __init__(self, nc, M, tiles, kt, src, ring, slots, banks):
        self.nc, self.ps, self.tiles, self.kt, self.src, self.banks = nc, M.ps, tiles, kt, src, banks
        self.ring, self.slots = ring, slots
        self.products = kt * len(tiles)
        self.multiplied = self.taken = 0

    def attach(self, s):
        self.s = s

    def load(self, sp):
        for j, (weights, _) in enumerate(self.tiles):
            if j >= self.slots:
                sp.wait_ge(self.s["side_done"], j - self.slots + 1)
            sp.dma_start(self.ring[:, j % self.slots], weights).then_inc(self.s["side_landed"][j % self.slots], 16)

    def multiply(self, pe, upto):
        banks = len(self.banks)
        while self.multiplied < min(upto, self.products):
            j, k = divmod(self.multiplied, self.kt)
            if k == 0:
                pe.wait_ge(self.s["side_landed"][j % self.slots], 16 * (j // self.slots) + 16)
                if j >= banks:
                    pe.wait_ge(self.s["side_taken"], j - banks + 1)
            ins = self.nc.tensor.matmul(self.ps[:, self.banks[j % banks], :], self.ring[:, j % self.slots, k, :],
                                        self.src[:, k, :], start=(k == 0), stop=(k == self.kt - 1))
            if k == self.kt - 1:
                ins.then_inc(self.s["side_done"], 1)
            self.multiplied += 1

    def take(self, act, upto):
        while self.taken < min(upto, len(self.tiles)):
            j = self.taken
            act.wait_ge(self.s["side_done"], j + 1)
            self.tiles[j][1](act, self.ps[:, self.banks[j % len(self.banks)], :]).then_inc(self.s["side_taken"], 1)
            self.taken += 1


def token_major(nc, M, weights, width, src, out, slices, ready, w=None):
    ps = M.ps
    with ExitStack() as stack:
        if w is None:
            w = buffer(nc, stack, "token_weights", [P, KT, width])
        with phase(nc, landed=0, tile_done=0, copied=0) as (block, s):
            @block.sync
            def _(sp):
                sp.dma_start(w[:, :, :], weights).then_inc(s["landed"], 16)

            @block.tensor
            def _(pe):
                pe.wait_ge(s["landed"], 16)
                if ready:
                    pe.wait_ge(*ready)
                for t in range(TT):
                    for a, b, tokens in slices:
                        for k in range(KT):
                            last = nc.tensor.matmul(ps[:, 4 + t, a:b], tokens(src[:, k, :], t), w[:, k, a:b],
                                                    start=(k == 0), stop=(k == KT - 1))
                    last.then_inc(s["tile_done"], 1)

            @block.vector
            def _(dve):
                for t in range(TT):
                    dve.wait_ge(s["tile_done"], t + 1)
                    nc.vector.tensor_copy(out[:, t, :], ps[:, 4 + t, 0:width]).then_inc(s["copied"], 1)


def in_order(row, t):
    return row[:, t * P:(t + 1) * P]


def by_residue(row, t):
    return row.rearrange("p (i r) -> p r i", r=4)[:, t, :]


def rope(nc, M, z, jobs):
    ps = M.ps
    with ExitStack() as stack:
        turned = buffer(nc, stack, "turned", [P, 2, S])
        with phase(nc, rotated=0, scaled=0, rot_used=0, dve=0) as (block, s):
            @block.tensor
            def _(pe):
                for j, (tile, table) in enumerate(jobs):
                    if j >= 4:
                        pe.wait_ge(s["rot_used"], j - 3)
                    nc.tensor.matmul(ps[:, j % 4, :], M.c(f"rot_{table}"), z[:, tile, :], start=True,
                                     stop=True).then_inc(s["rotated"], 1)

            @block.gpsimd
            def _(pool):
                for j, (tile, table) in enumerate(jobs):
                    pool.wait_ge(s["rotated"], j + 1)
                    nc.gpsimd.tensor_tensor(z[:, tile, :], z[:, tile, :], M.table(f"cos_{table}"),
                                            ALU.mult).then_inc(s["scaled"], 1)

            @block.vector
            def _(dve):
                own = Own(dve, s["dve"])
                for j, (tile, table) in enumerate(jobs):
                    dve.wait_ge(s["rotated"], j + 1)
                    if j >= 2:
                        dve.wait_ge(s["dve"], j - 1)
                    nc.vector.tensor_tensor(turned[:, j % 2, :], ps[:, j % 4, :], M.table(f"sin_{table}"),
                                            ALU.mult).then_inc(s["rot_used"], 1)
                    dve.wait_ge(s["rot_used"], j + 1)
                    dve.wait_ge(s["scaled"], j + 1)
                    own.mark(nc.vector.tensor_tensor(z[:, tile, :], z[:, tile, :], turned[:, j % 2, :], ALU.add))


def attention(nc, M, jobs, maxima, sums, side, beside=None, between=None):
    ps, n = M.ps, len(jobs)
    side_share = lambda i: -(-side.products * i // n)
    scale = HD ** -0.5
    with ExitStack() as stack:
        sb = lambda name, shape: buffer(nc, stack, name, shape)
        scores, probs, probs_t = sb("scores", [P, 2, S]), sb("probs", [P, 2, S]), sb("probs_t", [P, 2, S])
        minus_max, inverse = sb("minus_max", [P, 2]), sb("inverse", [P, 2])
        with phase(nc, scores_ready=0, bank_free=0, max_ready=0, exp_done=0, probs_ready=0, transposed=0,
                   probs_t_ready=0, pv_done=0, out_done=0, dve=0, beside=0, between=0, **SideProjection.SEMAPHORES) as (block, s):
            side.attach(s)

            @block.sync
            def _(sp):
                side.load(sp)

            @block.gpsimd
            def _(pool):
                if beside:
                    beside(pool, s)

            @block.tensor
            def _(pe):
                for i in range(n + 3):
                    if i < n:
                        job = jobs[i]
                        if i >= 2:
                            pe.wait_ge(s["bank_free"], i - 1)
                        nc.tensor.matmul(ps[:, i % 2, 0:job.keys], job.q, job.k, start=True,
                                         stop=True).then_inc(s["scores_ready"], 1)
                    side.multiply(pe, (side_share(i) + side_share(i + 1)) // 2)
                    if 2 <= i <= n + 1:
                        j = i - 2
                        pe.wait_ge(s["probs_ready"], j + 1)
                        if j >= 2:
                            pe.wait_ge(s["probs_t_ready"], j - 1)
                        for t in range(jobs[j].keys // P):
                            last = nc.tensor.transpose(ps[:, 2 + j % 2, t * P:(t + 1) * P],
                                                       probs[:, j % 2, t * P:(t + 1) * P], M.c("ident"))
                        last.then_inc(s["transposed"], 1)
                    side.multiply(pe, side_share(i + 1))
                    if i >= 3:
                        j = i - 3
                        job = jobs[j]
                        pe.wait_ge(s["probs_t_ready"], j + 1)
                        if j >= 2:
                            pe.wait_ge(s["out_done"], j - 1)
                        for t, v in enumerate(job.v):
                            last = nc.tensor.matmul(ps[job.rows:job.rows + HD, 4 + j % 2, 0:P], v,
                                                    probs_t[:, j % 2, t * P:(t + 1) * P],
                                                    start=(t == 0), stop=(t == len(job.v) - 1))
                        last.then_inc(s["pv_done"], 1)

            @block.scalar
            def _(act):
                for i in range(n + 2):
                    if i < n:
                        job = jobs[i]
                        act.wait_ge(s["max_ready"], i + 1)
                        if i >= 2:
                            act.wait_ge(s["transposed"], i - 1)
                        source = ps[:, i % 2, 0:job.keys] if job.bias is None else scores[:, i % 2, 0:job.keys]
                        nc.scalar.activation(probs[:, i % 2, 0:job.keys], source, ACT.Exp,
                                             bias=minus_max[:, i % 2:i % 2 + 1],
                                             scale=scale if job.bias is None else 1.0,
                                             accum_out=sums[:, i:i + 1]).then_inc(s["exp_done"], 1)
                        if job.bias is None:
                            act.wait_ge(s["exp_done"], i + 1)
                            act.sem_inc(s["bank_free"], 1)
                    if i >= 2:
                        j = i - 2
                        act.wait_ge(s["transposed"], j + 1)
                        if j >= 2:
                            act.wait_ge(s["pv_done"], j - 1)
                        nc.scalar.activation(probs_t[:, j % 2, 0:jobs[j].keys], ps[:, 2 + j % 2, 0:jobs[j].keys],
                                             ACT.Copy).then_inc(s["probs_t_ready"], 1)
                    side.take(act, side_share(i) // side.kt)
                side.take(act, len(side.tiles))

            @block.vector
            def _(dve):
                own = Own(dve, s["dve"])
                for i in range(n + 3):
                    if i < n:
                        job = jobs[i]
                        dve.wait_ge(s["scores_ready"], i + 1)
                        if i >= 2:
                            dve.wait_ge(s["exp_done"], i - 1)
                        source = ps[:, i % 2, 0:job.keys]
                        if job.bias is not None:
                            nc.vector.scalar_tensor_tensor(out=scores[:, i % 2, 0:job.keys], in0=source, scalar=scale,
                                                           in1=job.bias, op0=ALU.mult,
                                                           op1=ALU.add).then_inc(s["bank_free"], 1)
                            dve.wait_ge(s["bank_free"], i + 1)
                            source = scores[:, i % 2, 0:job.keys]
                        own.step(nc.vector.reduce_max(maxima[:, i:i + 1], source, AX.X))
                        nc.vector.tensor_scalar(minus_max[:, i % 2:i % 2 + 1], maxima[:, i:i + 1],
                                                -scale if job.bias is None else -1.0, None,
                                                ALU.mult).then_inc(s["max_ready"], 1)
                    if 1 <= i <= n:
                        j = i - 1
                        dve.wait_ge(s["exp_done"], j + 1)
                        own.step(nc.vector.reciprocal(inverse[:, j % 2:j % 2 + 1], sums[:, j:j + 1]))
                        keys = jobs[j].keys
                        nc.vector.tensor_scalar(probs[:, j % 2, 0:keys], probs[:, j % 2, 0:keys],
                                                inverse[:, j % 2:j % 2 + 1], None, ALU.mult).then_inc(s["probs_ready"], 1)
                    if i >= 3:
                        j = i - 3
                        job = jobs[j]
                        dve.wait_ge(s["pv_done"], j + 1)
                        made = ps[job.rows:job.rows + HD, 4 + j % 2, 0:P]
                        if job.gate is None:
                            nc.vector.tensor_copy(job.out, made).then_inc(s["out_done"], 1)
                        else:
                            nc.vector.tensor_tensor(job.out, made, job.gate, ALU.mult).then_inc(s["out_done"], 1)
                    if between:
                        between(dve, s, min(side_share(max(i - 2, 0)) // side.kt, len(side.tiles)), 2)
                if between:
                    between(dve, s, len(side.tiles), 1000)


def index_topk(nc, M, z, tok, bias, side):
    ps = M.ps
    with ExitStack() as stack:
        sb = lambda name, shape: buffer(nc, stack, name, shape)
        weight, relus, best = sb("index_weight", [P, TT, 8]), sb("relus", [P, 2, S]), sb("best", [P, 3, 8])
        with phase(nc, scored=0, relu_done=0, added=0, dve=0, **SideProjection.SEMAPHORES) as (block, s):
            side.attach(s)

            @block.sync
            def _(sp):
                side.load(sp)

            @block.tensor
            def _(pe):
                for j in range(24):
                    b, h = 1 + j // 8, j % 8
                    if j >= 4:
                        pe.wait_ge(s["relu_done"], j - 3)
                    rows = slice(32 * (h % 4), 32 * (h % 4) + 32)
                    nc.tensor.matmul(ps[:, h % 4, 0:(b + 1) * P], z[rows, A_IQ + h // 4, b * P:(b + 1) * P],
                                     z[rows, A_IK, 0:(b + 1) * P], start=True, stop=True,
                                     tile_position=(32 * (h % 4), 0)).then_inc(s["scored"], 1)
                    side.multiply(pe, j - 3)
                side.multiply(pe, side.products)

            @block.scalar
            def _(act):
                for j in range(24):
                    b, h = 1 + j // 8, j % 8
                    act.wait_ge(s["scored"], j + 1)
                    if j >= 2:
                        act.wait_ge(s["added"], j - 1)
                    nc.scalar.activation(relus[:, j % 2, 0:(b + 1) * P], ps[:, h % 4, 0:(b + 1) * P], ACT.Relu,
                                         scale=32 ** -0.5).then_inc(s["relu_done"], 1)
                    side.take(act, (j - 5) // KT)
                side.take(act, len(side.tiles))

            @block.vector
            def _(dve):
                own = Own(dve, s["dve"])
                own.step(nc.vector.tensor_scalar(weight[:, :, :], tok[:, :, V_IW:V_IW + 8], 8 ** -0.5, None, ALU.mult))
                own.step(nc.vector.tensor_copy(bias(0), M.c("neg_causal")))
                for j in range(24):
                    b, h = 1 + j // 8, j % 8
                    dve.wait_ge(s["relu_done"], j + 1)
                    r, w = relus[:, j % 2, 0:(b + 1) * P], weight[:, b, h:h + 1]
                    if h == 0:
                        ins = nc.vector.tensor_scalar(bias(b), r, w, None, ALU.mult)
                    else:
                        ins = nc.vector.scalar_tensor_tensor(out=bias(b), in0=r, scalar=w, in1=bias(b),
                                                             op0=ALU.mult, op1=ALU.add)
                    ins.then_inc(s["added"], 1)
                    dve.wait_ge(s["added"], j + 1)
                for b in range(1, TT):
                    last = bias(b)[:, b * P:(b + 1) * P]
                    own.step(nc.vector.tensor_tensor(last, last, M.c("neg_causal"), ALU.add))
                for turn in range(TOPK // 8):
                    for b in range(1, TT):
                        own.mark(nc.vector.max(best[:, b - 1, :], bias(b)))
                    own.settle()
                    for b in range(1, TT):
                        own.mark(nc.vector.match_replace(out=bias(b), in_to_replace=best[:, b - 1, :],
                                                         in_values=bias(b), imm_value=TAKEN))
                    own.settle()
                for b in range(1, TT):
                    own.mark(nc.vector.tensor_scalar(bias(b), bias(b), -2e38, NEG, ALU.is_gt, ALU.mult))


def combine_groups(nc, M, z, od, maxima, sums, y, room):
    ps = M.ps
    with ExitStack() as stack:
        sb = lambda name, shape: buffer(nc, stack, name, shape)
        lse, share, total = sb("lse", [P, 24]), sb("share", [P, 3, S]), sb("total", [P, S])
        diag, first, top = room[:, 0:6, :], room[:, 6, :], room[:, 7, :]
        with phase(nc, logs=0, diag_ready=0, spread_done=0, first_ready=0, centred=0, exp_done=0, dve=0) as (block, s):
            @block.scalar
            def _(act):
                nc.scalar.activation(lse[:, :], sums, ACT.Ln).then_inc(s["logs"], 1)
                act.wait_ge(s["spread_done"], 6)
                nc.scalar.activation(first, ps[:, 0, :], ACT.Copy).then_inc(s["first_ready"], 1)
                act.wait_ge(s["centred"], 3)
                nc.scalar.activation(share[:, :, :], share[:, :, :], ACT.Exp).then_inc(s["exp_done"], 1)

            @block.tensor
            def _(pe):
                for g in range(3):
                    for j in range(2):
                        pe.wait_ge(s["diag_ready"], 2 * g + j + 1)
                        row = ps[HD * j:HD * j + HD, g, :]
                        out = row.rearrange("p (t i) -> p t i", t=4) if g == 0 else row.rearrange(
                            "p (i r) -> p r i", r=4)
                        nc.tensor.matmul(out, M.c("ones")[:, 0:HD],
                                         diag[:, 2 * g + j, :].rearrange("p (t i) -> p t i", t=4),
                                         start=True, stop=True).then_inc(s["spread_done"], 1)

            @block.vector
            def _(dve):
                own = Own(dve, s["dve"])
                dve.wait_ge(s["logs"], 1)
                own.step(nc.vector.tensor_tensor(lse[:, :], lse[:, :], maxima, ALU.add))
                for g in range(3):
                    for j in range(2):
                        col = lse[:, 8 * g + j:8 * g + j + 7:2].unsqueeze(2).broadcast_to([P, 4, P])
                        nc.vector.tensor_tensor(diag[:, 2 * g + j, :].rearrange("p (t i) -> p t i", t=4),
                                                M.c("ident").unsqueeze(1).broadcast_to([P, 4, P]), col,
                                                ALU.mult).then_inc(s["diag_ready"], 1)
                dve.wait_ge(s["first_ready"], 1)
                own.step(nc.vector.tensor_tensor(top, first, ps[:, 1, :], ALU.max))
                own.step(nc.vector.tensor_tensor(top, top, ps[:, 2, :], ALU.max))
                for g in range(3):
                    nc.vector.tensor_tensor(share[:, g, :], ps[:, g, :], top, ALU.subtract).then_inc(s["centred"], 1)
                dve.wait_ge(s["exp_done"], 1)
                own.step(nc.vector.tensor_tensor(total[:, :], share[:, 0, :], share[:, 1, :], ALU.add))
                own.step(nc.vector.tensor_tensor(total[:, :], total[:, :], share[:, 2, :], ALU.add))
                own.step(nc.vector.reciprocal(total[:, :], total[:, :]))
                for g in range(3):
                    own.mark(nc.vector.tensor_tensor(share[:, g, :], share[:, g, :], total[:, :], ALU.mult))
                own.settle()
                for g in range(3):
                    own.mark(nc.vector.tensor_tensor(share[:, g, :], share[:, g, :], od[:, g, :], ALU.mult))
                own.settle()
                for g in range(3):
                    own.mark(nc.vector.tensor_tensor(y[:, 5 + g, :], share[:, g, :], z[:, A_DG + g, :], ALU.mult))


def attention_branches(nc, M, h, y, w_attn, w_tok, w_rwkv, raw, mixed_z, make_h):
    with ExitStack() as stack:
        sb = lambda name, shape: buffer(nc, stack, name, shape)
        z, tok = sb("attn_z", [P, N_A, S]), sb("attn_tok", [P, TT, N_V])
        bias_all = sb("bias", [P, P + 2 * P + 3 * P + 4 * P])
        bias = lambda b: bias_all[:, P * (b * (b + 1) // 2):P * ((b + 1) * (b + 2) // 2)]
        od = y[:, 5:8, :]
        maxima, sums = sb("maxima", [P, 40]), sb("sums", [P, 40])
        keep = lambda act, j, made: nc.scalar.activation(z[:, j, :], made, ACT.Copy)
        ring = sb("side_ring", [P, 4, KT, P])
        with together(nc):
            ready = make_h()
            project(nc, M, w_attn, A_G, KT, h, 4, keep, ready, ring)
            spare = mixed_z[:, :, :].rearrange("p j n -> p (j n)")[:, 0:KT * N_V].rearrange("p (k n) -> p k n", k=KT)
            token_major(nc, M, w_tok, N_V, h, tok, ((0, V_D1, in_order), (V_D1, N_V, by_residue)), ready, spare)
            with phase(nc, cleared=0) as (block, s):
                @block.vector
                def _(dve):
                    nc.vector.memset(raw[:, :, 0:1], 0.0).then_inc(s["cleared"], 1)
        rope(nc, M, z, [(t, "head") for t in range(A_IQ)] + [(t, "index") for t in range(A_IQ, A_IK + 1)])
        silu = lambda j: (w_attn(j), lambda act, made: nc.scalar.activation(z[:, j, :], made, ACT.Silu))
        mixed = lambda j: (w_rwkv(j), lambda act, made: nc.scalar.activation(raw[:, j, 1:S + 1], made, ACT.Copy))
        late = 9
        early = 4
        side = SideProjection(nc, M, [silu(j) for j in range(A_G, N_A)] + [mixed(j) for j in range(early)], KT, h, ring,
                              4, (4, 5, 6, 7))
        index_topk(nc, M, z, tok, bias, side)
        jobs = []
        for b in range(TT):
            for hd in range(4):
                rows = HD * (hd % 2)
                here = slice(b * P, (b + 1) * P)
                jobs.append(Job(
                    q=z[rows:rows + HD, A_Q + hd // 2, here], k=z[rows:rows + HD, A_K, 0:(b + 1) * P],
                    keys=(b + 1) * P, bias=bias(b), v=[tok[:, t, V_DSA:V_DSA + HD] for t in range(b + 1)],
                    out=y[rows:rows + HD, 3 + hd // 2, here], gate=z[rows:rows + HD, A_G + hd // 2, here], rows=rows))
        for g in range(3):
            for t in range(TT):
                for j in range(2):
                    rows = HD * j
                    row = lambda buf, tile: buf[rows:rows + HD, tile, :]
                    v0 = (V_D0 if g == 0 else V_D1 + P * (g - 1)) + HD * j
                    if g == 0:
                        here, first = slice(t * P, (t + 1) * P), max(t - 1, 0)
                        job = Job(q=row(z, A_DQ)[:, here], k=row(z, A_DK)[:, first * P:(t + 1) * P],
                                              keys=(t + 1 - first) * P, bias=M.c("band") if t else M.c("neg_causal"),
                                              v=[tok[:, u, v0:v0 + HD] for u in range(first, t + 1)],
                                              out=row(od, 0)[:, here], gate=None, rows=rows)
                    else:
                        job = Job(q=by_residue(row(z, A_DQ + g), t), k=by_residue(row(z, A_DK + g), t),
                                              keys=P, bias=M.c("neg_causal" if g == 1 else "neg_mod4"),
                                              v=[tok[:, t, v0:v0 + HD]], out=by_residue(row(od, g), t),
                                              gate=None, rows=rows)
                    jobs.append(job)
        side = SideProjection(nc, M, [mixed(j) for j in range(early, N_R)], KT, h, ring, 4, (6, 7))

        def shift(pool, s):
            for j in range(late):
                if j >= early:
                    pool.wait_ge(s["side_taken"], j - early + 1)
                nc.gpsimd.tensor_tensor(mixed_z[:, j, :], raw[:, j, 0:S], raw[:, j, 1:S + 1], ALU.subtract).then_inc(s["beside"], 1)
                pool.wait_ge(s["beside"], 3 * j + 1)
                nc.gpsimd.tensor_scalar(mixed_z[:, j, :], mixed_z[:, j, :], M.cols("mu")[:, j:j + 1], None,
                                        ALU.mult).then_inc(s["beside"], 1)
                pool.wait_ge(s["beside"], 3 * j + 2)
                nc.gpsimd.tensor_tensor(mixed_z[:, j, :], mixed_z[:, j, :], raw[:, j, 1:S + 1], ALU.add).then_inc(s["beside"], 1)
            pool.wait_ge(s["beside"], 3 * late)

        steps = [(j, i) for j in range(late, N_R) for i in range(2)]

        def shift_late(dve, s, taken, most):
            for _ in range(most):
                if not steps or steps[0][0] >= early + taken:
                    return
                j, i = steps.pop(0)
                if i == 0:
                    dve.wait_ge(s["side_taken"], j - early + 1)
                    ins = nc.vector.tensor_tensor(mixed_z[:, j, :], raw[:, j, 0:S], raw[:, j, 1:S + 1], ALU.subtract)
                else:
                    dve.wait_ge(s["between"], 2 * (j - late) + 1)
                    ins = nc.vector.scalar_tensor_tensor(out=mixed_z[:, j, :], in0=mixed_z[:, j, :], scalar=M.cols("mu")[:, j:j + 1],
                                                         in1=raw[:, j, 1:S + 1], op0=ALU.mult, op1=ALU.add)
                ins.then_inc(s["between"], 1)

        attention(nc, M, jobs, maxima, sums, side, shift, shift_late)
        combine_groups(nc, M, z, od, maxima[:, 16:40], sums[:, 16:40], y,
                       ring[:, :, :, :].rearrange("p u k c -> p (u k c)").rearrange("p (t n) -> p t n", n=S))


def invert(nc, M, lower, inv, inv_t, groups, gsize, signs, dirs):
    ps = M.ps
    blocks = gsize
    level = M.c("level").rearrange("p (l d t) -> p l d t", l=6, d=3)
    strict_sum = ALU.subtract if signs > 0 else ALU.add

    def mask(lv, flip):
        m = level[:, lv, flip:flip + dirs, :]
        if dirs == 1:
            return m.broadcast_to([P, blocks, CH])
        return m.unsqueeze(2).broadcast_to([P, dirs, blocks // dirs, CH])

    def view(ap):
        return ap if dirs == 1 else ap.rearrange("p (d b) t -> p d b t", d=dirs)

    def bank(i):
        return ps[:, i, 0:blocks * CH].rearrange("p (b t) -> p b t", b=blocks)

    with ExitStack() as stack:
        sb = lambda name, shape: buffer(nc, stack, name, shape)
        half, parts = sb("half", [P, 2, blocks, CH]), sb("parts", [P, 2, 2, blocks, CH])
        eye = M.c("ident2").unsqueeze(1).broadcast_to([P, blocks, CH])
        with phase(nc, lt_ready=0, t_ready=0, half_ready=0, half_copied=0, product=0, product_used=0, dve=0) as (block, s):
            def pairs():
                for b in range(blocks):
                    for rows in (slice(0, HD), slice(HD, P)):
                        yield b, rows

            def second(pe, job):
                g = job % groups
                pe.wait_ge(s["half_copied"], job + 1)
                if job >= 2:
                    pe.wait_ge(s["product_used"], job - 1)
                for b, rows in pairs():
                    y = half[rows, job % 2, b, :]
                    if job < 4 * groups:
                        nc.tensor.matmul(bank(4 + job % 2)[rows, b, :], y, inv[rows, g, b, :], start=True, stop=True)
                    last = nc.tensor.matmul(bank(6 + job % 2)[rows, b, :], inv[rows, g, b, :], y, start=True, stop=True)
                last.then_inc(s["product"], 1)

            @block.tensor
            def _(pe):
                for g in range(groups):
                    if g >= 2:
                        pe.wait_ge(s["t_ready"], g - 1)
                    for b, rows in pairs():
                        last = nc.tensor.matmul(bank(g % 2)[rows, b, :], lower[rows, g, b, :],
                                                M.c("ident2")[rows, :], start=True, stop=True)
                    last.then_inc(s["lt_ready"], 1)
                job = 0
                for lv in range(1, 6):
                    for g in range(groups):
                        pe.wait_ge(s["t_ready"], lv * groups - groups + g + 1)
                        if job >= 2:
                            pe.wait_ge(s["half_copied"], job - 1)
                        for b, rows in pairs():
                            last = nc.tensor.matmul(bank(2 + job % 2)[rows, b, :], lower[rows, g, b, :],
                                                    inv_t[rows, g, b, :], start=True, stop=True)
                        last.then_inc(s["half_ready"], 1)
                        job += 1
                        if job >= 2:
                            second(pe, job - 2)
                second(pe, job - 1)

            @block.scalar
            def _(act):
                for job in range(5 * groups):
                    act.wait_ge(s["half_ready"], job + 1)
                    if job >= 2:
                        act.wait_ge(s["product"], job - 1)
                    nc.scalar.activation(half[:, job % 2], bank(2 + job % 2), ACT.Copy,
                                         ).then_inc(s["half_copied"], 1)

            @block.vector
            def _(dve):
                own = Own(dve, s["dve"])
                for g in range(groups):
                    dve.wait_ge(s["lt_ready"], g + 1)
                    own.mark(nc.vector.tensor_tensor(view(inv[:, g]), view(lower[:, g]), mask(0, 0), ALU.mult))
                    own.step(nc.vector.tensor_tensor(view(inv_t[:, g]), view(bank(g % 2)), mask(0, 1), ALU.mult))
                    own.mark(nc.vector.tensor_tensor(inv[:, g], eye, inv[:, g], strict_sum))
                    own.step(nc.vector.tensor_tensor(inv_t[:, g], eye, inv_t[:, g], strict_sum))
                    dve.sem_inc(s["t_ready"], 1)
                for job in range(5 * groups):
                    lv, g = 1 + job // groups, job % groups
                    dve.wait_ge(s["product"], job + 1)
                    k = job % 2
                    if lv < 5:
                        own.mark(nc.vector.tensor_tensor(view(parts[:, k, 0]), view(bank(4 + k)), mask(lv, 0), ALU.mult))
                    own.mark(nc.vector.tensor_tensor(view(parts[:, k, 1]), view(bank(6 + k)), mask(lv, 1), ALU.mult))
                    own.settle()
                    dve.sem_inc(s["product_used"], 1)
                    if lv < 5:
                        own.mark(nc.vector.tensor_tensor(inv[:, g], inv[:, g], parts[:, k, 0], strict_sum))
                    own.step(nc.vector.tensor_tensor(inv_t[:, g], inv_t[:, g], parts[:, k, 1], strict_sum))
                    dve.sem_inc(s["t_ready"], 1)


def rwkv_branch(nc, M, x, y, raw, z, up_weights, w_out, w_ada, ada_rows, col):
    ps = M.ps
    with ExitStack() as outer:
        sb = lambda name, shape: buffer(nc, outer, name, shape)
        at, bt, kt_, bonus = (sb(x, [P, RP, S]) for x in ("rw_a", "rw_b", "rw_k", "bonus"))
        end_decay = sb("end_decay", [P, RP, NCH])
        r, k, v = z[:, R_R:R_R + 3, :], z[:, R_K:R_K + 3, :], z[:, R_V:R_V + 3, :]

        with ExitStack() as stack:
            sbt = lambda name, shape: buffer(nc, stack, name, shape)
            up = sbt("up", [P, RW])
            logw, cum, rate, tmp = (sbt(x, [P, RP, S]) for x in ("logw", "cum", "rate", "tmp"))
            grow, keep = sbt("grow", [P, RP, S]), sbt("keep", [P, RP])
            spare = raw[:, :, :].rearrange("p j n -> p (j n)")[:, 0:ADA_SLOTS * ADA_STRIPS * S].rearrange("p (j n) -> p j n", n=S)
            ada = SideModulation(nc, M, w_ada, M.cols("c_part"), ada_rows, spare, 7)
            with phase(nc, **SideModulation.SEMAPHORES, up_landed=0, tanh_done=0, raised=0, sig_done=0, log_ready=0, exps=0, squares=0, normed=0,
                       root_ready=0, root=0, inv_norm=0, spread=0, rk_ready=0, rk_summed=0, gated=0, dve=0) as (block, s):
                ada.attach(s)

                @block.sync
                def _(sp):
                    sp.dma_start(up[:, :], up_weights).then_inc(s["up_landed"], 16)
                    ada.load(sp)

                @block.tensor
                def _(pe):
                    pe.wait_ge(s["up_landed"], 16)
                    pe.wait_ge(s["tanh_done"], 1)
                    for j in range(RP):
                        nc.tensor.matmul(ps[:, j, :], up[0:HD, j * P:(j + 1) * P], z[0:HD, R_WA, :], start=True,
                                         stop=True).then_inc(s["raised"], 1)
                        nc.tensor.matmul(ps[:, 3 + j, :], up[HD:P, j * P:(j + 1) * P], z[HD:P, R_WA, :],
                                         start=True, stop=True).then_inc(s["raised"], 1)
                    ada.multiply(pe, 2)
                    pe.wait_ge(s["squares"], 1)
                    pe.wait_ge(s["sig_done"], 6)
                    for j in range(RP):
                        nc.tensor.matmul(ps[32 * j:32 * j + 32, 0, :], M.c("head_rows"), tmp[:, j, :], start=True,
                                         stop=True).then_inc(s["normed"], 1)
                    ada.multiply(pe, 4)
                    pe.wait_ge(s["inv_norm"], 1)
                    for j in range(RP):
                        w = slice(32 * j, 32 * j + 32)
                        nc.tensor.matmul(ps[:, (1, 2, 6)[j], :], M.c("head_spread")[w, :], grow[w, 0, :], start=True,
                                         stop=True, tile_position=(32 * j, 0)).then_inc(s["spread"], 1)
                    ada.multiply(pe, 7)
                    pe.wait_ge(s["rk_ready"], 1)
                    for j in range(RP):
                        nc.tensor.matmul(ps[:, 3 + j, :], M.c("head_ones"), bonus[:, j, :], start=True,
                                         stop=True).then_inc(s["rk_summed"], 1)
                    ada.multiply(pe, ADA_ROUNDS * ADA_K)

                @block.scalar
                def _(act):
                    nc.scalar.activation(z[0:HD, R_WA, :], z[0:HD, R_WA, :], ACT.Tanh).then_inc(s["tanh_done"], 1)
                    ada.prepare(act)
                    for j in range(RP):
                        act.wait_ge(s["raised"], 2 * j + 2)
                        nc.scalar.activation(logw[:, j, :], ps[:, j, :], ACT.Sigmoid,
                                             bias=col("w0", j)).then_inc(s["sig_done"], 1)
                        nc.scalar.activation(rate[:, j, :], ps[:, 3 + j, :], ACT.Sigmoid,
                                             bias=col("a0", j)).then_inc(s["sig_done"], 1)
                    act.wait_ge(s["root_ready"], 1)
                    nc.scalar.activation(tmp[:, :, :], tmp[:, :, :], ACT.Copy).then_inc(s["squares"], 1)
                    act.wait_ge(s["normed"], RP)
                    nc.scalar.activation(grow[0:32 * RP, 0, :], ps[0:32 * RP, 0, :], ACT.Sqrt).then_inc(s["root"], 1)
                    act.wait_ge(s["log_ready"], 1)
                    act.wait_ge(s["rk_ready"], 1)
                    nc.scalar.activation(tmp[:, :, :], cum[:, :, :], ACT.Exp).then_inc(s["exps"], 1)
                    act.wait_ge(s["root_ready"], 2)
                    nc.scalar.activation(grow[:, :, :], cum[:, :, :], ACT.Exp, scale=-1.0).then_inc(s["exps"], 1)
                    nc.scalar.activation(logw[:, :, :], logw[:, :, :], ACT.Exp).then_inc(s["exps"], 1)
                    nc.scalar.activation(z[:, R_G:R_G + 3, :], z[:, R_G:R_G + 3, :], ACT.Silu).then_inc(s["gated"], 1)

                @block.vector
                def _(dve):
                    own = Own(dve, s["dve"])
                    V = nc.vector
                    own.mark(V.tensor_scalar(keep[:, :], M.cols("k_a"), -1.0, 1.0, ALU.mult, ALU.add))
                    for j in range(RP):
                        own.mark(V.tensor_scalar(at[:, j, :], k[:, j, :], col("k_k", j), None, ALU.mult))
                    own.settle()
                    V.tensor_tensor(tmp[:, :, :], at[:, :, :], at[:, :, :], ALU.mult).then_inc(s["root_ready"], 1)
                    dve.wait_ge(s["sig_done"], 6)
                    own.step(V.tensor_scalar(logw[:, :, :], logw[:, :, :], -DECAY_SCALE, None, ALU.mult))
                    for j in range(RP):
                        own.mark(V.tensor_tensor_scan(cum[:, j, :], M.c("chunk_carry"), logw[:, j, :], 0.0,
                                                      ALU.mult, ALU.add))
                    own.settle()
                    V.tensor_tensor(logw[:, :, :], cum[:, :, :], logw[:, :, :], ALU.subtract).then_inc(s["log_ready"], 1)
                    dve.wait_ge(s["root"], 1)
                    norms = grow[0:32 * RP, 0, :]
                    own.step(V.tensor_scalar(norms, norms, 1e-12, None, ALU.max))
                    V.reciprocal(norms, norms).then_inc(s["inv_norm"], 1)
                    for j in range(RP):
                        dve.wait_ge(s["spread"], j + 1)
                        own.mark(V.tensor_tensor(at[:, j, :], at[:, j, :], ps[:, (1, 2, 6)[j], :], ALU.mult))
                    own.settle()
                    dve.sem_inc(s["root_ready"], 1)
                    ada.take(dve, 0)
                    dve.wait_ge(s["normed"], 3)
                    for j in range(RP):
                        own.mark(V.tensor_scalar(tmp[:, j, :], rate[:, j, :], col("k_a", j), keep[:, j:j + 1],
                                                 ALU.mult, ALU.add))
                    own.settle()
                    own.step(V.tensor_tensor(k, k, tmp[:, :, :], ALU.mult))
                    for j in range(RP):
                        own.mark(V.scalar_tensor_tensor(out=bonus[:, j, :], in0=r[:, j, :], scalar=col("r_k", j),
                                                        in1=k[:, j, :], op0=ALU.mult, op1=ALU.mult))
                    own.settle()
                    own.step(V.tensor_tensor(bt[:, :, :], at[:, :, :], rate[:, :, :], ALU.mult))
                    dve.sem_inc(s["rk_ready"], 1)
                    dve.wait_ge(s["exps"], 3)
                    own.mark(V.tensor_tensor(bt[:, :, :], bt[:, :, :], grow[:, :, :], ALU.mult))
                    own.mark(V.tensor_tensor(kt_[:, :, :], k, grow[:, :, :], ALU.mult))
                    own.mark(V.scalar_tensor_tensor(out=at[:, :, :], in0=at[:, :, :], scalar=-1.0, in1=logw[:, :, :],
                                                    op0=ALU.mult, op1=ALU.mult))
                    own.mark(V.tensor_tensor(r, r, tmp[:, :, :], ALU.mult))
                    own.mark(V.tensor_copy(end_decay[:, :, :], tmp[:, :, CH - 1:S:CH]))
                    dve.wait_ge(s["rk_summed"], 3)
                    for j in range(RP):
                        own.mark(V.tensor_tensor(bonus[:, j, :], ps[:, 3 + j, :], v[:, j, :], ALU.mult))
                    ada.take(dve, 1)
                    ada.take(dve, 2)

        with ExitStack() as stack:
            sbt = lambda name, shape: buffer(nc, stack, name, shape)
            block_shape = [P, NCH, RP, CH]
            ak_t, rb_t, rk_t = (sbt(x, block_shape) for x in ("ak_t", "rb_t", "rk_t"))
            spare = raw[:, :, :].rearrange("p j n -> p (j n)")[:, 0:4 * RP * S]
            v_tok, b_tok, k_tok, low = (spare[:, i * RP * S:(i + 1) * RP * S].rearrange("p (c j t) -> p c j t", c=NCH, j=RP)
                                        for i in range(4))
            inv, inv_t = sbt("inv", block_shape), sbt("inv_t", block_shape)
            chunked = lambda ap: ap.rearrange("p j (c t) -> p c j t", t=CH)
            rc, kc, vc, ac, bc = (chunked(x) for x in (r, kt_[:, :, :], v, at[:, :, :], bt[:, :, :]))
            eye = lambda c, j, rows: M.c("ident2")[rows, :]
            pick = lambda ap: (lambda c, j, rows: ap[rows, c, j, :])
            kinds = ((v_tok, pick(vc), eye, None), (b_tok, pick(bc), eye, None), (k_tok, pick(kc), eye, None),
                     (low, pick(ac), pick(bc), "strict"), (ak_t, pick(kc), pick(ac), "strict_T"),
                     (rb_t, pick(bc), pick(rc), "incl_T"), (rk_t, pick(kc), pick(rc), "incl_T"))
            bank = lambda i: ps[:, i, 0:2 * RP * CH].rearrange("p (c j t) -> p c j t", c=2, j=RP)
            todo = [(kind, c2) for c2 in range(NCH // 2) for kind in kinds]
            with phase(nc, made=0, taken=0) as (block, s):
                @block.tensor
                def _(pe):
                    for i, ((_, lhs, rhs, _), c2) in enumerate(todo):
                        if i >= 4:
                            pe.wait_ge(s["taken"], i - 3)
                        for c in range(2):
                            for j in range(RP):
                                for rows in (slice(0, HD), slice(HD, P)):
                                    last = nc.tensor.matmul(bank(i % 4)[rows, c, j, :], lhs(2 * c2 + c, j, rows),
                                                            rhs(2 * c2 + c, j, rows), start=True, stop=True)
                        last.then_inc(s["made"], 1)

                @block.vector
                def _(dve):
                    for i, ((target, _, _, mask), c2) in enumerate(todo):
                        dve.wait_ge(s["made"], i + 1)
                        out = target[:, 2 * c2:2 * c2 + 2]
                        if mask is None:
                            ins = nc.vector.tensor_copy(out, bank(i % 4))
                        else:
                            out = out.rearrange("p c j t -> p (c j) t")
                            made = bank(i % 4).rearrange("p c j t -> p (c j) t")
                            m = M.c(mask)[:, 0:CH].unsqueeze(1).broadcast_to([P, 2 * RP, CH])
                            ins = nc.vector.tensor_tensor(out, made, m, ALU.mult)
                        ins.then_inc(s["taken"], 1)

            pairs_of = lambda a: a[:, :, :, :].rearrange("p (g c) j t -> p g (c j) t", c=2)
            invert(nc, M, pairs_of(low), pairs_of(inv), pairs_of(inv_t), NCH // 2, 2 * RP, -1, 1)

            add = lambda j: (w_out(j)[:, RP:KT, :], lambda dve, made: nc.vector.tensor_tensor(x[:, j, :], made, x[:, j, :], ALU.add))
            side = SideProjection(nc, M, [add(j) for j in range(KT)], KT - RP, y[:, RP:KT, :],
                                  sbt("side_ring", [P, 4, KT - RP, P]), 4, (5, 6, 7))
            state, xs, sa = sbt("state", [P, 2, RP, HD]), sbt("xs", [P, 2, RP, CH]), sbt("sa", [P, 2, RP, CH])
            with phase(nc, zeroed=0, x_made=0, x_ready=0, sa_made=0, sa_ready=0, state_made=0, state_ready=0,
                       y_made=0, y_ready=0, dve=0, **SideProjection.SEMAPHORES) as (block, s):
                side.attach(s)

                @block.sync
                def _(sp):
                    side.load(sp)

                rows2 = (slice(0, HD), slice(HD, P))
                part = lambda i: ps[:, i, 0:RP * CH].rearrange("p (j t) -> p j t", j=RP)

                @block.tensor
                def _(pe):
                    mm = nc.tensor.matmul
                    for c in range(NCH):
                        old = state[:, c % 2]
                        pe.wait_ge(s["state_ready"], c + 1)
                        for j in range(RP):
                            for w in rows2:
                                mm(part(0)[w, j, :], ac[w, c, j, :], old[w, j, :], start=True, stop=False)
                                last = mm(part(0)[w, j, :], ak_t[w, c, j, :], v_tok[w, c, j, :], start=False, stop=True)
                        last.then_inc(s["x_made"], 1)
                        side.multiply(pe, (KT - RP) * c + 2)
                        pe.wait_ge(s["x_ready"], c + 1)
                        for j in range(RP):
                            for w in rows2:
                                last = mm(part(1)[w, j, :], inv_t[w, c, j, :], xs[w, c % 2, j, :], start=True, stop=True)
                        last.then_inc(s["sa_made"], 1)
                        side.multiply(pe, (KT - RP) * c + 4)
                        pe.wait_ge(s["sa_ready"], c + 1)
                        for j in range(RP):
                            for w in rows2:
                                mm(part(2)[w, j, :], b_tok[w, c, j, :], sa[w, c % 2, j, :], start=True, stop=False)
                                last = mm(part(2)[w, j, :], k_tok[w, c, j, :], v_tok[w, c, j, :], start=False, stop=True)
                        last.then_inc(s["state_made"], 1)
                        if c >= 2:
                            pe.wait_ge(s["y_ready"], c - 1)
                        for j in range(RP):
                            for w in rows2:
                                mm(part(3 + c % 2)[w, j, :], old[w, j, :], rc[w, c, j, :], start=True, stop=False)
                                mm(part(3 + c % 2)[w, j, :], sa[w, c % 2, j, :], rb_t[w, c, j, :], start=False, stop=False)
                                last = mm(part(3 + c % 2)[w, j, :], v_tok[w, c, j, :], rk_t[w, c, j, :], start=False, stop=True)
                        last.then_inc(s["y_made"], 1)
                        side.multiply(pe, (KT - RP) * (c + 1))

                @block.scalar
                def _(act):
                    for c in range(NCH):
                        act.wait_ge(s["y_made"], c + 1)
                        nc.scalar.activation(y[:, 0:RP, c * CH:(c + 1) * CH], part(3 + c % 2), ACT.Copy).then_inc(s["y_ready"], 1)

                @block.vector
                def _(dve):
                    own = Own(dve, s["dve"])
                    nc.vector.memset(state[:, 0], 0.0).then_inc(s["state_ready"], 1)
                    for c in range(NCH):
                        dve.wait_ge(s["x_made"], c + 1)
                        nc.vector.tensor_copy(xs[:, c % 2], part(0)).then_inc(s["x_ready"], 1)
                        dve.wait_ge(s["sa_made"], c + 1)
                        nc.vector.tensor_copy(sa[:, c % 2], part(1)).then_inc(s["sa_ready"], 1)
                        if c == NCH - 1:
                            break
                        side.take(dve, c)
                        dve.wait_ge(s["state_made"], c + 1)
                        if c >= 1:
                            dve.wait_ge(s["y_made"], c)
                        new = state[:, (c + 1) % 2]
                        own.step(nc.vector.tensor_tensor(new, part(2), state[:, c % 2], ALU.add))
                        nc.vector.tensor_tensor(new, new, end_decay[:, :, c:c + 1].broadcast_to([P, RP, HD]),
                                                ALU.mult).then_inc(s["state_ready"], 1)
                    side.take(dve, KT)

        with ExitStack() as stack:
            sbt = lambda name, shape: buffer(nc, stack, name, shape)
            sq, rstd = sbt("sq", [P, RP, S]), sbt("rstd", [P, S])
            yr = y[:, 0:RP, :]
            with phase(nc, mean_made=0, squared=0, var_made=0, inv_ready=0, root=0, spread=0, dve=0) as (block, s):
                @block.tensor
                def _(pe):
                    for j in range(RP):
                        nc.tensor.matmul(ps[:, j, :], M.c("head_ones"), y[:, j, :], start=True, stop=True).then_inc(s["mean_made"], 1)
                    for j in range(RP):
                        pe.wait_ge(s["squared"], j + 1)
                        nc.tensor.matmul(ps[32 * j:32 * j + 32, 3, :], M.c("head_rows"), sq[:, j, :], start=True, stop=True).then_inc(s["var_made"], 1)
                    pe.wait_ge(s["root"], 1)
                    for j in range(RP):
                        w = slice(32 * j, 32 * j + 32)
                        nc.tensor.matmul(ps[:, 4 + j, :], M.c("head_spread")[w, :], rstd[w, :], start=True, stop=True,
                                         tile_position=(32 * j, 0)).then_inc(s["spread"], 1)

                @block.scalar
                def _(act):
                    for j in range(RP):
                        act.wait_ge(s["dve"], j + 1)
                        nc.scalar.activation(sq[:, j, :], y[:, j, :], ACT.Square).then_inc(s["squared"], 1)
                    act.wait_ge(s["inv_ready"], 1)
                    nc.scalar.activation(rstd[0:32 * RP, :], rstd[0:32 * RP, :], ACT.Sqrt).then_inc(s["root"], 1)

                @block.vector
                def _(dve):
                    own = Own(dve, s["dve"])
                    for j in range(RP):
                        dve.wait_ge(s["mean_made"], j + 1)
                        own.mark(nc.vector.scalar_tensor_tensor(out=y[:, j, :], in0=ps[:, j, :], scalar=-1.0 / HD,
                                                                in1=y[:, j, :], op0=ALU.mult, op1=ALU.add))
                    dve.wait_ge(s["var_made"], RP)
                    var = rstd[0:32 * RP, :]
                    own.step(nc.vector.tensor_scalar(var, ps[0:32 * RP, 3, :], 1.0 / HD, 64e-5, ALU.mult, ALU.add))
                    nc.vector.reciprocal(var, var).then_inc(s["inv_ready"], 1)
                    for j in range(RP):
                        dve.wait_ge(s["spread"], j + 1)
                        own.mark(nc.vector.tensor_tensor(y[:, j, :], y[:, j, :], ps[:, 4 + j, :], ALU.mult))
                    own.settle()
                    for j in range(RP):
                        own.mark(nc.vector.tensor_scalar(y[:, j, :], y[:, j, :], col("ln_g", j), col("ln_b", j),
                                                         ALU.mult, ALU.add))
                    own.settle()
                    own.step(nc.vector.tensor_tensor(yr, yr, bonus[:, :, :], ALU.add))
                    own.step(nc.vector.tensor_tensor(yr, yr, z[:, R_G:R_G + 3, :], ALU.mult))


def add_projection(nc, M, weights, n, kt, src, x, gain=None, ready=None):
    ps = M.ps
    with ExitStack() as stack:
        ring = buffer(nc, stack, "weight_ring", [P, 4, kt, P])
        with phase(nc, landed=4, tile_done=0, added=0) as (block, s):
            @block.sync
            def _(sp):
                for j in range(n):
                    if j >= 4:
                        sp.wait_ge(s["tile_done"], j - 3)
                    sp.dma_start(ring[:, j % 4], weights(j)).then_inc(s["landed"][j % 4], 16)

            @block.tensor
            def _(pe):
                if ready:
                    pe.wait_ge(*ready)
                for j in range(n):
                    pe.wait_ge(s["landed"][j % 4], 16 * (j // 4) + 16)
                    if j >= 4:
                        pe.wait_ge(s["added"], j - 3)
                    for k in range(kt):
                        last = nc.tensor.matmul(ps[:, j % 4, :], ring[:, j % 4, k, :], src[:, k, :],
                                                start=(k == 0), stop=(k == kt - 1))
                    last.then_inc(s["tile_done"], 1)

            @block.vector
            def _(dve):
                for j in range(n):
                    dve.wait_ge(s["tile_done"], j + 1)
                    if gain is None:
                        ins = nc.vector.tensor_tensor(x[:, j, :], ps[:, j % 4, :], x[:, j, :], ALU.add)
                    else:
                        ins = nc.vector.scalar_tensor_tensor(out=x[:, j, :], in0=ps[:, j % 4, :], scalar=gain(j),
                                                             in1=x[:, j, :], op0=ALU.mult, op1=ALU.add)
                    ins.then_inc(s["added"], 1)
    return s["added"], 1


def gated_embedding(nc, M, w_gate, w_proj, p_layer, h, x, ready):
    ps = M.ps
    with ExitStack() as stack:
        sb = lambda name, shape: buffer(nc, stack, name, shape)
        ring, proj, emb, gate = sb("weight_ring", [P, 4, KT, P]), sb("proj", [P, KT, 2, P]), sb("emb", [P, 2, S]), sb("gate", [P, 2, S])
        with phase(nc, small_landed=0, landed=4, tile_done=0, gated=0, scaled=0, added=0) as (block, s):
            @block.sync
            def _(sp):
                sp.dma_start(proj[:, :, :, :], w_proj).then_inc(s["small_landed"], 16)
                sp.dma_start(emb[:, :, :], p_layer).then_inc(s["small_landed"], 16)
                for j in range(KT):
                    if j >= 4:
                        sp.wait_ge(s["tile_done"], j - 3)
                    sp.dma_start(ring[:, j % 4], w_gate(j)).then_inc(s["landed"][j % 4], 16)

            @block.tensor
            def _(pe):
                pe.wait_ge(s["small_landed"], 32)
                pe.wait_ge(*ready)
                for j in range(KT):
                    pe.wait_ge(s["landed"][j % 4], 16 * (j // 4) + 16)
                    if j >= 4:
                        pe.wait_ge(s["added"], j - 3)
                    for k in range(2):
                        nc.tensor.matmul(ps[:, 4 + j % 4, :], proj[:, j, k, :], emb[:, k, :], start=(k == 0), stop=(k == 1))
                    for k in range(KT):
                        last = nc.tensor.matmul(ps[:, j % 4, :], ring[:, j % 4, k, :], h[:, k, :],
                                                start=(k == 0), stop=(k == KT - 1))
                    last.then_inc(s["tile_done"], 1)

            @block.scalar
            def _(act):
                for j in range(KT):
                    act.wait_ge(s["tile_done"], j + 1)
                    if j >= 2:
                        act.wait_ge(s["added"], j - 1)
                    nc.scalar.activation(gate[:, j % 2, :], ps[:, j % 4, :], ACT.Sigmoid).then_inc(s["gated"], 1)

            @block.vector
            def _(dve):
                for j in range(KT):
                    dve.wait_ge(s["gated"], j + 1)
                    g = gate[:, j % 2, :]
                    nc.vector.tensor_tensor(g, ps[:, 4 + j % 4, :], g, ALU.mult).then_inc(s["scaled"], 1)
                    dve.wait_ge(s["scaled"], j + 1)
                    nc.vector.tensor_tensor(x[:, j, :], x[:, j, :], g, ALU.add).then_inc(s["added"], 1)


def modulation(nc, M, rows, mod):
    ps = M.ps
    with phase(nc, turned=0, dve=0) as (block, s):
        @block.tensor
        def _(pe):
            for r in range(ADA_ROUNDS):
                for g in range(ADA_STRIPS):
                    for i in range(4):
                        last = nc.tensor.matmul(ps[:, g, 4 * r + i:4 * r + i + 1],
                                                rows[quarter_row(g), r, i * P:(i + 1) * P], M.c("ones")[quarter_row(g), 0:1],
                                                start=True, stop=True)
            last.then_inc(s["turned"], 1)

        @block.vector
        def _(dve):
            dve.wait_ge(s["turned"], 1)
            by_strip = lambda ap: ap.rearrange("p (r g i) -> p g r i", r=ADA_ROUNDS, g=ADA_STRIPS)
            nc.vector.tensor_tensor(by_strip(mod[:, :]), ps[:, 0:4, 0:4 * ADA_ROUNDS].rearrange("p g (r i) -> p g r i", i=4),
                                    by_strip(M.last("b_ada")), ALU.add).then_inc(s["dve"], 1)


def head_norm(nc, M, z, n, share, eps, gain, ready=None):
    ps = M.ps
    packs = -(-n // 4)
    quarter = lambda j: slice(32 * (j % 4), 32 * (j % 4) + 32)
    rows = lambda b: slice(0, 32 * min(4, n - 4 * b))
    with ExitStack() as stack:
        scratch, rstd = buffer(nc, stack, "scratch", [P, 2, S]), buffer(nc, stack, "rstd", [P, packs, S])
        with phase(nc, squared=0, summed=0, inverse=0, root=0, spread=0, dve=0) as (block, s):
            @block.scalar
            def _(act):
                if ready:
                    act.wait_ge(*ready)
                for j in range(n):
                    if j >= 2:
                        act.wait_ge(s["summed"], j - 1)
                    nc.scalar.activation(scratch[:, j % 2, :], z(j), ACT.Square).then_inc(s["squared"], 1)
                for b in range(packs):
                    act.wait_ge(s["inverse"], b + 1)
                    nc.scalar.activation(rstd[rows(b), b, :], rstd[rows(b), b, :], ACT.Sqrt).then_inc(s["root"], 1)

            @block.tensor
            def _(pe):
                for j in range(n):
                    pe.wait_ge(s["squared"], j + 1)
                    nc.tensor.matmul(ps[quarter(j), j // 4, :], M.c("head_rows"), scratch[:, j % 2, :], start=True,
                                     stop=True).then_inc(s["summed"], 1)
                for j in range(n):
                    pe.wait_ge(s["root"], j // 4 + 1)
                    if j >= 4:
                        pe.wait_ge(s["dve"], packs + j - 3)
                    nc.tensor.matmul(ps[:, 2 + j % 4, :], M.c("head_spread")[quarter(j), :], rstd[quarter(j), j // 4, :],
                                     start=True, stop=True, tile_position=(32 * (j % 4), 0)).then_inc(s["spread"], 1)

            @block.vector
            def _(dve):
                own = Own(dve, s["dve"])
                for b in range(packs):
                    dve.wait_ge(s["summed"], min(n, 4 * b + 4))
                    own.step(nc.vector.tensor_scalar(rstd[rows(b), b, :], ps[rows(b), b, :], share, eps, ALU.mult, ALU.add))
                    nc.vector.reciprocal(rstd[rows(b), b, :], rstd[rows(b), b, :]).then_inc(s["inverse"], 1)
                for j in range(n):
                    dve.wait_ge(s["spread"], j + 1)
                    own.mark(nc.vector.scalar_tensor_tensor(out=z(j), in0=z(j), scalar=gain(j),
                                                            in1=ps[:, 2 + j % 4, :], op0=ALU.mult, op1=ALU.mult))


def full_attention(nc, M, a, h, out, raw, convolved, make_h):
    with ExitStack() as stack:
        sb = lambda name, shape: buffer(nc, stack, name, shape)
        z, tok, tables = sb("attn_z", [P, 6, S]), sb("attn_tok", [P, TT, P]), sb("tables", [P, 2, S])
        maxima, sums = sb("maxima", [P, 32]), sb("sums", [P, 32])
        M.table = lambda n: tables[:, 0 if n == "cos_axial" else 1, :]
        with together(nc):
            landed = load(nc, (tables[:, :, :], a["tables"][:, 4:6, :]))
            ready = make_h()
            project(nc, M, lambda j: a["w_attn2"][j], 6, KT, h, 3,
                    lambda act, j, made: nc.scalar.activation(z[:, j, :], made, ACT.Copy), ready)
            token_major(nc, M, a["w_v2"], P, h, tok, ((0, P, in_order),), ready)
            with phase(nc, cleared=0) as (block, s):
                @block.vector
                def _(dve):
                    dve.wait_ge(*landed)
                    nc.vector.memset(raw[:, :, 0:2], 0.0).then_inc(s["cleared"], 1)
                    nc.vector.memset(raw[:, :, S + 2:S + 4], 0.0).then_inc(s["cleared"], 1)
        head_norm(nc, M, lambda j: z[:, j, :], 6, 1.0 / HD, NORM_EPS, lambda j: M.last("q_norm" if j < 4 else "k_norm"))
        rope(nc, M, z, [(t, "axial") for t in range(6)])
        jobs = []
        for hd in range(8):
            rows, kv = HD * (hd % 2), hd // 4
            for b in range(TT):
                here = slice(b * P, (b + 1) * P)
                jobs.append(Job(q=z[rows:rows + HD, hd // 2, here], k=z[rows:rows + HD, 4 + kv, :], keys=S,
                                            bias=None, v=[tok[:, t, HD * kv:HD * kv + HD] for t in range(TT)],
                                            out=out[rows:rows + HD, hd // 2, here], gate=None, rows=rows))
        mixed = lambda j: (a["w_conv2"][j], lambda act, made: nc.scalar.activation(raw[:, j, 2:S + 2], made, ACT.Copy))
        side = SideProjection(nc, M, [mixed(j) for j in range(12)], KT, h, sb("side_ring", [P, 4, KT, P]), 4, (6, 7))
        conv, term = M.last("conv").rearrange("p (j i) -> p j i", i=5), sb("term", [P, 2, S])

        def convolve(pool, s):
            for n, j in enumerate(range(0, 12, 2)):
                pool.wait_ge(s["side_taken"], j + 1)
                nc.gpsimd.tensor_scalar(convolved(j), raw[:, j, 0:S], conv[:, j, 0:1], None, ALU.mult).then_inc(s["beside"], 1)
                for i in range(1, 5):
                    pool.wait_ge(s["beside"], 9 * n + 2 * i - 1)
                    nc.gpsimd.tensor_scalar(term[:, i % 2, :], raw[:, j, i:i + S], conv[:, j, i:i + 1], None,
                                            ALU.mult).then_inc(s["beside"], 1)
                    pool.wait_ge(s["beside"], 9 * n + 2 * i)
                    nc.gpsimd.tensor_tensor(convolved(j), convolved(j), term[:, i % 2, :], ALU.add).then_inc(s["beside"], 1)
            pool.wait_ge(s["beside"], 9 * 6)

        steps = [(j, i) for j in range(1, 12, 2) for i in range(5)]

        def convolve_odd(dve, s, taken, most):
            for _ in range(most):
                if not steps or steps[0][0] >= taken:
                    return
                j, i = steps.pop(0)
                if i == 0:
                    dve.wait_ge(s["side_taken"], j + 1)
                    ins = nc.vector.tensor_scalar(convolved(j), raw[:, j, 0:S], conv[:, j, 0:1], None, ALU.mult)
                else:
                    dve.wait_ge(s["between"], 5 * (j // 2) + i)
                    ins = nc.vector.scalar_tensor_tensor(out=convolved(j), in0=raw[:, j, i:i + S], scalar=conv[:, j, i:i + 1],
                                                         in1=convolved(j), op0=ALU.mult, op1=ALU.add)
                ins.then_inc(s["between"], 1)

        attention(nc, M, jobs, maxima, sums, side, convolve, convolve_odd)


def delta_net(nc, M, a, h, out, shared, inverses, key, gated):
    ps = M.ps
    JP = 4
    NB = 2 * JP
    halves = (slice(0, HD), slice(HD, P))
    with ExitStack() as outer:
        sb = lambda name, shape: buffer(nc, outer, name, shape)
        big = [P, NCH, 2, JP, CH]
        beta, decay_in, decay_out, decay_end = (sb(x, [P, NCH, 2, JP]) for x in ("beta", "decay_in", "decay_out", "decay_end"))
        q_dec, bv, kd = (sb(x, big) for x in ("q_dec", "bv", "kd"))
        low, at = (shared[:, i].rearrange("p (n d j t) -> p n d j t", n=NCH, d=2, j=JP) for i in range(2))
        chunk = lambda ap, c: ap[:, :, c * CH:(c + 1) * CH]
        with ExitStack() as stack:
            sbt = lambda name, shape: buffer(nc, stack, name, shape)
            qv = inverses[:, 0].rearrange("p (k n) -> p k n", k=KT)
            query, value = qv[:, 0:JP, :], qv[:, JP:2 * JP, :]
            with together(nc):
                with phase(nc, gated=0) as (block, s):
                    @block.scalar
                    def _(act):
                        for tiles in (query, key[:, :, :], value):
                            nc.scalar.activation(tiles, tiles, ACT.Silu).then_inc(s["gated"], 1)
                head_norm(nc, M, lambda j: query[:, j, :] if j < JP else key[:, j - JP, :], 2 * JP, 1.0, 1e-6,
                          lambda j: HD ** -0.5 if j < JP else 1.0, (s["gated"], 3))

            w_ba, raw_ba = sbt("w_ba", [P, KT, 32]), sbt("raw_ba", [P, 2, NCH, 2, JP])
            mag, cum, total = sbt("mag", [P, NCH, 2, JP]), sbt("cum", [P, NCH, 2, JP]), sbt("total", [P, NCH, 2, JP])
            gate, coef = sbt("gate", [P, NCH, 2, JP]), sbt("coef", [P, 2 * JP])
            with phase(nc, landed=0, made=0, copied=0, exps=0, act_in=0, g_ready=0, summed=0, cum_ready=0, dve=0) as (block, s):
                @block.sync
                def _(sp):
                    sp.dma_start(w_ba[:, :, :], a["w_ba2"]).then_inc(s["landed"], 16)

                @block.tensor
                def _(pe):
                    pe.wait_ge(s["landed"], 16)
                    for c in range(NCH):
                        for hp, w in enumerate(halves):
                            for k in range(KT):
                                last = nc.tensor.matmul(ps[w, 0, 16 * c:16 * c + 16], h[:, k, c * CH:(c + 1) * CH],
                                                        w_ba[:, k, 16 * hp:16 * hp + 16], start=(k == 0), stop=(k == KT - 1))
                    last.then_inc(s["made"], 1)
                    pe.wait_ge(s["g_ready"], 1)
                    for d, m in enumerate(("sum_until", "sum_from")):
                        for n in range(NCH):
                            nc.tensor.matmul(ps[:, 1, (2 * n + d) * JP:(2 * n + d + 1) * JP], M.c(m), gate[:, n, d, :], start=True, stop=True)
                    nc.tensor.matmul(ps[:, 2, 0:2 * NCH * JP], M.c("head_ones"), gate[:, :, :, :].rearrange("p n d j -> p (n d j)"),
                                     start=True, stop=True).then_inc(s["summed"], 1)

                @block.scalar
                def _(act):
                    act.wait_ge(s["copied"], 4)
                    nc.scalar.activation(beta[:, :, :, :], raw_ba[:, 0], ACT.Sigmoid).then_inc(s["exps"], 1)
                    nc.scalar.activation(coef[:, :], M.last("a_log"), ACT.Exp).then_inc(s["exps"], 1)
                    act.wait_ge(s["act_in"], 1)
                    nc.scalar.activation(mag[:, :, :, :], mag[:, :, :, :], ACT.Exp, scale=-1.0).then_inc(s["exps"], 1)
                    act.wait_ge(s["act_in"], 2)
                    nc.scalar.activation(mag[:, :, :, :], mag[:, :, :, :], ACT.Ln).then_inc(s["exps"], 1)
                    act.wait_ge(s["cum_ready"], 1)
                    nc.scalar.activation(decay_in[:, :, :, :], cum[:, :, :, :], ACT.Exp).then_inc(s["exps"], 1)
                    nc.scalar.activation(decay_out[:, :, :, :], mag[:, :, :, :], ACT.Exp).then_inc(s["exps"], 1)
                    nc.scalar.activation(decay_end[:, :, :, :], total[:, :, :, :], ACT.Exp).then_inc(s["exps"], 1)

                @block.vector
                def _(dve):
                    own = Own(dve, s["dve"])
                    V = nc.vector
                    dve.wait_ge(s["made"], 1)
                    made = ps[:, 0, 0:16 * NCH].rearrange("p (c k d j) -> p c k d j", c=NCH, k=2, d=2)
                    for kind in range(2):
                        V.tensor_copy(raw_ba[:, kind, :, 0, :], made[:, :, kind, 0, :]).then_inc(s["copied"], 1)
                        V.tensor_copy(raw_ba[:, kind, :, 1, :], made[:, ::-1, kind, 1, :]).then_inc(s["copied"], 1)
                    dve.wait_ge(s["copied"], 4)
                    av = raw_ba[:, 1].rearrange("p n d j -> p n (d j)")
                    bias = M.last("dt_bias").unsqueeze(1).broadcast_to([P, NCH, 2 * JP])
                    own.step(V.tensor_tensor(av, av, bias, ALU.add))
                    own.step(V.tensor_scalar(mag[:, :, :, :], raw_ba[:, 1], -1.0, None, ALU.mult))
                    V.tensor_tensor(mag[:, :, :, :], mag[:, :, :, :], raw_ba[:, 1], ALU.max).then_inc(s["act_in"], 1)
                    dve.wait_ge(s["exps"], 3)
                    V.tensor_scalar(mag[:, :, :, :], mag[:, :, :, :], 1.0, None, ALU.add).then_inc(s["act_in"], 1)
                    own.step(V.tensor_scalar(raw_ba[:, 1], raw_ba[:, 1], 0.0, None, ALU.max))
                    dve.wait_ge(s["exps"], 4)
                    own.step(V.tensor_tensor(raw_ba[:, 1], raw_ba[:, 1], mag[:, :, :, :], ALU.add))
                    own.step(V.tensor_scalar(coef[:, :], coef[:, :], -1.0, None, ALU.mult))
                    V.tensor_tensor(gate[:, :, :, :].rearrange("p n d j -> p n (d j)"), av,
                                    coef[:, :].unsqueeze(1).broadcast_to([P, NCH, 2 * JP]), ALU.mult).then_inc(s["g_ready"], 1)
                    dve.wait_ge(s["summed"], 1)
                    flat = lambda t: t[:, :, :, :].rearrange("p n d j -> p (n d j)")
                    own.mark(V.tensor_copy(flat(cum), ps[:, 1, 0:2 * NCH * JP]))
                    own.step(V.tensor_copy(flat(total), ps[:, 2, 0:2 * NCH * JP]))
                    V.tensor_tensor(mag[:, :, :, :], total[:, :, :, :], cum[:, :, :, :], ALU.subtract).then_inc(s["cum_ready"], 1)
                    dve.wait_ge(s["exps"], 7)
                    own.step(V.scalar_tensor_tensor(out=decay_in[:, :, :, :], in0=decay_in[:, :, :, :], scalar=-1.0,
                                                    in1=beta[:, :, :, :], op0=ALU.mult, op1=ALU.mult))

            rhs, dif = sbt("spread_rhs", [P, 2, NB, CH]), sbt("difference", [P, 2, NB, CH])
            per = lambda t, n: t[:, n].rearrange("p d j -> p (d j)")
            block_of = lambda t, n: t[:, n].rearrange("p d j t -> p (d j) t")
            bank8 = lambda i: ps[:, i, :].rearrange("p (b t) -> p b t", b=NB)
            with phase(nc, rhs_ready=0, spread=0, q_exp=0, capped=0, exp_done=0, masked=0, dve=0) as (block, s):
                @block.tensor
                def _(pe):
                    for n in range(NCH):
                        pe.wait_ge(s["rhs_ready"], n + 1)
                        if n >= 2:
                            pe.wait_ge(s["q_exp"], n - 1)
                            pe.wait_ge(s["capped"], 2 * n - 2)
                        nc.tensor.matmul(ps[:, n % 2, :], M.c("head_ones"), rhs[:, n % 2].rearrange("p b t -> p (b t)"),
                                         start=True, stop=True).then_inc(s["spread"], 1)

                @block.scalar
                def _(act):
                    for n in range(NCH):
                        act.wait_ge(s["spread"], n + 1)
                        nc.scalar.activation(block_of(q_dec, n), bank8(n % 2), ACT.Exp).then_inc(s["q_exp"], 1)
                        act.wait_ge(s["capped"], 2 * n + 2)
                        nc.scalar.activation(block_of(at, n), block_of(at, n), ACT.Exp).then_inc(s["exp_done"], 1)
                        nc.scalar.activation(block_of(low, n), block_of(low, n), ACT.Exp, scale=-1.0).then_inc(s["exp_done"], 1)

                @block.gpsimd
                def _(pool):
                    for n in range(NCH):
                        pool.wait_ge(s["exp_done"], 2 * n + 2)
                        for target, name in ((at, "incl_T"), (low, "strict")):
                            m = M.c(name).rearrange("p (d t) -> p d t", d=2).unsqueeze(2).broadcast_to([P, 2, JP, CH])
                            nc.gpsimd.tensor_tensor(target[:, n], target[:, n], m, ALU.mult).then_inc(s["masked"], 1)
                    pool.wait_ge(s["masked"], 2 * NCH)

                @block.vector
                def _(dve):
                    own = Own(dve, s["dve"])
                    for n in range(NCH):
                        c = per(cum, n).unsqueeze(2).broadcast_to([P, NB, CH])
                        if n >= 2:
                            dve.wait_ge(s["spread"], n - 1)
                        nc.vector.tensor_tensor(rhs[:, n % 2], M.c("ident2").unsqueeze(1).broadcast_to([P, NB, CH]), c,
                                                ALU.mult).then_inc(s["rhs_ready"], 1)
                        dve.wait_ge(s["q_exp"], n + 1)
                        own.step(nc.vector.tensor_tensor(dif[:, n % 2], bank8(n % 2), c, ALU.subtract))
                        nc.vector.tensor_scalar(block_of(at, n), dif[:, n % 2], 0.0, None, ALU.min).then_inc(s["capped"], 1)
                        nc.vector.tensor_scalar(block_of(low, n), dif[:, n % 2], 0.0, None, ALU.max).then_inc(s["capped"], 1)

            with phase(nc, made=0, taken=0, q_scaled=0, dve=0) as (block, s):
                bank4 = lambda i: ps[:, i, 0:JP * CH].rearrange("p (j t) -> p j t", j=JP)

                @block.tensor
                def _(pe):
                    for c in range(NCH):
                        if c >= 2:
                            pe.wait_ge(s["taken"], c - 1)
                        here = slice(c * CH, (c + 1) * CH)
                        for j in range(JP):
                            for w in halves:
                                kc, qc, vc = key[w, j, here], query[w, j, here], value[w, j, here]
                                for i, (lhs, rh) in enumerate(((kc, kc), (kc, qc), (kc, M.c("ident2")[w, :]), (vc, M.c("ident2")[w, :]))):
                                    last = nc.tensor.matmul(bank4(4 * (c % 2) + i)[w, j, :], lhs, rh, start=True, stop=True)
                        last.then_inc(s["made"], 1)

                @block.gpsimd
                def _(pool):
                    for n in range(NCH):
                        for d, c in ((0, n), (1, NCH - 1 - n)):
                            nc.gpsimd.tensor_tensor(q_dec[:, n, d], q_dec[:, n, d], chunk(query, c), ALU.mult).then_inc(s["q_scaled"], 1)
                    pool.wait_ge(s["q_scaled"], 2 * NCH)

                @block.vector
                def _(dve):
                    own = Own(dve, s["dve"])
                    for c in range(NCH):
                        dve.wait_ge(s["made"], c + 1)
                        b = 4 * (c % 2)
                        for d, n in ((0, c), (1, NCH - 1 - c)):
                            wide = lambda t: t[:, n, d, :].unsqueeze(2).broadcast_to([P, JP, CH])
                            own.mark(nc.vector.tensor_tensor(low[:, n, d], bank4(b), low[:, n, d], ALU.mult))
                            own.mark(nc.vector.tensor_tensor(at[:, n, d], bank4(b + 1), at[:, n, d], ALU.mult))
                            own.mark(nc.vector.tensor_tensor(kd[:, n, d], bank4(b + 2), wide(decay_out), ALU.mult))
                            own.step(nc.vector.tensor_tensor(bv[:, n, d], bank4(b + 3), wide(beta), ALU.mult))
                            own.step(nc.vector.tensor_tensor(low[:, n, d], low[:, n, d], wide(beta), ALU.mult))
                        dve.sem_inc(s["taken"], 1)

        with ExitStack() as stack:
            sbt = lambda name, shape: buffer(nc, stack, name, shape)
            inv, inv_t = (inverses[:, i].rearrange("p (n d j t) -> p n d j t", n=NCH, d=2, j=JP) for i in range(2))
            flat = lambda t: t[:, :, :, :, :].rearrange("p n d j t -> p n (d j) t")
            invert(nc, M, flat(low), flat(inv), flat(inv_t), NCH, NB, 1, 2)

            state, kept = inv[:, 0:2], inv[:, 2:4]
            xs, fresh = inv[:, 4:6], inv[:, 6:8]
            silu = lambda j: (a["w_z2"][j], lambda act, made: nc.scalar.activation(gated[:, j, :], made, ACT.Silu))
            side = SideProjection(nc, M, [silu(j) for j in range(JP)], KT, h, sbt("side_ring", [P, 2, KT, P]), 2, (5, 6, 7))
            with phase(nc, x_made=0, scaled=0, x_ready=0, v_made=0, v_ready=0, state_made=0, kept_ready=0, state_ready=0,
                       o_made=0, o_ready=0, dve=0, **SideProjection.SEMAPHORES) as (block, s):
                side.attach(s)

                @block.sync
                def _(sp):
                    side.load(sp)

                bank = lambda i: ps[:, i, :].rearrange("p (d j t) -> p d j t", d=2, j=JP)

                @block.tensor
                def _(pe):
                    mm = nc.tensor.matmul
                    every = [(d, j, w) for d in range(2) for j in range(JP) for w in halves]
                    for n in range(NCH):
                        old, k2 = state[:, n % 2], n % 2
                        here = lambda d: slice((n if d == 0 else NCH - 1 - n) * CH, (n if d == 0 else NCH - 1 - n) * CH + CH)
                        pe.wait_ge(s["state_ready"], n + 1)
                        for d, j, w in every:
                            last = mm(bank(0)[w, d, j, :], key[w, j, here(d)], old[w, d, j, :], start=True, stop=True)
                        last.then_inc(s["x_made"], 1)
                        side.multiply(pe, JP * n + 2)
                        pe.wait_ge(s["x_ready"], n + 1)
                        for d, j, w in every:
                            last = mm(bank(1)[w, d, j, :], inv_t[w, n, d, j, :], xs[w, k2, d, j, :], start=True, stop=True)
                        last.then_inc(s["v_made"], 1)
                        side.multiply(pe, JP * n + 4)
                        pe.wait_ge(s["v_ready"], n + 1)
                        for d, j, w in every:
                            last = mm(bank(2)[w, d, j, :], kd[w, n, d, j, :], fresh[w, k2, d, j, :], start=True, stop=True)
                        last.then_inc(s["state_made"], 1)
                        if n >= 2:
                            pe.wait_ge(s["o_ready"], 2 * n - 2)
                        for d, j, w in every:
                            mm(bank(3 + k2)[w, d, j, :], old[w, d, j, :], q_dec[w, n, d, j, :], start=True, stop=False)
                            last = mm(bank(3 + k2)[w, d, j, :], fresh[w, k2, d, j, :], at[w, n, d, j, :], start=False, stop=True)
                        last.then_inc(s["o_made"], 1)

                @block.scalar
                def _(act):
                    for n in range(NCH):
                        act.wait_ge(s["v_made"], n + 1)
                        if n >= 2:
                            act.wait_ge(s["o_made"], n - 1)
                        nc.scalar.activation(fresh[:, n % 2], bank(1), ACT.Copy).then_inc(s["v_ready"], 1)
                        side.take(act, n // 2)
                    side.take(act, JP)

                @block.vector
                def _(dve):
                    own = Own(dve, s["dve"])
                    V = nc.vector
                    V.memset(state[:, 0], 0.0).then_inc(s["state_ready"], 1)
                    for n in range(NCH):
                        k2 = n % 2
                        wide = lambda t: t[:, n].unsqueeze(3).broadcast_to([P, 2, JP, CH])
                        dve.wait_ge(s["x_made"], n + 1)
                        own.step(V.tensor_tensor(xs[:, k2], bank(0), wide(decay_in), ALU.mult))
                        V.tensor_tensor(xs[:, k2], xs[:, k2], bv[:, n], ALU.add).then_inc(s["x_ready"], 1)
                        if n < NCH - 1:
                            dve.wait_ge(s["state_ready"], n + 1)
                            own.step(V.tensor_tensor(kept[:, k2], state[:, k2], wide(decay_end), ALU.mult))
                            dve.wait_ge(s["state_made"], n + 1)
                            if n >= 1:
                                dve.wait_ge(s["o_made"], n)
                            V.tensor_tensor(state[:, 1 - k2], bank(2), kept[:, k2], ALU.add).then_inc(s["state_ready"], 1)
                        dve.wait_ge(s["o_made"], n + 1)
                        for d, c in ((0, n), (1, NCH - 1 - n)):
                            o = chunk(out, c)
                            if n < NCH // 2:
                                ins = V.tensor_copy(o, bank(3 + k2)[:, d])
                            else:
                                dve.wait_ge(s["o_ready"], 2 * (NCH // 2))
                                ins = V.tensor_tensor(o, bank(3 + k2)[:, d], o, ALU.add)
                            ins.then_inc(s["o_ready"], 1)

    head_norm(nc, M, lambda j: out[:, j, :], JP, 1.0 / HD, NORM_EPS, lambda j: M.last("dn_norm"))
    with phase(nc, dve=0) as (block, s):
        @block.vector
        def _(dve):
            Own(dve, s["dve"]).step(nc.vector.tensor_tensor(out, out, gated[:, :, :], ALU.mult))


def merge(nc, M, w_merge, h, attn, delta, merged):
    ps = M.ps
    with ExitStack() as stack:
        ring, gates = buffer(nc, stack, "weight_ring", [P, 2, 24, P]), buffer(nc, stack, "gates", [P, 2, 2, S])
        with phase(nc, landed=2, tile_done=0, gated=0, taken=0, dve=0) as (block, s):
            parts = [(0, k, h[:, k, :]) for k in range(8)] + [(1, 8 + k, h[:, k, :]) for k in range(8)] + [
                (2, 16 + k, attn[:, k, :]) for k in range(4)] + [(3, 20 + k, delta[:, k, :]) for k in range(4)]

            @block.sync
            def _(sp):
                for m in range(KT):
                    if m >= 2:
                        sp.wait_ge(s["tile_done"], m - 1)
                    sp.dma_start(ring[:, m % 2], w_merge[m]).then_inc(s["landed"][m % 2], 16)

            @block.tensor
            def _(pe):
                for m in range(KT):
                    pe.wait_ge(s["landed"][m % 2], 16 * (m // 2) + 16)
                    if m >= 2:
                        pe.wait_ge(s["taken"], m - 1)
                    for i, (bank, k, src) in enumerate(parts):
                        last = nc.tensor.matmul(ps[:, 4 * (m % 2) + bank, :], ring[:, m % 2, k, :], src,
                                                start=(i == 0 or parts[i - 1][0] != bank),
                                                stop=(i == 23 or parts[i + 1][0] != bank))
                    last.then_inc(s["tile_done"], 1)

            @block.scalar
            def _(act):
                for m in range(KT):
                    act.wait_ge(s["tile_done"], m + 1)
                    if m >= 2:
                        act.wait_ge(s["taken"], m - 1)
                    nc.scalar.activation(gates[:, m % 2], ps[:, 4 * (m % 2):4 * (m % 2) + 2, :], ACT.Sigmoid).then_inc(s["gated"], 1)

            @block.vector
            def _(dve):
                own = Own(dve, s["dve"])
                for m in range(KT):
                    g = gates[:, m % 2]
                    dve.wait_ge(s["gated"], m + 1)
                    own.step(nc.vector.tensor_tensor(g, ps[:, 4 * (m % 2) + 2:4 * (m % 2) + 4, :], g, ALU.mult))
                    nc.vector.tensor_tensor(merged[:, m, :], g[:, 0, :], g[:, 1, :], ALU.add).then_inc(s["taken"], 1)
    return s["taken"], KT


def route(nc, M, w_router, h, tokens, aff, chosen):
    ps = M.ps
    E, CAP = 16, 64
    with ExitStack() as stack:
        sb = lambda name, shape: buffer(nc, stack, name, shape)
        w, stat = sb("w_router", [P, KT, E]), sb("stat", [P, TT])
        rank, taken, best = sb("rank", [E, S]), sb("taken", [E, S]), sb("best", [E, 8])
        ones_row, slot = sb("ones_row", [E, S]), sb("slot", [P, TT, E])
        with phase(nc, landed=0, logits=0, centred=0, exp_done=0, aff_ready=0, turned=0, slot_ready=0, slots_made=0,
                   h_turned=0, h_copied=0, dve=0) as (block, s):
            @block.sync
            def _(sp):
                sp.dma_start(w[:, :, :], w_router).then_inc(s["landed"], 16)

            @block.tensor
            def _(pe):
                pe.wait_ge(s["landed"], 16)
                for t in range(TT):
                    for k in range(KT):
                        last = nc.tensor.matmul(ps[:, 0, E * t:E * t + E], h[:, k, t * P:(t + 1) * P], w[:, k, :],
                                                start=(k == 0), stop=(k == KT - 1))
                last.then_inc(s["logits"], 1)
                for i in range(2 * TT):
                    t, half = i // 2, i % 2
                    if i >= 4:
                        pe.wait_ge(s["h_copied"], i - 3)
                    for k in range(4):
                        last = nc.tensor.transpose(ps[:, 4 + i % 4, k * P:(k + 1) * P], h[:, 4 * half + k, t * P:(t + 1) * P], M.c("ident"))
                    last.then_inc(s["h_turned"], 1)
                pe.wait_ge(s["aff_ready"], 1)
                for t in range(TT):
                    last = nc.tensor.transpose(ps[0:E, 1, t * P:(t + 1) * P], aff[:, t, :], M.c("ident"))
                last.then_inc(s["turned"], 1)
                pe.wait_ge(s["slot_ready"], 1)
                for t in range(TT):
                    last = nc.tensor.transpose(ps[:, 2, t * E:(t + 1) * E], rank[:, t * P:(t + 1) * P], M.c("ident")[0:E, 0:E])
                last.then_inc(s["slots_made"], 1)

            @block.scalar
            def _(act):
                act.wait_ge(s["centred"], 1)
                nc.scalar.activation(aff[:, :, :], aff[:, :, :], ACT.Exp).then_inc(s["exp_done"], 1)
                for i in range(2 * TT):
                    act.wait_ge(s["h_turned"], i + 1)
                    nc.scalar.activation(tokens[:, i // 2, 512 * (i % 2):512 * (i % 2) + 512], ps[:, 4 + i % 4, :], ACT.Copy).then_inc(s["h_copied"], 1)

            @block.vector
            def _(dve):
                own = Own(dve, s["dve"])
                V = nc.vector
                own.mark(V.memset(ones_row[:, :], 1.0))
                own.mark(V.memset(chosen[:, :, E:E + 2, :], 0.0))
                dve.wait_ge(s["logits"], 1)
                logits = ps[:, 0, 0:E * TT].rearrange("p (t e) -> p t e", t=TT)
                own.step(V.reduce_max(stat[:, :], logits, AX.X))
                V.tensor_tensor(aff[:, :, :], logits, stat[:, :].unsqueeze(2).broadcast_to([P, TT, E]), ALU.subtract).then_inc(s["centred"], 1)
                dve.wait_ge(s["exp_done"], 1)
                own.step(V.reduce_sum(stat[:, :], aff[:, :, :], AX.X))
                own.step(V.reciprocal(stat[:, :], stat[:, :]))
                V.tensor_tensor(aff[:, :, :], aff[:, :, :], stat[:, :].unsqueeze(2).broadcast_to([P, TT, E]), ALU.mult).then_inc(s["aff_ready"], 1)
                dve.wait_ge(s["turned"], 1)
                own.step(V.tensor_copy(rank[:, :], ps[0:E, 1, :]))
                for _ in range(CAP // 8):
                    own.step(V.max(best[:, :], rank[:, :]))
                    own.step(V.match_replace(out=rank[:, :], in_to_replace=best[:, :], in_values=rank[:, :], imm_value=-1.0))
                own.step(V.tensor_scalar(taken[:, :], rank[:, :], 0.0, None, ALU.is_lt))
                own.step(V.tensor_tensor_scan(rank[:, :], ones_row[:, :], taken[:, :], 0.0, ALU.mult, ALU.add))
                own.step(V.tensor_tensor(rank[:, :], rank[:, :], taken[:, :], ALU.mult))
                V.tensor_scalar(rank[:, :], rank[:, :], -1.0, None, ALU.add).then_inc(s["slot_ready"], 1)
                dve.wait_ge(s["slots_made"], 1)
                own.step(V.tensor_copy(slot[:, :, :].rearrange("p t e -> p (t e)"), ps[:, 2, 0:TT * E]))
                for t in range(TT):
                    wide = lambda ap: ap[:, t, :].unsqueeze(2).broadcast_to([P, E, CAP])
                    own.step(V.tensor_tensor(chosen[:, t, 0:E], M.c("slots").unsqueeze(1).broadcast_to([P, E, CAP]), wide(slot), ALU.is_equal))


def turn_weights(nc, M, chosen, aff, weighted, back):
    ps = M.ps
    with phase(nc, cleared=0, weighted=0, turned=0, copied=0) as (block, s):
        @block.vector
        def _(dve):
            nc.vector.memset(back[:, 0, :], 0.0).then_inc(s["cleared"], 1)
            for t in range(TT):
                nc.vector.tensor_tensor(weighted[:, t], chosen[:, t, 0:16], aff[:, t, :].unsqueeze(2).broadcast_to([P, 16, 64]),
                                        ALU.mult).then_inc(s["weighted"], 1)
            for i in range(8):
                dve.wait_ge(s["turned"], i + 1)
                nc.vector.tensor_copy(back[:, i + 1, :], ps[:, i % 4, :]).then_inc(s["copied"], 1)

        @block.tensor
        def _(pe):
            pe.wait_ge(s["weighted"], TT)
            for i in range(8):
                if i >= 4:
                    pe.wait_ge(s["copied"], i - 3)
                for t in range(TT):
                    last = nc.tensor.transpose(ps[:, i % 4, t * P:(t + 1) * P],
                                               weighted[:, t, 2 * i:2 * i + 2, :].rearrange("p e c -> p (e c)"), M.c("ident"))
                last.then_inc(s["turned"], 1)


PAIRS, UNITS, SLOTS = 8, 24, 12

TURNS = UNITS // SLOTS


def first_experts(nc, ring, w_expert, landed):
    with phase(nc) as (block, s):
        @block.sync
        def _(sp):
            for i in range(SLOTS):
                sp.dma_start(ring[:, i], w_expert[0, i]).then_inc(landed[i], 16)


def experts(nc, M, w_expert, tokens, chosen, room, back, gain, x, ring, landed):
    ps = M.ps
    one, two = slice(0, HD), slice(HD, P)
    with ExitStack() as stack:
        sb = lambda name, shape: buffer(nc, stack, name, shape)
        xe = sb("xe", [P, 2, KT, 64])
        flat = lambda first, tiles: room[:, first:first + tiles, :].rearrange("p k n -> p (k n)")
        made = flat(0, 2)
        act_in = flat(2, 4).rearrange("p (e n) -> p e n", e=2)
        act_t = flat(6, 2).rearrange("p (e k c) -> p e k c", e=2, k=KT)
        turned_in = lambda a, b: ps[:, 4:6, :].rearrange("p b (f c) -> p (b f) c", f=4)[:, :, a:b]
        with phase(nc, used=SLOTS, x_ready=0, in_copied=0, turned=0, silu_done=0, act_ready=0, out_ready=0,
                   summed=0, added=0, gathered=0) as (block, s):
            used = s["used"]

            @block.sync
            def _(sp):
                with sp.Fori(0, PAIRS - 1) as r:
                    for i in range(UNITS):
                        j = i + SLOTS
                        sp.wait_ge(used[i % SLOTS], r * TURNS + i // SLOTS + 1)
                        sp.dma_start(ring[:, i % SLOTS], w_expert[r + j // UNITS, j % UNITS]).then_inc(landed[i % SLOTS], 16)
                for i in range(UNITS - SLOTS):
                    sp.wait_ge(used[i % SLOTS], (PAIRS - 1) * TURNS + i // SLOTS + 1)
                    sp.dma_start(ring[:, i % SLOTS], w_expert[PAIRS - 1, i + SLOTS]).then_inc(landed[i % SLOTS], 16)

            @block.tensor
            def _(pe):
                def gather(tiles, pair_of):
                    for k in tiles:
                        for t in range(TT):
                            last = nc.tensor.matmul(ps[:, k // 4, (k % 4) * P:(k % 4 + 1) * P], tokens[:, t, k * P:(k + 1) * P],
                                                    pair_of(t), start=(t == 0), stop=(t == TT - 1))
                        if k % 4 == 3:
                            last.then_inc(s["gathered"], 1)

                gather(range(KT), lambda t: chosen[:, t, 0:2, :].rearrange("p e c -> p (e c)"))
                with pe.Fori(0, PAIRS) as r:
                    def arrived(unit):
                        pe.wait_ge(landed[unit % SLOTS], r * (16 * TURNS) + 16 * (unit // SLOTS) + 16)

                    for ep in range(2):
                        if ep == 1:
                            pe.wait_ge(s["out_ready"], r + 1)
                            for m in range(KT):
                                pe.wait_ge(s["added"], r * 8 + m + 1)
                                nc.tensor.matmul(ps[:, 4 + m % 2, :], made[:, m * P:(m + 1) * P],
                                                 back[:, bass.ds(r, 1), :].rearrange("p o n -> p (o n)"),
                                                 start=True, stop=True).then_inc(s["summed"], 1)
                        pe.wait_ge(s["x_ready"], r + 1)
                        for kp in range(4):
                            gate, up = 8 * ep + 2 * kp, 8 * ep + 2 * kp + 1
                            arrived(gate)
                            arrived(up)
                            for k2 in range(2):
                                k = 2 * kp + k2
                                for half in range(2):
                                    for unit, w in ((gate, one), (up, two)):
                                        last = nc.tensor.matmul(ps[w, 2 * ep + half, :], xe[:, ep, k, :],
                                                                ring[:, unit % SLOTS, k2, S * half:S * half + S],
                                                                start=(k == 0), stop=(k == KT - 1))
                                        if k2 == 1 and half == 1:
                                            last.then_inc(used[unit % SLOTS], 1)
                    pe.wait_ge(s["added"], r * 8 + 10)
                    for ep in range(2):
                        pe.wait_ge(s["in_copied"], r * 2 + ep + 1)
                        pe.wait_ge(s["act_ready"], r * 2 + ep + 1)
                        for f in range(KT):
                            last = nc.tensor.transpose(ps[:, 4 + f // 4, (f % 4) * P:(f % 4 + 1) * P],
                                                       act_in[:, ep, f * P:(f + 1) * P], M.c("ident"))
                        last.then_inc(s["turned"], 1)
                        gather(range(4 * ep, 4 * ep + 4), lambda t: chosen[:, t, bass.ds(r * 2 + 2, 2), :].rearrange("p e c -> p (e c)"))
                    pe.wait_ge(s["act_ready"], r * 2 + 3)
                    pe.wait_ge(s["out_ready"], r + 1)
                    for fp in range(4):
                        units = (16 + 2 * fp, 17 + 2 * fp)
                        for unit in units:
                            arrived(unit)
                        for f2 in range(2):
                            f = 2 * fp + f2
                            for half in range(2):
                                for ep, w in ((0, one), (1, two)):
                                    last = nc.tensor.matmul(ps[w, 6 + half, :], act_t[:, ep, f, :],
                                                            ring[:, units[ep] % SLOTS, f2, S * half:S * half + S],
                                                            start=(f == 0), stop=(f == KT - 1))
                                    if f2 == 1 and half == 1:
                                        last.then_inc(used[units[ep] % SLOTS], 1)
                pe.wait_ge(s["out_ready"], PAIRS + 1)
                for m in range(KT):
                    if m >= 4:
                        pe.wait_ge(s["added"], PAIRS * 8 + m - 1)
                    nc.tensor.matmul(ps[:, m % 4, :], made[:, m * P:(m + 1) * P], back[:, PAIRS, :],
                                     start=True, stop=True).then_inc(s["summed"], 1)

            @block.scalar
            def _(act):
                with act.Fori(0, PAIRS) as r:
                    for ep in range(2):
                        last = 8 * ep + 7
                        act.wait_ge(used[last % SLOTS], r * TURNS + last // SLOTS + 1)
                        nc.scalar.activation(act_in[:, ep, :], ps[:, 2 * ep:2 * ep + 2, :].rearrange("p b n -> p (b n)"),
                                             ACT.Copy).then_inc(s["in_copied"], 1)
                    act.wait_ge(s["out_ready"], r + 1)
                    for ep in range(2):
                        act.wait_ge(s["turned"], r * 2 + ep + 1)
                        nc.scalar.activation(act_t[:, ep], turned_in(0, 64), ACT.Silu).then_inc(s["silu_done"], 1)

            @block.vector
            def _(dve):
                def add(m, bank):
                    nc.vector.scalar_tensor_tensor(out=x[:, m, :], in0=ps[:, bank, :], scalar=gain(m), in1=x[:, m, :],
                                                   op0=ALU.mult, op1=ALU.add).then_inc(s["added"], 1)

                dve.sem_inc(s["act_ready"], 1)
                dve.sem_inc(s["added"], 2)
                nc.vector.memset(made, 0.0).then_inc(s["out_ready"], 1)
                gathered = ps[:, 0:2, :].rearrange("p b (k e c) -> p e (b k) c", e=2, c=64)
                dve.wait_ge(s["gathered"], 2)
                nc.vector.tensor_copy(xe[:, :, :, :], gathered).then_inc(s["x_ready"], 1)
                with dve.Fori(0, PAIRS) as r:
                    dve.wait_ge(s["added"], r * 8 + 2)
                    for m in range(KT):
                        dve.wait_ge(s["summed"], r * 8 + m + 1)
                        add(m, 4 + m % 2)
                    for ep in range(2):
                        dve.wait_ge(s["silu_done"], r * 2 + ep + 1)
                        nc.vector.tensor_tensor(act_t[:, ep], turned_in(64, 128), act_t[:, ep], ALU.mult).then_inc(s["act_ready"], 1)
                    dve.wait_ge(s["gathered"], r * 2 + 4)
                    dve.wait_ge(s["x_ready"], r + 1)
                    nc.vector.tensor_copy(xe[:, :, :, :], gathered).then_inc(s["x_ready"], 1)
                    dve.wait_ge(used[SLOTS - 1], r * TURNS + TURNS)
                    nc.vector.tensor_copy(made, ps[:, 6:8, :].rearrange("p b n -> p (b n)")).then_inc(s["out_ready"], 1)
                dve.wait_ge(s["added"], PAIRS * 8 + 2)
                for m in range(KT):
                    dve.wait_ge(s["summed"], PAIRS * 8 + m + 1)
                    add(m, m % 4)


def second_block(nc, M, a, x, h, store, mod):
    E = 16
    with ExitStack() as stack:
        sb = lambda name, shape: buffer(nc, stack, name, shape)
        gains = sb("gains", [P, 2, KT])
        mcol = lambda i, k: mod[:, KT * i + k:KT * i + k + 1]
        with phase(nc, dve=0) as (block, s):
            @block.vector
            def _(dve):
                own = Own(dve, s["dve"])
                for i, name in enumerate(("norm1", "norm2")):
                    own.mark(nc.vector.scalar_tensor_tensor(out=gains[:, i, :], in0=mod[:, KT * (3 * i + 1):KT * (3 * i + 2)], scalar=1.0,
                                                            in1=M.last(name), op0=ALU.add, op1=ALU.mult))
        make_h = lambda: norm(nc, M, x, lambda k: gains[:, 0, k:k + 1], h, shift=lambda k: mcol(0, k))
        attn, delta = store[:, 0:4, :], store[:, 4:8, :]
        with ExitStack() as inner:
            matrices, gated = buffer(nc, inner, "matrices", [P, 2, KT * S]), buffer(nc, inner, "gated", [P, 4, S])
            inverses, key = buffer(nc, inner, "inverses", [P, 2, KT * S]), buffer(nc, inner, "key", [P, 4, S])
            qv = inverses[:, 0].rearrange("p (k n) -> p k n", k=KT)
            convolved = lambda j: qv[:, j, :] if j < 4 else key[:, j - 4, :] if j < 8 else qv[:, j - 4, :]
            raw = matrices[:, :, :].rearrange("p m n -> p (m n)")[:, 0:12 * (S + 4)].rearrange("p (j n) -> p j n", j=12)
            full_attention(nc, M, a, h, attn, raw, convolved, make_h)
            delta_net(nc, M, a, h, delta, matrices, inverses, key, gated)
        with ExitStack() as inner:
            merged = buffer(nc, inner, "merged", [P, KT, S])
            with together(nc):
                ready = merge(nc, M, a["w_merge2"], h, attn, delta, merged)
                added = add_projection(nc, M, lambda j: a["w_o2"][j], KT, KT, merged, x, gain=lambda j: mcol(2, j), ready=ready)
                norm(nc, M, x, lambda k: gains[:, 1, k:k + 1], h, shift=lambda k: mcol(3, k), source=added)
        with ExitStack() as inner:
            sbi = lambda name, shape: buffer(nc, inner, name, shape)
            back, aff, chosen = sbi("back", [P, PAIRS + 1, S]), sbi("aff", [P, TT, E]), sbi("chosen", [P, TT, E + 2, 64])
            ring = sbi("expert_ring", [P, SLOTS, 2, D])
            landed = [inner.enter_context(nc.semaphore(f"expert_landed_{i}")) for i in range(SLOTS)]
            tokens = store[:, 0:KT, :].rearrange("p (t k) n -> p t (k n)", t=TT)
            weighted = h.rearrange("p (t q) n -> p t (q n)", t=TT).rearrange("p t (e c) -> p t e c", c=64)
            with together(nc):
                route(nc, M, a["w_router2"], h, tokens, aff, chosen)
                first_experts(nc, ring, a["w_expert2"], landed)
            turn_weights(nc, M, chosen, aff, weighted, back)
            experts(nc, M, a["w_expert2"], tokens, chosen, h, back, lambda j: mcol(5, j), x, ring, landed)


def program(nc, a, out):
    with ExitStack() as stack:
        sb = lambda name, shape: buffer(nc, stack, name, shape)
        const_at, const_width = constant_offsets()
        layer_at, layer_width = offsets(LAYER_COLUMNS)
        last_at, last_width = offsets(LAST_COLUMNS)
        consts = sb("consts", [P, const_width])
        layer_cols, last_cols = sb("layer_cols", [P, layer_width]), sb("last_cols", [P, last_width])
        x, store = sb("x", [P, KT, S]), sb("store", [P, 2 * KT, S])
        y, h = store[:, 0:KT, :], store[:, KT:2 * KT, :]
        mod = sb("mod", [P, 6 * KT])
        early = stack.enter_context(ExitStack())
        ada_rows = buffer(nc, early, "ada_rows", [P, ADA_ROUNDS, S])
        ps = stack.enter_context(nc.psum_tensor("ps", [P, 8, S], F32))
        M = Core(
            ps=ps, c=lambda n: consts[:, const_at[n][0]:sum(const_at[n])],
            cols=lambda n: layer_cols[:, layer_at[n][0]:sum(layer_at[n])],
            last=lambda n: last_cols[:, last_at[n][0]:sum(last_at[n])])
        col = lambda n, j: M.cols(n)[:, j:j + 1]
        lcol = lambda n, j: M.last(n)[:, j:j + 1]
        with phase(nc, landed=0, cleared=0) as (block, s):
            @block.sync
            def _(sp):
                sp.dma_start(consts[:, :], a["consts"]).then_inc(s["landed"], 16)
                sp.dma_start(x[:, :, :], a["x"]).then_inc(s["landed"], 16)
                sp.dma_start(last_cols[:, :], a["last_cols"]).then_inc(s["landed"], 16)
                sp.wait_ge(s["landed"], 48)

            @block.vector
            def _(dve):
                nc.vector.memset(ada_rows[:, :, :], 0.0).then_inc(s["cleared"], 1)
                dve.wait_ge(s["cleared"], 1)

        with nc.Fori(0, DEPTH) as layer:
            with ExitStack() as inner:
                tables = buffer(nc, inner, "tables", [P, 4, S])
                names = ("cos_head", "sin_head", "cos_index", "sin_index")
                M.table = lambda n: tables[:, names.index(n), :]

                def make_h():
                    landed = load(nc, (layer_cols[:, :], a["layer_cols"][layer]), (tables[:, :, :], a["tables"][:, 0:4, :]))
                    return norm(nc, M, x, lambda k: col("norm_g", k), h, params=landed)

                raw = buffer(nc, inner, "raw", [P, N_R, S + 1])
                mixed_z = buffer(nc, inner, "mixed", [P, N_R, S])
                attention_branches(nc, M, h, y, lambda j: a["w_attn"][layer, j], a["w_tok"][layer],
                                   lambda j: a["w_rwkv"][layer, j], raw, mixed_z, make_h)
                w_out = lambda j: a["w_out"][layer, j]
                rwkv_branch(nc, M, x, y, raw, mixed_z, a["w_up"][layer], w_out, lambda i: a["w_ada2"][layer, i], ada_rows, col)
                with together(nc):
                    added = add_projection(nc, M, lambda j: w_out(j)[:, 0:RP, :], KT, RP, y[:, 0:RP, :], x)
                    ready = norm(nc, M, x, lambda k: col("ple_g", k), h, source=added)
                    gated_embedding(nc, M, lambda j: a["ple_gate"][layer, j], a["ple_proj"][layer], a["p"][layer], h, x, ready)
        with together(nc):
            modulation(nc, M, ada_rows, mod)
            norm(nc, M, x, lambda k: lcol("final_g", k), x, scratch=h)
        early.close()
        second_block(nc, M, a, x, h, store, mod)
        with phase(nc, stored=0) as (block, s):
            @block.sync
            def _(sp):
                sp.dma_start(out, x[:, :, :]).then_inc(s["stored"], 16)
                sp.wait_ge(s["stored"], 16)


def columns(vectors):
    return np.ascontiguousarray(np.concatenate([v.reshape(-1, P).T for v in vectors], axis=1))


def tiles(w, cols):
    w = w[:, cols]
    k, n = w.shape[0] // P, w.shape[1] // P
    return np.ascontiguousarray(w.reshape(k, P, n, P).transpose(2, 1, 0, 3))


def rows_first(w, cols=slice(None)):
    w = w[:, cols]
    return np.ascontiguousarray(w.reshape(w.shape[0] // P, P, w.shape[1]).transpose(1, 0, 2))


def layout(inp):
    r = np.arange
    g = {k: np.asarray(v) for k, v in inp.items()}
    dsa, dil = 1664, 2600
    attn = np.concatenate([dsa + r(256), np.tile(dsa + 256 + r(64), 2), dil + r(768), dsa + 384 + r(256),
                           np.tile(dsa + 640 + r(32), 4), dsa + 680 + r(256), dil + 1152 + r(384)])
    tok = np.concatenate([dsa + 320 + r(64), dsa + 672 + r(8), dil + 768 + r(384)])
    L = range(DEPTH)
    a = {
        "consts": np.concatenate(list(constant_parts().values()), axis=1),
        "tables": np.stack(list(rope_tables().values()), axis=1),
        "x": np.ascontiguousarray(g["x"][0].T.reshape(KT, P, S).transpose(1, 0, 2)),
        "p": np.stack([g["p"][l, 0].T.reshape(2, P, S).transpose(1, 0, 2) for l in L]),
        "layer_cols": np.stack([columns([g[n][l].reshape(-1) for n in (
            "norm_g", "tshift_mu", "rwkv_w0", "rwkv_a0", "rwkv_k_k", "rwkv_k_a", "rwkv_r_k", "rwkv_ln_g",
            "rwkv_ln_b", "ple_norm_g")] + [g["c_2"][0].reshape(DEPTH, -1)[l]]) for l in L]),
        "w_attn": np.stack([tiles(g["w_in"][l], attn) for l in L]),
        "w_rwkv": np.stack([tiles(g["w_in"][l], r(1664)) for l in L]),
        "w_tok": np.stack([rows_first(g["w_in"][l], tok) for l in L]),
        "w_up": np.concatenate([g["rwkv_w_up"], g["rwkv_a_up"]], axis=1),
        "w_out": np.stack([tiles(g["w_out"][l], slice(None)) for l in L]),
        "ple_gate": np.stack([tiles(g["ple_w_gate"][l], slice(None)) for l in L]),
        "ple_proj": np.stack([tiles(g["ple_w_proj"][l], slice(None)).transpose(1, 0, 2, 3) for l in L]),
    }
    w2 = g["w_in_2"][0]
    head_order = np.concatenate([kind + 8 * d + 2 * r(4) + hp for hp in range(2) for kind in (2816, 2832) for d in range(2)])
    a["w_attn2"] = tiles(w2, np.concatenate([r(512), np.tile(512 + r(64), 2), np.tile(576 + r(64), 2)]))
    a["w_v2"] = rows_first(w2, 640 + r(128))
    a["w_conv2"] = tiles(w2, 768 + r(1536))
    a["w_z2"] = tiles(w2, 2304 + r(512))
    a["w_ba2"] = rows_first(w2, head_order)
    a["w_merge2"] = np.concatenate([tiles(w2, 2848 + r(1024)), tiles(w2, 3872 + r(1024)),
                                    tiles(g["w_attn_up_2"][0], slice(None)), tiles(g["w_dn_up_2"][0], slice(None))], axis=2)
    a["w_ada2"] = g["w_ada_2"][0].reshape(DEPTH, ADA_K, P, ADA_ROUNDS, ADA_STRIPS, S).transpose(0, 3, 1, 2, 4, 5).reshape(
        DEPTH, ADA_ROUNDS * ADA_K, P, ADA_STRIPS, S)
    a["w_o2"] = tiles(g["w_o_2"][0], slice(None))
    a["w_router2"] = rows_first(g["w_router_2"][0])
    cut = lambda w: w.reshape(8, 2, 4, 2, P, D).transpose(0, 1, 2, 4, 3, 5)
    up = np.stack([cut(g["w_gate_2"][0]), cut(g["w_up_2"][0])], axis=3).reshape(8, 16, P, 2, D)
    down = cut(g["w_down_2"][0]).transpose(0, 2, 1, 3, 4, 5).reshape(8, 8, P, 2, D)
    a["w_expert2"] = np.concatenate([up, down], axis=1)
    twice = lambda v: np.concatenate([v, v])
    conv = g["conv_w_2"][0]
    per_head = lambda v: np.repeat(v.reshape(2, 4, 2).transpose(2, 0, 1)[:, None], 64, axis=1).reshape(P, 8)
    a["last_cols"] = np.concatenate([
        columns([g["final_norm_g"], g["norm1_w_2"][0], g["norm2_w_2"][0], g["b_ada_2"][0],
                 twice(g["q_norm_w_2"][0]), twice(g["k_norm_w_2"][0]), twice(g["dn_norm_w_2"][0])]),
        conv.reshape(5, 12, P).transpose(2, 1, 0).reshape(P, 60),
        per_head(g["a_log_2"][0]), per_head(g["dt_bias_2"][0])], axis=1)
    return {n: np.ascontiguousarray(v) for n, v in a.items()}


def kernel(**inputs):
    import concourse.bacc as bacc
    from concourse.bass_utils import run_bass_kernel_spmd

    nc = bacc.Bacc("TRN2", target_bir_lowering=False, num_devices=1)
    arrays = {f"in_{n}": v for n, v in layout(inputs).items()}
    aps = {n[3:]: nc.dram_tensor(n, v.shape, mybir.dt.from_np(v.dtype), kind="ExternalInput").ap() for n, v in arrays.items()}
    out = nc.dram_tensor("out", (P, KT, S), F32, kind="ExternalOutput").ap()
    program(nc, aps, out)
    got = run_bass_kernel_spmd(nc, [arrays], core_ids=[0]).results[0]["out"]
    return np.ascontiguousarray(got.transpose(1, 0, 2).reshape(D, S).T).reshape(1, S, D)
```
